# Optimizing a Trainium2 kernel written in Bass

```python
import jax, jax.numpy as jnp
from jax import lax
import numpy as np

D_MODEL = 1024
BATCH = 1
SEQ = 128
DEPTH = 1
DEC_BATCH = 1
DEC_SEQ = 512
PAST_LEN = 128

GRID_W = 64
N_HEADS = 4
DM = 2 * D_MODEL
DV = DM // N_HEADS
DQK = DV // 2
N_FGROUPS = 4
DF = D_MODEL
DG = DF // N_FGROUPS
D_FF = ((8 * D_MODEL // 3 + 255) // 256) * 256
CHUNK = 64
N_GATES = 4 * N_HEADS
ALPHA = (2 * DEPTH) ** 0.25
BETA = (8 * DEPTH) ** -0.25
LN_EPS = 1e-5

Q_END = N_HEADS * DQK
K_END = Q_END + N_HEADS * DQK
V_END = K_END + DM
O_END = V_END + DM
G_END = O_END + N_GATES
F_END = G_END + DF
GA_END = F_END + D_MODEL
N_IN = GA_END + D_MODEL
SPLITS = [Q_END, K_END, V_END, O_END, G_END, F_END, GA_END]

kernel_name = 'hybrid_mlstm_fnet_diffusion_step'

def layer_norm(x, g, b):
    xf = x.astype(jnp.float32)
    mu = xf.mean(-1, keepdims=True)
    var = jnp.square(xf - mu).mean(-1, keepdims=True)
    return ((xf - mu) * lax.rsqrt(var + LN_EPS) * g + b).astype(x.dtype)

def mlstm_chunkwise(q, k, v, ig, lf, C0, n0, m0):
    B, H, S, _ = q.shape
    nc = S // CHUNK

    def to_chunks(t):
        return jnp.moveaxis(t.reshape(B, H, nc, CHUNK, *t.shape[3:]), 2, 0)

    causal = jnp.tril(jnp.ones((CHUNK, CHUNK), bool))

    def step(carry, xs):
        C, n, m = carry
        qc, kc, vc, ic, fc = xs
        b = jnp.cumsum(fc, axis=-1)
        a = b + m[..., None]
        d = jnp.where(causal, b[..., :, None] - b[..., None, :] + ic[..., None, :], -jnp.inf)
        mt = jnp.maximum(a, d.max(-1))
        w = jnp.exp(d - mt[..., None])
        inter = jnp.exp(a - mt)
        s = jnp.einsum('bhtd,bhsd->bhts', qc, kc) * w
        num = jnp.einsum('bhts,bhsv->bhtv', s, vc) + inter[..., None] * jnp.einsum('bhvd,bhtd->bhtv', C, qc)
        den = s.sum(-1) + inter * jnp.einsum('bhd,bhtd->bht', n, qc)
        h = num / jnp.maximum(jnp.abs(den), jnp.exp(-mt))[..., None]
        bl = b[..., -1]
        g = bl[..., None] - b + ic
        ml = jnp.maximum(bl + m, g.max(-1))
        decay = jnp.exp(bl + m - ml)
        wg = jnp.exp(g - ml[..., None])
        C_new = decay[..., None, None] * C + jnp.einsum('bhsv,bhsd->bhvd', vc * wg[..., None], kc)
        n_new = decay[..., None] * n + jnp.einsum('bhs,bhsd->bhd', wg, kc)
        return (C_new, n_new, ml), h

    (C, n, m), hs = lax.scan(step, (C0, n0, m0),
                             (to_chunks(q), to_chunks(k), to_chunks(v), to_chunks(ig), to_chunks(lf)))
    h = jnp.moveaxis(hs, 0, 2).reshape(B, H, S, DV)
    return h, (C, n, m)

def mlstm_bidir(q, k, v, gates, init):
    hs, finals = [], []
    for d in range(2):
        ig = gates[..., d, 0]
        lf = jax.nn.log_sigmoid(gates[..., d, 1])
        if d == 0:
            h, fin = mlstm_chunkwise(q, k, v, ig, lf, *init[d])
        else:
            h, fin = mlstm_chunkwise(jnp.flip(q, 2), jnp.flip(k, 2), jnp.flip(v, 2),
                                     jnp.flip(ig, 2), jnp.flip(lf, 2), *init[d])
            h = jnp.flip(h, 2)
        hs.append(h)
        finals.append(fin)
    return hs[0] + hs[1], finals

def fourier_seq(u):
    B, S, _ = u.shape
    ug = u.astype(jnp.float32).reshape(B, S, N_FGROUPS, DG)
    return jnp.fft.fftn(ug, axes=(1, 3), norm='ortho').real.reshape(B, S, DF).astype(u.dtype)

def fourier_grid(u):
    B, S, _ = u.shape
    rows = S // GRID_W
    ug = u.astype(jnp.float32).reshape(B, rows, GRID_W, N_FGROUPS, DG)
    return jnp.fft.fftn(ug, axes=(1, 2, 4), norm='ortho').real.reshape(B, S, DF).astype(u.dtype)

def mixer(h, l, p, init, fourier_fn):
    B, S, _ = h.shape
    proj = h @ p['w_in'][l]
    q, k, v, o, gt, uf, ga, gb = jnp.split(proj, SPLITS, axis=-1)

    def heads(t, dim):
        return t.reshape(B, S, N_HEADS, dim).transpose(0, 2, 1, 3).astype(jnp.float32)

    qh = heads(q, DQK)
    kh = heads(k, DQK) * DQK ** -0.5
    vh = heads(v, DV)
    gates = (gt + p['b_gate'][l]).astype(jnp.float32).reshape(B, S, 2, 2, N_HEADS).transpose(0, 4, 1, 2, 3)
    h_m, finals = mlstm_bidir(qh, kh, vh, gates, init)
    hf = h_m.transpose(0, 2, 1, 3)
    mu = hf.mean(-1, keepdims=True)
    var = jnp.square(hf - mu).mean(-1, keepdims=True)
    hn = (hf - mu) * lax.rsqrt(var + LN_EPS) * p['mh_gain'][l].reshape(N_HEADS, DV)
    og = jax.nn.sigmoid(o.reshape(B, S, N_HEADS, DV).astype(jnp.float32))
    y_a = (hn * og).reshape(B, S, DM).astype(h.dtype) @ p['w_branch_a'][l]
    y_b = fourier_fn(uf) @ p['w_branch_b'][l]
    merged = jax.nn.sigmoid(ga) * y_a + jax.nn.sigmoid(gb) * y_b
    return merged @ p['w_out'][l], finals

def trunk_layer(x, mod, l, p, init, fourier_fn):
    sh1, sc1, g1, sh2, sc2, g2 = jnp.split(mod, 6, axis=-1)
    h = x * (1 + sc1) + sh1
    out, finals = mixer(h, l, p, init, fourier_fn)
    x = layer_norm(ALPHA * x + g1 * out, p['ln_gain'][l, 0], p['ln_bias'][l, 0])
    h2 = x * (1 + sc2) + sh2
    a, u = jnp.split(h2 @ p['w_ffn_in'][l], 2, axis=-1)
    f = (jax.nn.silu(a) * u) @ p['w_ffn_out'][l]
    x = layer_norm(ALPHA * x + g2 * f, p['ln_gain'][l, 1], p['ln_bias'][l, 1])
    return x, finals

def setup_inputs(seed: int = 0) -> dict:
    key = jax.random.key(seed)
    ks = jax.random.split(key, 20)

    def nrm(k, shape, scale):
        return jax.random.normal(k, shape, jnp.float32) * scale

    x_prompt = nrm(ks[0], (BATCH, SEQ, D_MODEL), 1.0)
    x_sample = nrm(ks[1], (DEC_BATCH, DEC_SEQ, D_MODEL), 1.0)
    c = nrm(ks[2], (DEC_BATCH, D_MODEL), 1.0)
    state_C = nrm(ks[3], (DEC_BATCH, DEPTH, 2, N_HEADS, DV, DQK), 0.1)
    state_n = nrm(ks[4], (DEC_BATCH, DEPTH, 2, N_HEADS, DQK), 0.1)
    state_m = jax.random.uniform(ks[5], (DEC_BATCH, DEPTH, 2, N_HEADS), jnp.float32, 0.0, 2.0)
    c_ctx = nrm(ks[6], (D_MODEL,), 1.0)
    w_mod = nrm(ks[7], (DEPTH, D_MODEL, 6 * D_MODEL), D_MODEL ** -0.5)
    b_mod = nrm(ks[8], (DEPTH, 6 * D_MODEL), 0.02)
    w_in = nrm(ks[9], (DEPTH, D_MODEL, N_IN), D_MODEL ** -0.5)
    gate_base = jnp.array([0.0, 3.0], jnp.float32).reshape(1, 1, 2, 1)
    b_gate = (gate_base + nrm(ks[10], (DEPTH, 2, 2, N_HEADS), 0.1)).reshape(DEPTH, N_GATES)
    mh_gain = 1.0 + nrm(ks[11], (DEPTH, DM), 0.02)
    w_branch_a = nrm(ks[12], (DEPTH, DM, D_MODEL), DM ** -0.5)
    w_branch_b = nrm(ks[13], (DEPTH, DF, D_MODEL), DF ** -0.5)
    w_out = nrm(ks[14], (DEPTH, D_MODEL, D_MODEL), BETA * D_MODEL ** -0.5)
    ln_gain = 1.0 + nrm(ks[15], (DEPTH, 2, D_MODEL), 0.02)
    ln_bias = nrm(ks[16], (DEPTH, 2, D_MODEL), 0.02)
    w_ffn_in = nrm(ks[17], (DEPTH, D_MODEL, 2 * D_FF), D_MODEL ** -0.5)
    w_ffn_out = nrm(ks[18], (DEPTH, D_FF, D_MODEL), BETA * D_FF ** -0.5)
    return {'x_prompt': x_prompt, 'x_sample': x_sample, 'c': c,
            'state_C': state_C, 'state_n': state_n, 'state_m': state_m,
            'c_ctx': c_ctx, 'w_mod': w_mod, 'b_mod': b_mod, 'w_in': w_in, 'b_gate': b_gate,
            'mh_gain': mh_gain, 'w_branch_a': w_branch_a, 'w_branch_b': w_branch_b, 'w_out': w_out,
            'ln_gain': ln_gain, 'ln_bias': ln_bias, 'w_ffn_in': w_ffn_in, 'w_ffn_out': w_ffn_out}

def reference(x_prompt, x_sample, c, state_C, state_n, state_m, c_ctx, w_mod, b_mod, w_in, b_gate,
              mh_gain, w_branch_a, w_branch_b, w_out, ln_gain, ln_bias, w_ffn_in, w_ffn_out):
    p = {'w_in': w_in, 'b_gate': b_gate, 'mh_gain': mh_gain, 'w_branch_a': w_branch_a,
         'w_branch_b': w_branch_b, 'w_out': w_out, 'ln_gain': ln_gain, 'ln_bias': ln_bias,
         'w_ffn_in': w_ffn_in, 'w_ffn_out': w_ffn_out}
    f32 = jnp.float32
    bp = x_prompt.shape[0]
    zero_state = (jnp.zeros((bp, N_HEADS, DV, DQK), f32), jnp.zeros((bp, N_HEADS, DQK), f32),
                  jnp.zeros((bp, N_HEADS), f32))
    xp = x_prompt
    xs = x_sample
    new_C, new_n, new_m = [], [], []
    for l in range(DEPTH):
        mod_ctx = (jax.nn.silu(c_ctx) @ w_mod[l] + b_mod[l])[None, None, :]
        xp, fin = trunk_layer(xp, mod_ctx, l, p, (zero_state, zero_state), fourier_seq)
        new_C.append(jnp.stack([fin[0][0], fin[1][0]], axis=1))
        new_n.append(jnp.stack([fin[0][1], fin[1][1]], axis=1))
        new_m.append(jnp.stack([fin[0][2], fin[1][2]], axis=1))
        mod_lat = (jax.nn.silu(c) @ w_mod[l] + b_mod[l])[:, None, :]
        init_lat = tuple((state_C[:, l, d].astype(f32), state_n[:, l, d].astype(f32),
                          state_m[:, l, d].astype(f32)) for d in range(2))
        xs, _ = trunk_layer(xs, mod_lat, l, p, init_lat, fourier_grid)
    new_state_C = jnp.stack(new_C, axis=1)
    new_state_n = jnp.stack(new_n, axis=1)
    new_state_m = jnp.stack(new_m, axis=1)
    return (xp, xs, new_state_C, new_state_n, new_state_m)


_drawn_inputs = setup_inputs


def setup_inputs(seed=0):
    import zlib

    import numpy as np

    out = dict(_drawn_inputs(seed))
    spreads = {}
    factors = {'state_C': 5.045, 'state_n': 8.0, 'state_m': 8.0, 'mh_gain': 8.0}
    for name, (base, spread) in spreads.items():
        noise = np.random.default_rng([zlib.crc32(name.encode()), seed]).standard_normal(out[name].shape)
        drawn = base * np.exp(spread * noise) if base else spread * noise
        out[name] = __import__('jax').numpy.asarray(drawn.astype(out[name].dtype))
    for name, factor in factors.items():
        out[name] = (out[name] * factor).astype(out[name].dtype)
    return out
```

```python
from contextlib import ExitStack

import numpy as np

import concourse.bass as bass
from concourse import mybir

F32 = mybir.dt.float32
F32R = mybir.dt.float32r
I32 = mybir.dt.int32
ALU = mybir.AluOpType
ACT = mybir.ActivationFunctionType

P = 128
DMODEL = 1024
NC = 128
NL = 512
NT = NC + NL
TT = NT // P
LT = NL // P
GRID_W = 64
H = 4
DM = 2 * DMODEL
DV = DM // H
DQK = DV // 2
KD = DMODEL // P
KQ = DQK // P
KV = DV // P
NG = 4
DG = DMODEL // NG
XW = DG + 2
DFF = ((8 * DMODEL // 3 + 255) // 256) * 256
KF = DFF // P
ALPHA = float(np.float32(2.0 ** 0.25))
EPS = 1e-5
QSCALE = DQK ** -0.5
UB = 8
UW = UB * P
FB = KF // 2
FW = FB * P

U_PASS1 = 0
U_B = 2 * NG
U_GA = U_B + 2 * KD
U_HEAD = U_GA + KD
HU = 2 * KQ + 4 + KV
U_MIX = U_HEAD + H * HU
U_OUT = U_MIX + 2 * KD
U_FF1 = U_OUT + KD
U_FF2 = U_FF1 + 2 * KF
U_END = U_FF2 + 2 * KD
NMOD = 6 * KD
MOD1 = 2 * KD

A_F = 0
A_B = A_F + 2 * NG
A_GA = A_B + KD
A_HEAD = A_GA + KD // 2
HA = 7
A_MIX = A_HEAD + HA * H
A_OUT = A_MIX + KD // 2
A_XT = A_OUT + KD // 2
A_FF1 = A_XT + KD // 2
A_FF2 = A_FF1 + KF
MAGIC = float(0x5F3759DF)


def build(nc, wunits, wffo, wmod, xT, cT, bmod, consts, dft_c, dft_l, dft_x, wgate, gate_bias,
          stateC, state_n, m0_rows, m0_bcast, gainT, lnT, ln_rows,
          y_prompt, y_sample, new_C, new_n, new_m):
    ctx = ExitStack()
    with ctx:
        sem = lambda name: ctx.enter_context(nc.semaphore(name))
        psum = ctx.enter_context(nc.psum_tensor("psum", [P, 8, 512], F32))
        flat = psum[:, :, :].rearrange("p b c -> p (b c)")

        z_dram = nc.dram_tensor("z_dram", [KD, P, NT], F32, kind="Internal").ap()
        ga_dram = nc.dram_tensor("ga_dram", [KD, P, NT], F32, kind="Internal").ap()
        yg_dram = nc.dram_tensor("yg_dram", [H, KV, P, NT], F32, kind="Internal").ap()
        x1_dram = nc.dram_tensor("x1_dram", [KD, P, NT], F32, kind="Internal").ap()

        top = [(nc.sbuf_base + 63) // 64 * 64]

        def at(name, shape, dt, cursor):
            t = nc.alloc_sbuf_tensor_at(name, shape, dt, offset=cursor[0])
            size = int(np.prod(shape[1:])) * 4
            cursor[0] += (size + 63) // 64 * 64
            assert cursor[0] <= nc.sbuf_usable_end, (name, cursor[0])
            return t

        keep = lambda name, shape, dt=F32: at(name, shape, dt, top)
        const_sb = keep("const_sb", [P, 5 * P + H])
        ident, mask_f, mask_b, sel_f, sel_b = (const_sb[:, i * P:(i + 1) * P] for i in range(5))
        onehot = const_sb[:, 5 * P:5 * P + H]
        ones_r = keep("ones_r", [P, P], F32R)
        c_sb = keep("c_sb", [P, KD, 2])
        c_silu = keep("c_silu", [P, KD, 2])
        bmod_sb = keep("bmod_sb", [P, NMOD, 2])
        mod_sb = keep("mod_sb", [P, NMOD, 2])
        gbias = keep("gbias", [P, 1])
        zero = keep("zero", [P, 1])
        em_t = keep("em_t", [P, TT, 4, 32])
        enm_t = keep("enm_t", [P, TT, 2, 32])
        r_rows = keep("r_rows", [P, NT])
        r_head = keep("r_head", [P, NT])
        m0r = keep("m0r", [H, 2])
        m0b = keep("m0b", [P, 2, H])
        n0_sb = keep("n0_sb", [P, H, 2, KQ, 2])
        n0_hi = keep("n0_hi", [P, H, 2, KQ, 2], F32R)
        n0_lo = keep("n0_lo", [P, H, 2, KQ, 2], F32R)
        gain_sb = keep("gain_sb", [P, H * KV])
        gain_h = keep("gain_h", [P, H * KV])
        ln_sb = keep("ln_sb", [P, 2, KD])
        aln = keep("aln", [P, 2, KD])
        h2_s = keep("h2_s", [P, KD, 2])
        h2_b = keep("h2_b", [P, KD, 2])
        stats = keep("stats", [P, TT, 2, 6])
        mv = keep("mv", [P, TT, 2])
        rstd = keep("rstd", [P, TT])
        sd = keep("sd", [P, TT])
        den_sb = keep("den_sb", [P, 2])
        rec = keep("rec", [P, 2])
        wg = keep("wg", [P, 2])
        nt_v = keep("nt_v", [P, 1])
        nt_y = keep("nt_y", [P, 1])
        nt_a = keep("nt_a", [P, 1])

        c1 = [top[0]]
        raw = at("raw", [P, 2, UW], F32, c1)
        w_hi = at("w_hi", [P, 2, UW], F32R, c1)
        w_lo = at("w_lo", [P, 2, UW], F32R, c1)
        ring_end = c1[0]
        h_hi = at("h_hi", [P, KD, NT], F32R, c1)
        h_lo = at("h_lo", [P, KD, NT], F32R, c1)
        h_end = c1[0]
        c0 = [h_end]
        x_sb = at("x_sb", [P, KD, NT], F32, c0)
        mod_first = at("mod_first", [P, 8, UW], F32, c0)
        cs = [h_end + 4 * KD * NT]
        dl_st = at("dl_st", [P, 2 * LT * NL], F32, cs)
        dc_st = at("dc_st", [P, 2 * NC], F32, cs)
        dx_st = at("dx_st", [P, 2 * XW], F32, cs)
        assert cs[0] <= h_end + 2 * 4 * 2 * NG * NT
        cp = [h_end]
        ft_hi = at("ft_hi", [P, 2 * NG, NT], F32R, cp)
        ft_lo = at("ft_lo", [P, 2 * NG, NT], F32R, cp)
        uf_hi = at("uf_hi", [P, 2, NT], F32R, cp)
        uf_lo = at("uf_lo", [P, 2, NT], F32R, cp)
        x_hi = at("xch_hi", [P, TT, XW], F32R, cp)
        x_lo = at("xch_lo", [P, TT, XW], F32R, cp)
        dl_hi = at("dl_hi", [P, 2, LT, NL], F32R, cp)
        dl_lo = at("dl_lo", [P, 2, LT, NL], F32R, cp)
        dc_hi = at("dc_hi", [P, 2, NC], F32R, cp)
        dc_lo = at("dc_lo", [P, 2, NC], F32R, cp)
        dx_hi = at("dx_hi", [P, 2, XW], F32R, cp)
        dx_lo = at("dx_lo", [P, 2, XW], F32R, cp)
        wb_sum = at("wb_sum", [P, UW], F32, cp)
        mod_ring = at("mod_ring", [P, 2, UW], F32, cp)
        cq = [uf_hi_off := h_end + 2 * 2 * NG * NT * 4]
        gb_sb = at("gb_sb", [P, NT], F32, cq)
        z_sb = at("z_sb", [P, NT], F32, cq)
        ga_sb = at("ga_sb", [P, 2, NT], F32, cq)
        gate_w = at("gate_w", [P, UW], F32, cq)
        gw_hi = at("gw_hi", [P, UW], F32R, cq)
        gw_lo = at("gw_lo", [P, UW], F32R, cq)
        gt = at("gt", [P, NT], F32, cq)
        gt_e = at("gt_e", [P, NT], F32, cq)
        gt_m = at("gt_m", [P, NT], F32, cq)
        igs = at("igs", [H, 2, NT], F32, cq)
        lfs = at("lfs", [H, 2, NT], F32, cq)
        bs = at("bs", [H, 2, NT], F32, cq)
        ms = at("ms", [H, 2, NT], F32, cq)
        one4 = at("one4", [H, NT], F32, cq)
        em_rows = at("em_rows", [P, NT], F32, cq)
        assert cq[0] <= cp[0] - 4 * (UW + 2 * UW)
        ch = [h_end]
        q_hi = at("q_hi", [P, KQ, NT], F32R, ch)
        q_lo = at("q_lo", [P, KQ, NT], F32R, ch)
        k_hi = at("k_hi", [P, KQ, NT], F32R, ch)
        k_lo = at("k_lo", [P, KQ, NT], F32R, ch)
        q_f = at("q_f", [P, KQ, NL], F32, ch)
        k_c = at("k_c", [P, KQ, NC], F32, ch)
        v_hi = at("v_hi", [P, TT, DV], F32R, ch)
        v_lo = at("v_lo", [P, TT, DV], F32R, ch)
        og = at("og", [P, KV, NT], F32, ch)
        r_sb = at("r_sb", [P, 2, NT], F32, ch)
        w_sb = at("w_sb", [P, LT + 1, P], F32, ch)
        i_sb = at("i_sb", [P, 2, P], F32, ch)
        qi_f = at("qi_f", [P, 2, KQ, P], F32, ch)
        p_hi = at("p_hi", [P, 2, LT + 1, P], F32R, ch)
        p_lo = at("p_lo", [P, 2, LT + 1, P], F32R, ch)
        qi_hi = at("qi_hi", [P, 2, 2, KQ, P], F32R, ch)
        qi_lo = at("qi_lo", [P, 2, 2, KQ, P], F32R, ch)
        c_raw = at("c_raw", [P, 2, KQ, DV], F32, ch)
        c_hi = at("c_hi", [P, 2, KQ, DV], F32R, ch)
        c_lo = at("c_lo", [P, 2, KQ, DV], F32R, ch)
        kw_f = at("kw_f", [P, 2, DQK], F32, ch)
        kw_hi = at("kw_hi", [P, 2, DQK], F32R, ch)
        kw_lo = at("kw_lo", [P, 2, DQK], F32R, ch)
        h_sb = at("h_sb", [P, DV], F32, ch)
        hn_sb = at("hn_sb", [P, DV], F32, ch)
        yg_sb = at("yg_sb", [P, KV, P], F32, ch)
        st_sb = at("st_sb", [P, 2, 2 * DQK], F32, ch)
        nn_sb = at("nn_sb", [1, 2 * DQK], F32, ch)
        cm = [ring_end]
        yg_hi = at("yg_hi", [P, H * KV, NT], F32R, cm)
        yg_lo = at("yg_lo", [P, H * KV, NT], F32R, cm)
        mg_hi = at("mg_hi", [P, KD, NT], F32R, cm)
        mg_lo = at("mg_lo", [P, KD, NT], F32R, cm)
        yg_st = at("yg_st", [P, 4, NT], F32, cm)
        z_st = at("z_st", [P, 2, NT], F32, cm)
        g_st = at("g_st", [P, 2, NT], F32, cm)
        m_sb = at("m_sb", [P, NT], F32, cm)
        co = [ring_end]
        x_st = at("x_st", [P, 2, NT], F32, co)
        r_t = at("r_t", [P, 2, NT], F32, co)
        rows = at("rows", [P, TT, DMODEL], F32, co)
        assert co[0] <= ring_end + 4 * 2 * H * KV * NT
        cf = [ring_end]
        f_hi = at("f_hi", [P, KF, NT], F32R, cf)
        f_lo = at("f_lo", [P, KF, NT], F32R, cf)
        h2_hi = at("h2_hi", [P, KD, NT], F32R, cf)
        h2_lo = at("h2_lo", [P, KD, NT], F32R, cf)
        s_sb = at("s_sb", [P, NT], F32, cf)
        ff_sb = at("ff_sb", [P, NT], F32, cf)
        cx = [co[0]]
        x1_sb = at("x1_sb", [P, NT], F32, cx)
        h2_f = at("h2_f", [P, NT], F32, cx)
        assert cx[0] <= ring_end + 4 * 2 * KF * NT
        c2 = [ring_end + 4 * 2 * KF * NT]
        raw2 = at("raw2", [P, 2, FW], F32, c2)
        w2_hi = at("w2_hi", [P, 2, FW], F32R, c2)
        w2_lo = at("w2_lo", [P, 2, FW], F32R, c2)
        x2_st = at("x2_st", [P, 2, NT], F32, c2)
        r2_t = at("r2_t", [P, 2, NT], F32, c2)
        rows2 = at("rows2", [P, TT, DMODEL], F32, [top[0]])
        ln_row = at("ln_row", [P, 2, DMODEL], F32, c2)
        assert top[0] + 4 * TT * DMODEL <= ring_end

        small_in = sem("small_in")
        gw_in = sem("gw_in")
        zero_ok = sem("zero_ok")
        x_in = sem("x_in")
        dft_in = sem("dft_in")
        raw_in = [sem(f"raw_in{r}") for r in range(2)]
        mod_in = [sem(f"mod_in{r}") for r in range(8)]
        mod2_in = [sem(f"mod2_in{r}") for r in range(2)]
        c_in = sem("c_in")
        w_half = sem("w_half")
        w_split = sem("w_split")
        units_done = sem("units_done")
        mod_done = sem("mod_done")
        taken = [sem("taken_a"), sem("taken_b")]
        once = sem("once")
        once_v = sem("once_v")
        x_mod = sem("x_mod")
        h_hi_ok = sem("h_hi_ok")
        h_ok = sem("h_ok")
        dft_hi_ok = sem("dft_hi_ok")
        dft_ok = sem("dft_ok")
        uf_hi_ok = sem("uf_hi_ok")
        xch_done = sem("xch_done")
        xch_hi_ok = sem("xch_hi_ok")
        xch_ok = sem("xch_ok")
        pos_done = sem("pos_done")
        ft_hi_ok = sem("ft_hi_ok")
        z_stored = sem("z_stored")
        ga_stored = [sem("ga_stored0"), sem("ga_stored1")]
        gate_acc = sem("gate_acc")
        gate_act = sem("gate_act")
        gates_ok = sem("gates_ok")
        em_acc = sem("em_acc")
        em_ok = sem("em_ok")
        m_stored = sem("m_stored")
        dve = sem("dve")
        rh_ok = sem("rh_ok")
        r_done = sem("r_done")
        r_ok = sem("r_ok")
        qk_hi_ok = sem("qk_hi_ok")
        c_hi_ok = sem("c_hi_ok")
        c_ok = sem("c_ok")
        v_hi_ok = sem("v_hi_ok")
        v_ok = sem("v_ok")
        diag_ok = sem("diag_ok")
        e_ok = sem("e_ok")
        s_done = sem("s_done")
        s_free = sem("s_free")
        p_f_ok = sem("p_f_ok")
        p_hi_ok = sem("p_hi_ok")
        p_ok = sem("p_ok")
        den_done = sem("den_done")
        den_read = sem("den_read")
        num_done = sem("num_done")
        rec_ok = sem("rec_ok")
        hf_ok = sem("hf_ok")
        num_free = sem("num_free")
        hn_ok = sem("hn_ok")
        t_done = sem("t_done")
        yg_ok = sem("yg_ok")
        yg_stored = sem("yg_stored")
        kt_done = sem("kt_done")
        kw_hi_ok = sem("kw_hi_ok")
        kw_ok = sem("kw_ok")
        st_done = sem("st_done")
        st_stored = [sem("st_stored0"), sem("st_stored1")]
        nn_stored = sem("nn_stored")
        ygs_in = [sem(f"ygs_in{r}") for r in range(4)]
        ygs_hi_ok = sem("ygs_hi_ok")
        ygs_ok = sem("ygs_ok")
        zg_in = [sem("zg_in0"), sem("zg_in1")]
        m_f_ok = sem("m_f_ok")
        m_hi_ok = sem("m_hi_ok")
        m_ok = sem("m_ok")
        xs_in = [sem("xs_in0"), sem("xs_in1")]
        rt_done = sem("rt_done")
        rows_ok = sem("rows_ok")
        stats_seen = sem("stats_seen")
        var_ok = sem("var_ok")
        sd_ok = sem("sd_ok")
        xn_ok = sem("xn_ok")
        xt_done = sem("xt_done")
        x1_ok = sem("x1_ok")
        x1_stored = sem("x1_stored")
        h2f_ok = sem("h2f_ok")
        h2_hi_ok = sem("h2_hi_ok")
        f_hi_ok = sem("f_hi_ok")
        f_ok = sem("f_ok")
        x1s_in = [sem("x1s_in0"), sem("x1s_in1")]
        lnr_in = sem("lnr_in")
        rt2_done = sem("rt2_done")
        rows2_ok = sem("rows2_ok")
        var2_ok = sem("var2_ok")
        sd2_ok = sem("sd2_ok")
        y_ok = sem("y_ok")
        y_stored = sem("y_stored")

        def halves(pair):
            return psum[:, 2 * pair:2 * pair + 2, 0:NT // 2]

        def joined(pair):
            a = 2 * pair * 512 + 512 - NC
            return flat[:, a:a + NT]

        def two(ap):
            return ap.rearrange("p (a b) -> p a b", a=2)

        def wlat(tt):
            return slice(NC + P * tt, NC + P * tt + P)

        N_SMALL = 12
        block = ctx.enter_context(nc.Block())

        @block.sync
        def _(sp):
            for dst, src in ((c_sb[:], cT), (bmod_sb[:], bmod), (const_sb[:], consts), (gbias[:], gate_bias),
                             (m0r[:], m0_rows), (m0b[:], m0_bcast), (n0_sb[:], state_n), (gain_sb[:], gainT),
                             (ln_sb[:], lnT)):
                sp.dma_start(dst, src).then_inc(small_in, 16)
            for m in range(8):
                sp.dma_start(mod_first[:, m, :], wmod[m]).then_inc(mod_in[m], 16)
            sp.dma_start(x_sb[:], xT).then_inc(x_in, 16)
            for r in range(2):
                sp.dma_start(raw[:, r, :], wunits[r]).then_inc(raw_in[r], 16)
            for m in range(8):
                sp.wait_ge(mod_done, m + 1)
                sp.dma_start(mod_first[:, m, :], wmod[8 + m]).then_inc(mod_in[m], 16)
            sp.wait_ge(mod_done, MOD1)
            for dst, src in ((dl_st, dft_l), (dc_st, dft_c), (dx_st, dft_x)):
                sp.dma_start(dst[:], src).then_inc(dft_in, 16)
            for r in range(2):
                sp.dma_start(mod_ring[:, r, :], wmod[MOD1 + r]).then_inc(mod2_in[r], 16)
            with sp.Fori(1, U_HEAD // 2) as i:
                for r in range(2):
                    sp.wait_ge(w_split, 2 * i + r - 1)
                    sp.dma_start(raw[:, r, :], wunits[2 * i + r]).then_inc(raw_in[r], 16)
                for r in range(2):
                    sp.wait_ge(mod_done, 2 * i + r + MOD1 - 1)
                    sp.dma_start(mod_ring[:, r, :], wmod[2 * i + r + MOD1]).then_inc(mod2_in[r], 16)
            with sp.Fori(0, H) as h:
                sp.wait_ge(c_ok, h + 1)
                sp.wait_ge(mod_done, NMOD)
                sp.wait_ge(em_ok, 2)
                sp.dma_start(c_raw[:], stateC[h]).then_inc(c_in, 16)
                for r in range(HU):
                    sp.wait_ge(w_split, U_HEAD + HU * h + r - 1)
                    sp.dma_start(raw[:, r % 2, :], wunits[U_HEAD + HU * h + r]).then_inc(raw_in[r % 2], 16)
            for r in range(2):
                sp.wait_ge(w_split, U_MIX + r - 1)
                sp.dma_start(raw[:, r, :], wunits[U_MIX + r]).then_inc(raw_in[r], 16)
            sp.wait_ge(yg_stored, 16 * (H * TT + 1))
            for r in range(2):
                sp.wait_ge(st_stored[r], 16 * (2 * H + 1))
            sp.wait_ge(nn_stored, 16 * (H + 1))
            yg_tiles = yg_dram.rearrange("h v p t -> (h v) p t")
            with sp.Fori(0, H * KV // 4) as i:
                for r in range(4):
                    sp.wait_ge(ygs_ok, 4 * i + r + 1)
                    sp.dma_start(yg_st[:, r, :], yg_tiles[4 * i + r]).then_inc(ygs_in[r], 16)
            sp.wait_ge(z_stored, 16 * (KD + 1))
            for r in range(2):
                sp.wait_ge(ga_stored[r], 16 * (KD // 2 + 1))
            with sp.Fori(0, KD // 2) as i:
                for r in range(2):
                    sp.wait_ge(m_ok, 2 * i + r + 1)
                    sp.dma_start(z_st[:, r, :], z_dram[2 * i + r]).then_inc(zg_in[r], 16)
                    sp.dma_start(g_st[:, r, :], ga_dram[2 * i + r]).then_inc(zg_in[r], 16)
                    for q in range(2):
                        sp.wait_ge(w_split, U_MIX + 4 * i + 2 * r + q + 1)
                        sp.dma_start(raw[:, q, :], wunits[U_MIX + 2 + 4 * i + 2 * r + q]).then_inc(raw_in[q], 16)
            sp.wait_ge(units_done, U_OUT)
            with sp.Fori(0, KD // 2) as i:
                for r in range(2):
                    sp.wait_ge(taken[r], A_OUT + i + 1)
                    sp.dma_start(x_st[:, r, :], xT[:, 2 * i + r, :]).then_inc(xs_in[r], 16)
                for r in range(2):
                    sp.wait_ge(w_split, U_OUT + 2 * i + r + 1)
                    sp.dma_start(raw[:, r, :], wunits[U_OUT + 2 + 2 * i + r]).then_inc(raw_in[r], 16)
            with sp.Fori(1, KF) as i:
                for r in range(2):
                    sp.wait_ge(w_split, U_FF1 + 2 * i + r - 1)
                    sp.dma_start(raw[:, r, :], wunits[U_FF1 + 2 * i + r]).then_inc(raw_in[r], 16)
            sp.wait_ge(units_done, U_FF2)
            for r in range(2):
                sp.dma_start(raw2[:, r, :], wffo[r]).then_inc(raw_in[r], 16)
            sp.wait_ge(f_ok, KF + 1)
            sp.dma_start(ln_row[:], ln_rows).then_inc(lnr_in, 16)
            sp.wait_ge(x1_stored, 16 * (KD + 1))
            for r in range(2):
                sp.dma_start(x2_st[:, r, :], x1_dram[r]).then_inc(x1s_in[r], 16)
            with sp.Fori(0, KD // 2 - 1) as i:
                for r in range(2):
                    for q in range(2):
                        sp.wait_ge(w_split, U_FF2 + 4 * i + 2 * r + q + 1)
                        sp.dma_start(raw2[:, q, :], wffo[4 * i + 2 * r + q + 2]).then_inc(raw_in[q], 16)
                for r in range(2):
                    sp.wait_ge(taken[r], A_FF2 + i + 2)
                    sp.dma_start(x2_st[:, r, :], x1_dram[2 * i + r + 2]).then_inc(x1s_in[r], 16)
            for q in range(2):
                sp.wait_ge(w_split, U_END - 4 + q + 1)
                sp.dma_start(raw2[:, q, :], wffo[2 * KD - 2 + q]).then_inc(raw_in[q], 16)
            for tt in range(TT):
                sp.wait_ge(y_ok, tt + 1)
                dst = y_prompt if tt == 0 else y_sample[(tt - 1) * P:tt * P, :]
                sp.dma_start(dst, rows2[:, tt, :]).then_inc(y_stored, 16)
            sp.wait_ge(y_stored, 16 * TT)
            sp.wait_ge(m_stored, 32)

        @block.gpsimd
        def _(pool):
            def split(u, slot, first, combine=False, ring=(raw, w_hi, w_lo), n_in=None):
                src, hi, lo = (t[:, slot, :] for t in ring)
                pool.wait_ge(raw_in[slot], n_in)
                if not first:
                    pool.wait_ge(units_done, u - 1)
                if combine:
                    half = UW // 2
                    pool.tensor_tensor(wb_sum[:, 0:half], src[:, 0:half], src[:, half:UW], ALU.add)
                    pool.tensor_tensor(wb_sum[:, half:UW], src[:, half:UW], src[:, 0:half], ALU.subtract)\
                        .then_inc(w_half, 1)
                return src, hi, lo

            def rounded(src, hi):
                pool.tensor_tensor(hi, src, zero[:, 0:1].broadcast_to([P, src.shape[1]]), ALU.add)\
                    .then_inc(w_half, 1)

            def rest(src, hi, lo):
                pool.tensor_tensor(lo, src, hi.bitcast(F32), ALU.subtract).then_inc(w_split, 1)

            pool.memset(zero[:], 0.0).then_inc(zero_ok, 1)
            pool.wait_ge(zero_ok, 1)
            for u in range(2):
                src, hi, lo = split(u, u, True, n_in=16)
                rounded(src, hi)
                pool.wait_ge(w_half, u + 1)
                rest(src, hi, lo)
            with pool.Fori(1, NG) as i:
                for r in range(2):
                    src, hi, lo = split(2 * i + r, r, False, n_in=16 * i + 16)
                    rounded(src, hi)
                    pool.wait_ge(w_half, 2 * i + r + 1)
                    rest(src, hi, lo)
            with pool.Fori(0, KD) as j:
                src, hi, lo = split(U_B + 2 * j, 0, False, n_in=16 * j + 16 * (NG + 1))
                rounded(src, hi)
                pool.wait_ge(w_half, U_B + 3 * j + 1)
                rest(src, hi, lo)
                src, hi, lo = split(U_B + 2 * j + 1, 1, False, True, n_in=16 * j + 16 * (NG + 1))
                pool.wait_ge(w_half, U_B + 3 * j + 2)
                rounded(wb_sum[:], hi)
                pool.wait_ge(w_half, U_B + 3 * j + 3)
                rest(wb_sum[:], hi, lo)
            half0 = U_GA + KD
            with pool.Fori(0, (U_FF2 - U_GA) // 2) as i:
                for r in range(2):
                    src, hi, lo = split(U_GA + 2 * i + r, r, False, n_in=16 * i + 16 * (U_GA // 2 + 1))
                    rounded(src, hi)
                    pool.wait_ge(w_half, half0 + 2 * i + r + 1)
                    rest(src, hi, lo)
            half1 = half0 + U_FF2 - U_GA
            with pool.Fori(0, KD) as i:
                for r in range(2):
                    src, hi, lo = split(U_FF2 + 2 * i + r, r, False, ring=(raw2, w2_hi, w2_lo),
                                        n_in=16 * i + 16 * (U_FF2 // 2 + 1))
                    if r == 0:
                        pool.wait_ge(units_done, U_FF2)
                    rounded(src, hi)
                    pool.wait_ge(w_half, half1 + 2 * i + r + 1)
                    rest(src, hi, lo)

        @block.tensor
        def _(pe):
            mm = pe.matmul

            def unit_cols(out, u, slot, act_hi, act_lo, k0=0, last=True, first=True, nb=UB, split320=True,
                          ring=(w_hi, w_lo), k_ready=None):
                pe.wait_ge(w_split, u + 1)
                spans = [(0, NT // 2), (NT // 2, NT)] if split320 else [(0, NC), (NC, NT)]
                for b in range(nb):
                    if k_ready is not None:
                        pe.wait_ge(k_ready, b + 1)
                    cols = slice(b * P, (b + 1) * P)
                    terms = ((ring[0], act_hi), (ring[0], act_lo), (ring[1], act_hi))
                    for n, (w, x) in enumerate(terms):
                        for half, (a, z) in enumerate(spans):
                            dst = out[:, half, :] if split320 else out[:, a:z]
                            ins = mm(dst, w[:, slot, cols], x[:, k0 + b, a:z],
                                     start=(first and b == 0 and n == 0),
                                     stop=(last and b == nb - 1 and n == 2))
                ins.then_inc(units_done, 1)

            def mod_unit(slot, ring, landed, value, col):
                pe.wait_ge(landed, value)
                for k in range(KD):
                    ins = mm(psum[:, 7, bass.ds(col, 2)], ring[:, slot, k * P:(k + 1) * P], c_silu[:, k, :],
                             start=(k == 0), stop=(k == KD - 1))
                ins.then_inc(mod_done, 1)

            def mod_pair(i):
                for r in range(2):
                    mod_unit(r, mod_ring, mod2_in[r], 16 * i + 16, 2 * (MOD1 + r) + 4 * i)

            for p in range(2):
                pe.sem_inc(taken[p], 1)
            pe.wait_ge(once, 1)
            for g in range(2):
                for m in range(8):
                    mod_unit(m, mod_first, mod_in[m], 16 * g + 16, 16 * g + 2 * m)

            with pe.Fori(0, NG) as g:
                for p in range(2):
                    pe.wait_ge(taken[p], A_F + 2 * g + 1)
                    unit_cols(halves(p), U_PASS1 + 2 * g + p, p, h_hi, h_lo, k_ready=h_ok if p == 0 else None)
                if True:
                    pe.wait_ge(dft_ok, 3)
                mod_pair(g)
                for p in range(2):
                    pe.wait_ge(taken[p], A_F + 2 * g + 2)
                for tt in range(TT):
                    if tt >= 3:
                        pe.wait_ge(xch_ok, 5 * g + tt - 2)
                    n = 0
                    for k in range(2):
                        for u, d in ((uf_hi, dx_hi), (uf_lo, dx_hi), (uf_hi, dx_lo)):
                            ins = mm(psum[:, 4 + tt % 3, 0:XW], u[:, k, tt * P:(tt + 1) * P], d[:, k, :],
                                     start=(n == 0), stop=(n == 5))
                            n += 1
                    ins.then_inc(xch_done, 1)
                pe.wait_ge(xch_ok, 5 * g + 5)
                for kind in range(2):
                    out = joined(kind)
                    cols = slice(kind * P, kind * P + P)
                    for span, tiles, dh, dl in ((slice(0, NC), range(1), dc_hi, dc_lo),
                                                (slice(NC, NT), range(1, TT), dl_hi, dl_lo)):
                        for t in tiles:
                            pos = (lambda d, c: d[:, c, :]) if t == 0 else (lambda d, c, t=t: d[:, c, t - 1, :])
                            jobs = [(x_hi, cols, pos(dh, kind)), (x_lo, cols, pos(dh, kind)),
                                    (x_hi, cols, pos(dl, kind))]
                            if kind == 1:
                                nyq = slice(2 * P, 2 * P + 2)
                                jobs += [(x_hi, nyq, pos(dh, 0)), (x_lo, nyq, pos(dh, 0)), (x_hi, nyq, pos(dl, 0))]
                            for n, (x, cc, d) in enumerate(jobs):
                                m = cc.stop - cc.start
                                ins = mm(out[0:m, span], x[:, t, cc], d,
                                         start=(t == tiles[0] and n == 0),
                                         stop=(t == tiles[-1] and n == len(jobs) - 1), skip_group_check=True)
                    ins.then_inc(pos_done, 1)

            with pe.Fori(0, KD) as j:
                pe.wait_ge(taken[0], A_B + j + 1)
                unit_cols(halves(0), U_B + 2 * j, 0, h_hi, h_lo)
                pe.wait_ge(taken[1], A_B + j + 1)
                unit_cols(halves(1), U_B + 2 * j + 1, 1, ft_hi, ft_lo)
                mod_pair(j + NG)

            pe.wait_ge(gates_ok, 1)
            for k in range(KD):
                for n, (w, x) in enumerate(((gw_hi, h_hi), (gw_hi, h_lo), (gw_lo, h_hi))):
                    for half in range(2):
                        ins = mm(psum[:, 5 + half, 0:NT // 2], w[:, k * P:(k + 1) * P],
                                 x[:, k, half * NT // 2:(half + 1) * NT // 2],
                                 start=(k == 0 and n == 0), stop=(k == KD - 1 and n == 2))
            ins.then_inc(gate_acc, 1)

            with pe.Fori(0, KD // 2) as i:
                for p in range(2):
                    pe.wait_ge(taken[p], A_GA + i + 1)
                    unit_cols(halves(p), U_GA + 2 * i + p, p, h_hi, h_lo)
                mod_pair(i + NG + KD)
            pe.wait_ge(gates_ok, 2)
            for tt in range(TT):
                ins = pe.transpose(flat[:, 5 * 512 + tt * P:5 * 512 + (tt + 1) * P],
                                   em_rows[:, tt * P:(tt + 1) * P], ident)
            ins.then_inc(em_acc, 1)

            with pe.Fori(0, H) as h:
                U = U_HEAD + HU * h
                A = A_HEAD + HA * h

                def project(pair, tile, unit, slot, joint):
                    pe.wait_ge(taken[pair], A + tile + 1)
                    unit_cols(joined(pair) if joint else halves(pair), U + unit, slot, h_hi, h_lo,
                              split320=not joint)

                def scores(u):
                    if u == 0:
                        pe.wait_ge(v_ok, 5 * h + 2)
                    else:
                        pe.wait_ge(s_free, 5 * h + u)
                    srcs = range(LT) if u < LT else range(1)
                    tq = wlat(u) if u < LT else slice(0, NC)
                    for s in srcs:
                        sk = wlat(s) if u < LT else slice(0, NC)
                        n = 0
                        for d in range(KQ):
                            for a, b in ((k_hi, q_hi), (k_hi, q_lo), (k_lo, q_hi)):
                                ins = mm(psum[:, 4, s * P:(s + 1) * P], a[:, d, sk], b[:, d, tq],
                                         start=(n == 0), stop=(n == 3 * KQ - 1))
                                n += 1
                    ins.then_inc(s_done, 1)

                def numer(u):
                    buf = u % 2
                    if u == 0:
                        pe.wait_ge(v_ok, 5 * h + 5)
                        pe.wait_ge(c_ok, h + 2)
                    else:
                        pe.wait_ge(den_read, 5 * h + u)
                        pe.wait_ge(num_free, 5 * h + u)
                    if u >= 2:
                        pe.wait_ge(yg_ok, 5 * h + u)
                    pe.wait_ge(p_ok, 5 * h + u + 1)
                    blocks = [list(range(u + 1)), list(range(u, LT))] if u < LT else [[0], [0]]
                    starts = [0, u + 1] if u < LT else [0, 1]
                    for part in range(2):
                        for d in range(2):
                            jobs = []
                            for n, s in enumerate(blocks[d]):
                                pos = starts[d] + n
                                hi, lo = p_hi[:, buf, pos, :], p_lo[:, buf, pos, :]
                                if part == 0:
                                    jobs += [(hi, ones_r[:, 0:2]), (lo, ones_r[:, 0:2])]
                                else:
                                    vt = s + 1 if u < LT else 0
                                    jobs += [(hi, v_hi[:, vt, :]), (lo, v_hi[:, vt, :]), (hi, v_lo[:, vt, :])]
                            if u < LT:
                                for k in range(KQ):
                                    hi, lo = qi_hi[:, buf, d, k, :], qi_lo[:, buf, d, k, :]
                                    a, b = ((n0_hi[:, h, d, k, :], n0_lo[:, h, d, k, :]) if part == 0
                                            else (c_hi[:, d, k, :], c_lo[:, d, k, :]))
                                    jobs += [(hi, a), (lo, a), (hi, b)]
                            out = psum[:, 7, 2 * d:2 * d + 2] if part == 0 else psum[:, 5 + d, :]
                            for n, (a, b) in enumerate(jobs):
                                ins = mm(out, a, b, start=(n == 0), stop=(n == len(jobs) - 1))
                        ins.then_inc(num_done if part else den_done, 1)

                def turn(u):
                    pe.wait_ge(hn_ok, 5 * h + u + 1)
                    pe.wait_ge(den_read, 5 * h + min(u + 2, 5))
                    if u >= 1:
                        pe.wait_ge(yg_ok, 5 * h + u + 1)
                    for v in range(KV):
                        ins = pe.transpose(psum[:, 7, v * P:(v + 1) * P], hn_sb[:, v * P:(v + 1) * P], ident)
                    ins.then_inc(t_done, 1)

                project(0, 0, 0, 0, True)
                pe.wait_ge(rh_ok, h + 1)
                pe.wait_ge(em_ok, 1)
                pe.wait_ge(yg_ok, 5 * h + 1)
                for d, s in enumerate((sel_f, sel_b)):
                    dst = joined(2 + d)
                    mm(dst[:, 0:NC], s[0:64, :], r_head[0:64, 0:NC], start=True, stop=True)
                    mm(dst[:, NC:NT], s[0:64, :], r_head[0:64, NC:NT], start=True, stop=True).then_inc(r_done, 1)
                project(1, 0, 1, 1, True)
                project(0, 1, 2, 0, True)
                project(1, 1, 3, 1, True)
                pe.wait_ge(taken[0], A + 3)
                pe.wait_ge(r_ok, 2 * h + 2)
                v_banks = [0, 4, 5, 6, 7]
                for q in range(4):
                    pe.wait_ge(w_split, U + 4 + q + 1)
                    for kk in range(2):
                        k = 2 * q + kk
                        cols = slice(kk * DV, (kk + 1) * DV)
                        for tt in range(TT):
                            for n, (x, w) in enumerate(((h_hi, w_hi), (h_lo, w_hi), (h_hi, w_lo))):
                                ins = mm(psum[:, v_banks[tt], :], x[:, k, tt * P:(tt + 1) * P],
                                         w[:, q % 2, cols], start=(k == 0 and n == 0),
                                         stop=(k == KD - 1 and n == 2))
                    ins.then_inc(units_done, 1)
                project(1, 2, 8, 0, False)
                pe.wait_ge(v_ok, 5 * h + 1)
                project(0, 2, 9, 1, False)
                scores(0)
                project(1, 3, 10, 0, False)
                scores(1)
                numer(0)
                project(0, 3, 11, 1, False)
                pe.wait_ge(taken[1], A + 5)
                for k in range(KQ):
                    ins = pe.transpose(psum[:, 2, k * P:(k + 1) * P], k_c[:, k, :], ident)
                ins.then_inc(kt_done, 1)
                scores(2)
                numer(1)
                turn(0)
                scores(3)
                numer(2)
                turn(1)
                scores(4)
                numer(3)
                turn(2)
                numer(4)
                turn(3)
                pe.wait_ge(kw_ok, h + 1)
                for v in range(KV + 1):
                    p, tile = v % 2, 4 + (v + 1) // 2
                    pe.wait_ge(taken[p], A + tile + 1)
                    if v < KV:
                        cc = slice(v * P, (v + 1) * P)
                        jobs = [(v_hi[:, 0, cc], kw_hi), (v_lo[:, 0, cc], kw_hi), (v_hi[:, 0, cc], kw_lo)]
                    else:
                        jobs = [(ones_r[:, :], kw_hi), (ones_r[:, :], kw_lo)]
                    for n, (a, b) in enumerate(jobs):
                        ins = mm(psum[:, 2 * p, :], a, b[:, :, :].rearrange("p a b -> p (a b)"),
                                 start=(n == 0), stop=(n == len(jobs) - 1))
                    ins.then_inc(st_done, 1)
                turn(4)

            with pe.Fori(0, KD // 2) as i:
                for p in range(2):
                    pe.wait_ge(taken[p], A_MIX + i + 1)
                    for q in range(2):
                        u = U_MIX + 4 * i + 2 * p + q
                        pe.wait_ge(ygs_ok, 4 + 8 * q + 8)
                        unit_cols(halves(p), u, q, yg_hi, yg_lo, k0=8 * q, first=(q == 0), last=(q == 1))

            with pe.Fori(0, KD // 2) as i:
                for p in range(2):
                    pe.wait_ge(taken[p], A_OUT + i + 1)
                    if p == 0:
                        pe.wait_ge(m_ok, 2 + KD)
                    unit_cols(joined(p), U_OUT + 2 * i + p, p, mg_hi, mg_lo, split320=False)
                for p in range(2):
                    pe.wait_ge(taken[p], A_OUT + i + 2)
                    pe.wait_ge(rows_ok, 2 * i + p + 1)
                    for tt in range(TT):
                        a = (4 + 2 * p) * 512 + tt * P
                        ins = pe.transpose(flat[:, a:a + P], r_t[:, p, tt * P:(tt + 1) * P], ident)
                    ins.then_inc(rt_done, 1)
            pe.wait_ge(xn_ok, TT)
            for j in range(KD):
                p = j % 2
                pe.wait_ge(taken[p], A_XT + j // 2 + 1)
                for tt in range(TT):
                    ins = pe.transpose(joined(p)[:, tt * P:(tt + 1) * P], rows[:, tt, j * P:(j + 1) * P], ident)
                ins.then_inc(xt_done, 1)

            pe.wait_ge(taken[1], A_FF1 + 1)
            with pe.Fori(0, KF) as i:
                for p in range(2):
                    pe.wait_ge(taken[p], A_FF1 + i + 1)
                    unit_cols(halves(p), U_FF1 + 2 * i + p, p, h2_hi, h2_lo)
            pe.wait_ge(f_ok, KF + 1)
            with pe.Fori(0, KD // 2) as i:
                for p in range(2):
                    pe.wait_ge(taken[p], A_FF2 + i + 1)
                    for q in range(2):
                        unit_cols(joined(p), U_FF2 + 4 * i + 2 * p + q, q, f_hi, f_lo, k0=FB * q, nb=FB,
                                  first=(q == 0), last=(q == 1), split320=False, ring=(w2_hi, w2_lo))
                for p in range(2):
                    pe.wait_ge(taken[p], A_FF2 + i + 2)
                    pe.wait_ge(rows2_ok, 2 * i + p + 1)
                    for tt in range(TT):
                        a = (4 + 2 * p) * 512 + tt * P
                        ins = pe.transpose(flat[:, a:a + P], r2_t[:, p, tt * P:(tt + 1) * P], ident)
                    ins.then_inc(rt2_done, 1)

        @block.scalar
        def _(act):
            A_ = act.activation
            act.sem_inc(z_stored, 16)
            for r in range(2):
                act.sem_inc(ga_stored[r], 16)
                act.sem_inc(st_stored[r], 16)
                act.sem_inc(rows_ok, 1)
                act.sem_inc(rows2_ok, 1)
            act.sem_inc(nn_stored, 16)
            act.sem_inc(yg_stored, 16)
            act.sem_inc(x1_stored, 16)
            act.wait_ge(small_in, 16 * 9)
            A_(c_silu[:], c_sb[:], ACT.Silu).then_inc(once, 1)
            A_(ones_r[:], ident, ACT.Identity, bias=1.0, scale=0.0)
            A_(n0_hi[:], n0_sb[:], ACT.Copy).then_inc(once, 1)
            for k in range(KD):
                act.wait_ge(x_mod, 2 * k + 2)
                A_(h_hi[:, k, :], x_sb[:, k, :], ACT.Copy).then_inc(h_hi_ok, 1)
            act.wait_ge(dft_in, 48)
            for hi, st in ((dl_hi[:].rearrange("p a b c -> p (a b c)"), dl_st),
                           (dc_hi[:].rearrange("p a b -> p (a b)"), dc_st),
                           (dx_hi[:].rearrange("p a b -> p (a b)"), dx_st)):
                A_(hi, st[:], ACT.Copy).then_inc(dft_hi_ok, 1)

            with act.Fori(0, NG) as g:
                for p in range(2):
                    act.wait_ge(units_done, U_PASS1 + 2 * g + p + 1)
                    A_(two(uf_hi[:, p, :]), halves(p), ACT.Copy).then_inc(uf_hi_ok, 1)
                for tt in range(TT):
                    act.wait_ge(xch_done, 5 * g + tt + 1)
                    A_(x_hi[:, tt, :], psum[:, 4 + tt % 3, 0:XW], ACT.Copy).then_inc(xch_hi_ok, 1)
                for kind in range(2):
                    act.wait_ge(pos_done, 2 * g + kind + 1)
                    A_(ft_hi[:, NG * kind + g, :], joined(kind), ACT.Copy).then_inc(ft_hi_ok, 1)

            act.dma_start(gate_w[:], wgate).then_inc(gw_in, 16)
            act.wait_ge(gw_in, 16)
            A_(gw_hi[:], gate_w[:], ACT.Copy).then_inc(gate_act, 1)
            with act.Fori(0, KD) as j:
                act.wait_ge(units_done, U_B + 2 * j + 1)
                A_(two(gb_sb[:]), halves(0), ACT.Sigmoid).then_inc(taken[0], 1)
                act.wait_ge(taken[1], A_B + j + 2)
                act.dma_start(z_dram[j], z_sb[:]).then_inc(z_stored, 16)
            act.wait_ge(gate_acc, 1)
            A_(two(gt[:]), psum[:, 5:7, 0:NT // 2], ACT.Identity, bias=gbias[:, 0:1]).then_inc(gate_act, 1)
            act.wait_ge(gate_act, 2)
            A_(gt_e[:], gt[:], ACT.Abs).then_inc(gate_act, 1)
            act.wait_ge(gate_act, 3)
            A_(gt_e[:], gt_e[:], ACT.Exp, scale=-1.0).then_inc(gate_act, 1)
            act.wait_ge(gate_act, 4)
            A_(gt_e[:], gt_e[:], ACT.Ln, bias=1.0).then_inc(gate_act, 1)
            with act.Fori(0, KD // 2) as i:
                for p in range(2):
                    act.wait_ge(units_done, U_GA + 2 * i + p + 1)
                    act.wait_ge(ga_stored[p], 16 * i + 16)
                    A_(two(ga_sb[:, p, :]), halves(p), ACT.Sigmoid).then_inc(taken[p], 1)
                    act.wait_ge(taken[p], A_GA + i + 2)
                    act.dma_start(ga_dram[2 * i + p], ga_sb[:, p, :]).then_inc(ga_stored[p], 16)
            act.wait_ge(gates_ok, 2)
            act.dma_start(new_m[0], em_rows[64:64 + H, NC - 1:NC]).then_inc(m_stored, 16)
            act.dma_start(new_m[1], em_rows[96:96 + H, 0:1]).then_inc(m_stored, 16)
            act.wait_ge(em_acc, 1)
            em_flat = em_t[:].rearrange("p t g c -> p (t g c)")
            A_(em_flat, flat[:, 5 * 512:5 * 512 + NT], ACT.Copy).then_inc(em_ok, 1)
            act.wait_ge(em_ok, 1)
            A_(enm_t[:], em_t[:, :, 2:4, :], ACT.Exp, scale=-1.0).then_inc(em_ok, 1)

            act.wait_ge(m_stored, 32)
            act.wait_ge(z_stored, 16 * (KD + 1))
            for r in range(2):
                act.wait_ge(ga_stored[r], 16 * (KD // 2 + 1))
            with act.Fori(0, H) as h:
                U = U_HEAD + HU * h
                A = A_HEAD + HA * h

                def gate(v):
                    pair = 1 - v % 2
                    act.wait_ge(units_done, U + 8 + v + 1)
                    A_(two(og[:, v, :]), halves(pair), ACT.Tanh, scale=0.5).then_inc(taken[pair], 1)

                def weights(u):
                    act.wait_ge(diag_ok, 5 * h + u + 1)
                    if u == LT:
                        A_(w_sb[:, 0:2, :], w_sb[:, 0:2, :], ACT.Exp).then_inc(e_ok, 1)
                        return
                    A_(w_sb[:, u:u + 2, :], w_sb[:, u:u + 2, :], ACT.Exp)
                    for s in range(u):
                        A_(w_sb[:, s, :], r_sb[:, 0, wlat(u)], ACT.Exp, bias=em_t[:, 1 + s, 0, bass.ds(h, 1)])
                    for s in range(u + 1, LT):
                        A_(w_sb[:, s + 1, :], r_sb[:, 1, wlat(u)], ACT.Exp, bias=em_t[:, 1 + s, 1, bass.ds(h, 1)])
                    for d in range(2):
                        ins = A_(i_sb[:, d, :], r_sb[:, d, wlat(u)], ACT.Exp, bias=m0b[:, d, bass.ds(h, 1)])
                    ins.then_inc(e_ok, 1)

                def p_round(u):
                    act.wait_ge(p_f_ok, 5 * h + u + 1)
                    if u >= 2:
                        act.wait_ge(num_done, 5 * h + u - 1)
                    if u < LT:
                        A_(p_hi[:, u % 2, :, :], w_sb[:], ACT.Copy)
                        A_(qi_hi[:, u % 2, :, :, :], qi_f[:], ACT.Copy).then_inc(p_hi_ok, 1)
                    else:
                        A_(p_hi[:, u % 2, 0:2, :], w_sb[:, 0:2, :], ACT.Copy).then_inc(p_hi_ok, 1)

                def forward(u):
                    act.wait_ge(rec_ok, 5 * h + u + 1)
                    act.wait_ge(num_done, 5 * h + u + 1)
                    A_(h_sb[:], psum[:, 5, :], ACT.Copy, scale=rec[:, 0:1]).then_inc(hf_ok, 1)

                def store(u):
                    tok = wlat(u) if u < LT else slice(0, NC)
                    act.wait_ge(yg_ok, 5 * h + u + 2)
                    act.dma_start(yg_dram[h, :, :, tok].rearrange("v p t -> p v t"), yg_sb[:])\
                        .then_inc(yg_stored, 16)

                def qk(n, dst, scale):
                    act.wait_ge(units_done, U + n + 1)
                    A_(dst[:, n % 2, :], joined(n % 2), ACT.Copy, scale=scale).then_inc(qk_hi_ok, 1)

                qk(0, q_hi, 1.0)
                for d in range(2):
                    act.wait_ge(r_done, 2 * h + d + 1)
                    A_(r_sb[:, d, :], joined(2 + d), ACT.Copy).then_inc(r_ok, 1)
                qk(1, q_hi, 1.0)
                qk(2, k_hi, QSCALE)
                qk(3, k_hi, QSCALE)
                act.wait_ge(c_in, 16 * h + 16)
                A_(c_hi[:], c_raw[:], ACT.Copy).then_inc(c_hi_ok, 1)
                act.wait_ge(units_done, U + 8)
                for tt in range(TT):
                    A_(v_hi[:, tt, :], psum[:, (0, 4, 5, 6, 7)[tt], :], ACT.Copy).then_inc(v_hi_ok, 1)
                weights(0)
                gate(0)
                gate(1)
                p_round(0)
                weights(1)
                gate(2)
                p_round(1)
                forward(0)
                weights(2)
                gate(3)
                p_round(2)
                forward(1)
                weights(3)
                store(0)
                p_round(3)
                forward(2)
                weights(4)
                store(1)
                p_round(4)
                act.wait_ge(taken[1], A + 6)
                A_(kw_hi[:], kw_f[:], ACT.Copy).then_inc(kw_hi_ok, 1)
                forward(3)
                store(2)
                forward(4)
                store(3)
                for v in range(KV + 1):
                    p, tile = v % 2, 4 + (v + 1) // 2
                    act.wait_ge(st_done, 5 * h + v + 1)
                    if v < KV:
                        act.wait_ge(st_stored[p], 32 * h + 16 * (v // 2) + 16)
                        A_(st_sb[:, p, :], psum[:, 2 * p, :], ACT.Copy).then_inc(taken[p], 1)
                        act.wait_ge(taken[p], A + tile + 2)
                        act.dma_start(new_C[:, h, v * P:(v + 1) * P, :].rearrange("a p d -> p a d"),
                                      st_sb[:, p, :].rearrange("p (a d) -> p a d", a=2)).then_inc(st_stored[p], 16)
                    else:
                        act.wait_ge(nn_stored, 16 * h + 16)
                        A_(nn_sb[:], psum[0:1, 2 * p, :], ACT.Copy).then_inc(taken[p], 1)
                        act.wait_ge(taken[p], A + tile + 2)
                        act.dma_start(new_n[:, h, :].unsqueeze(0),
                                      nn_sb[:, :].rearrange("p (a d) -> p a d", a=2)).then_inc(nn_stored, 16)
                store(4)

            with act.Fori(0, H * KV // 4) as i:
                for r in range(4):
                    act.wait_ge(ygs_in[r], 16 * i + 16)
                    A_(yg_hi[:, 4 * i + r, :], yg_st[:, r, :], ACT.Copy,
                       scale=gain_h[:, bass.ds(4 * i + r, 1)]).then_inc(ygs_hi_ok, 1)
            with act.Fori(0, KD) as j:
                act.wait_ge(m_f_ok, j + 1)
                A_(mg_hi[:, j, :], m_sb[:], ACT.Copy).then_inc(m_hi_ok, 1)
            with act.Fori(0, KD // 2) as i:
                for p in range(2):
                    act.wait_ge(rt_done, 2 * i + p + 1)
                    dst = rows[:, :, :].rearrange("p t (j c) -> p t j c", c=P)[:, :, 2 * i + p, :]
                    a = (4 + 2 * p) * 512
                    A_(dst, flat[:, a:a + NT].rearrange("p (t c) -> p t c", c=P), ACT.Copy).then_inc(rows_ok, 1)
            act.wait_ge(var_ok, 1)
            A_(sd[:], sd[:], ACT.Sqrt).then_inc(sd_ok, 1)
            with act.Fori(0, KD // 2) as i:
                for p in range(2):
                    j = 2 * i + p
                    act.wait_ge(xt_done, j + 1)
                    src = joined(p)
                    A_(h2_f[:, 0:NC], src[:, 0:NC], ACT.Identity, scale=h2_s[:, j, 0:1], bias=h2_b[:, j, 0:1])
                    A_(h2_f[:, NC:NT], src[:, NC:NT], ACT.Identity, scale=h2_s[:, j, 1:2],
                       bias=h2_b[:, j, 1:2]).then_inc(h2f_ok, 1)
                    act.wait_ge(h2f_ok, j + 1)
                    A_(h2_hi[:, j, :], h2_f[:], ACT.Copy).then_inc(h2_hi_ok, 1)
                    act.wait_ge(taken[p], A_XT + i + 2)
                    act.dma_start(x1_dram[j], x1_sb[:]).then_inc(x1_stored, 16)

            act.wait_ge(x1_stored, 16 * (KD + 1))
            with act.Fori(0, KF) as i:
                act.wait_ge(units_done, U_FF1 + 2 * i + 1)
                A_(two(s_sb[:]), halves(0), ACT.Silu).then_inc(taken[0], 1)
                act.wait_ge(taken[1], A_FF1 + i + 2)
                A_(f_hi[:, i, :], ff_sb[:], ACT.Copy).then_inc(f_hi_ok, 1)
            act.wait_ge(w_split, U_FF2 + 1)
            with act.Fori(0, KD // 2) as i:
                for p in range(2):
                    act.wait_ge(rt2_done, 2 * i + p + 1)
                    dst = rows2[:, :, :].rearrange("p t (j c) -> p t j c", c=P)[:, :, 2 * i + p, :]
                    a = (4 + 2 * p) * 512
                    A_(dst, flat[:, a:a + NT].rearrange("p (t c) -> p t c", c=P), ACT.Copy).then_inc(rows2_ok, 1)
            act.wait_ge(var2_ok, 1)
            A_(sd[:], sd[:], ACT.Sqrt).then_inc(sd2_ok, 1)

        @block.vector
        def _(v):
            steps = [0]

            def own(ins, value=None):
                steps[0] += 1
                ins.then_inc(dve, 1)
                v.wait_ge(dve, steps[0] if value is None else value(steps[0]))

            def sub(out, a, b):
                return v.tensor_tensor(out, a, b.bitcast(F32), ALU.subtract)

            v.sem_inc(yg_ok, 1)
            v.sem_inc(c_ok, 1)
            v.sem_inc(f_ok, 1)
            for _i in range(2):
                v.sem_inc(m_ok, 1)
            for _i in range(4):
                v.sem_inc(ygs_ok, 1)
            v.wait_ge(small_in, 16 * 9)
            own(v.tensor_scalar(gain_h[:], gain_sb[:], 0.5, None, ALU.mult))
            own(v.tensor_scalar(aln[:], ln_sb[:], ALPHA, None, ALU.mult))
            v.wait_ge(once, 2)
            sub(n0_lo[:], n0_sb[:], n0_hi[:]).then_inc(once_v, 1)
            v.wait_ge(mod_done, MOD1)
            ps_mod = psum[:, 7, 0:2 * NMOD].rearrange("p (m g) -> p m g", g=2)
            own(v.tensor_tensor(mod_sb[:, 0:MOD1, :], ps_mod[:, 0:MOD1, :], bmod_sb[:, 0:MOD1, :], ALU.add))
            own(v.tensor_scalar(mod_sb[:, KD:MOD1, :], mod_sb[:, KD:MOD1, :], 1.0, None, ALU.add))
            v.wait_ge(x_in, 16)

            def h_rest(k):
                v.wait_ge(h_hi_ok, k + 1)
                sub(h_lo[:, k, :], x_sb[:, k, :], h_hi[:, k, :]).then_inc(h_ok, 1)

            for k in range(KD):
                for g, span in enumerate((slice(0, NC), slice(NC, NT))):
                    v.tensor_scalar(x_sb[:, k, span], x_sb[:, k, span], mod_sb[:, KD + k, g:g + 1],
                                    mod_sb[:, k, g:g + 1], ALU.mult, ALU.add).then_inc(x_mod, 1)
                if k >= 1:
                    h_rest(k - 1)
            h_rest(KD - 1)
            for n, (lo, hi, st, form) in enumerate(((dl_lo, dl_hi, dl_st, "p a b c -> p (a b c)"),
                                                    (dc_lo, dc_hi, dc_st, "p a b -> p (a b)"),
                                                    (dx_lo, dx_hi, dx_st, "p a b -> p (a b)"))):
                v.wait_ge(dft_hi_ok, n + 1)
                sub(lo[:].rearrange(form), st[:], hi[:].rearrange(form)).then_inc(dft_ok, 1)

            with v.Fori(0, NG) as g:
                for p in range(2):
                    v.wait_ge(uf_hi_ok, 2 * g + p + 1)
                    sub(two(uf_lo[:, p, :]), halves(p), two(uf_hi[:, p, :])).then_inc(taken[p], 1)
                for tt in range(TT):
                    v.wait_ge(xch_hi_ok, 5 * g + tt + 1)
                    sub(x_lo[:, tt, :], psum[:, 4 + tt % 3, 0:XW], x_hi[:, tt, :]).then_inc(xch_ok, 1)
                for kind in range(2):
                    v.wait_ge(ft_hi_ok, 2 * g + kind + 1)
                    sub(ft_lo[:, NG * kind + g, :], joined(kind), ft_hi[:, NG * kind + g, :])\
                        .then_inc(taken[kind], 1)

            v.wait_ge(gate_act, 1)
            sub(gw_lo[:], gate_w[:], gw_hi[:]).then_inc(gates_ok, 1)
            with v.Fori(0, KD) as j:
                v.wait_ge(taken[0], A_B + j + 2)
                v.wait_ge(units_done, U_B + 2 * j + 2)
                v.wait_ge(z_stored, 16 * j + 16)
                v.tensor_tensor(two(z_sb[:]), halves(1), two(gb_sb[:]), ALU.mult).then_inc(taken[1], 1)

            own(v.memset(one4[:], 1.0))
            own(v.memset(r_rows[:], 0.0))
            own(v.memset(em_rows[:], 0.0))
            v.wait_ge(gate_act, 2)
            own(v.tensor_scalar(gt_m[:], gt[:], 0.0, None, ALU.min))
            v.wait_ge(gate_act, 5)
            own(v.tensor_tensor(gt_m[:], gt_m[:], gt_e[:], ALU.subtract))
            spans = (slice(0, NC), slice(NC, NT))
            backs = (slice(NC - 1, None, -1), slice(NT - 1, NC - 1, -1))
            for src, dst, row in ((gt, igs, 0), (gt_m, lfs, 64)):
                own(v.tensor_copy(dst[:, 0, :], src[row:row + H, :]))
                for s, b in zip(spans, backs):
                    own(v.tensor_copy(dst[:, 1, s], src[row + 32:row + 32 + H, b]))
            for d in range(2):
                for n, s in enumerate(spans):
                    own(v.tensor_tensor_scan(bs[:, d, s], one4[:, s], lfs[:, d, s], 0.0, ALU.mult, ALU.add))
                    own(v.tensor_tensor_scan(ms[:, d, s], lfs[:, d, s], igs[:, d, s],
                                             m0r[:, d:d + 1] if n else 0.0, ALU.add, ALU.max))
            own(v.tensor_tensor(r_rows[0:H, :], bs[:, 0, :], ms[:, 0, :], ALU.subtract))
            own(v.tensor_tensor(em_rows[0:H, :], igs[:, 0, :], bs[:, 0, :], ALU.subtract))
            own(v.tensor_copy(em_rows[64:64 + H, :], ms[:, 0, :]))
            for s, b in zip(spans, backs):
                own(v.tensor_tensor(r_rows[32:32 + H, s], bs[:, 1, b], ms[:, 1, b], ALU.subtract))
                own(v.tensor_tensor(em_rows[32:32 + H, s], igs[:, 1, b], bs[:, 1, b], ALU.subtract))
                if s is spans[0]:
                    own(v.tensor_copy(em_rows[96:96 + H, s], ms[:, 1, b]))
                else:
                    v.tensor_copy(em_rows[96:96 + H, s], ms[:, 1, b]).then_inc(gates_ok, 1)
            v.wait_ge(mod_done, NMOD)
            own(v.tensor_tensor(mod_sb[:, MOD1:NMOD, :], ps_mod[:, MOD1:NMOD, :], bmod_sb[:, MOD1:NMOD, :], ALU.add))
            own(v.tensor_scalar(mod_sb[:, 4 * KD:5 * KD, :], mod_sb[:, 4 * KD:5 * KD, :], 1.0, None, ALU.add))
            lg = ln_sb[:, 0, :].unsqueeze(2).broadcast_to([P, KD, 2])
            lb = ln_sb[:, 1, :].unsqueeze(2).broadcast_to([P, KD, 2])
            own(v.tensor_tensor(h2_s[:], mod_sb[:, 4 * KD:5 * KD, :], lg, ALU.mult))
            own(v.tensor_tensor(h2_b[:], mod_sb[:, 4 * KD:5 * KD, :], lb, ALU.mult))
            own(v.tensor_tensor(h2_b[:], h2_b[:], mod_sb[:, 3 * KD:4 * KD, :], ALU.add))

            base = steps[0]
            PER_HEAD = 92
            with v.Fori(0, H) as h:
                U = U_HEAD + HU * h
                A = A_HEAD + HA * h
                steps[0] = 0

                def chain(ins):
                    steps[0] += 1
                    ins.then_inc(dve, 1)
                    v.wait_ge(dve, h * PER_HEAD + (base + steps[0]))

                def diag(u):
                    if u == 0:
                        v.wait_ge(r_ok, 2 * h + 2)
                        v.wait_ge(em_ok, 2)
                    else:
                        v.wait_ge(p_ok, 5 * h + u)
                    pos, tile, tok = (u, 1 + u, wlat(u)) if u < LT else (0, 0, slice(0, NC))
                    v.scalar_tensor_tensor(out=w_sb[:, pos, :], in0=r_sb[:, 0, tok],
                                           scalar=em_t[:, tile, 0, bass.ds(h, 1)], in1=mask_f,
                                           op0=ALU.add, op1=ALU.add)
                    v.scalar_tensor_tensor(out=w_sb[:, pos + 1, :], in0=r_sb[:, 1, tok],
                                           scalar=em_t[:, tile, 1, bass.ds(h, 1)], in1=mask_b,
                                           op0=ALU.add, op1=ALU.add).then_inc(diag_ok, 1)

                def probs(u):
                    v.wait_ge(e_ok, 5 * h + u + 1)
                    if u == LT:
                        chain(v.tensor_copy(wg[:, 0:1], w_sb[:, 0, NC - 1:NC]))
                        chain(v.tensor_copy(wg[:, 1:2], w_sb[:, 1, 0:1]))
                    v.wait_ge(s_done, 5 * h + u + 1)
                    if u < LT:
                        s4 = psum[:, 4, :].rearrange("p (s t) -> p s t", t=P)
                        v.tensor_tensor(w_sb[:, 0:u + 1, :], w_sb[:, 0:u + 1, :], s4[:, 0:u + 1, :], ALU.mult)
                        v.tensor_tensor(w_sb[:, u + 1:, :], w_sb[:, u + 1:, :], s4[:, u:, :], ALU.mult)\
                            .then_inc(s_free, 1)
                        for d in range(2):
                            ins = v.tensor_tensor(qi_f[:, d, :, :], q_f[:, :, u * P:(u + 1) * P],
                                                  i_sb[:, d, :].unsqueeze(1).broadcast_to([P, KQ, P]), ALU.mult)
                        ins.then_inc(p_f_ok, 1)
                    else:
                        s1 = psum[:, 4, 0:P]
                        v.tensor_tensor(w_sb[:, 0, :], w_sb[:, 0, :], s1, ALU.mult)
                        v.tensor_tensor(w_sb[:, 1, :], w_sb[:, 1, :], s1, ALU.mult).then_inc(s_free, 1)
                        v.wait_ge(s_free, 5 * h + 5)
                        v.sem_inc(p_f_ok, 1)

                def p_rest(u):
                    v.wait_ge(p_hi_ok, 5 * h + u + 1)
                    if u < LT:
                        sub(p_lo[:, u % 2, :, :], w_sb[:], p_hi[:, u % 2, :, :])
                        sub(qi_lo[:, u % 2, :, :, :], qi_f[:], qi_hi[:, u % 2, :, :, :]).then_inc(p_ok, 1)
                    else:
                        sub(p_lo[:, u % 2, 0:2, :], w_sb[:, 0:2, :], p_hi[:, u % 2, 0:2, :]).then_inc(p_ok, 1)

                def combine(u):
                    tile = 1 + u if u < LT else 0
                    v.wait_ge(den_done, 5 * h + u + 1)
                    den = psum[:, 7, 0:4].rearrange("p (a b) -> p a b", b=2)[:, :, 0]
                    chain(v.scalar_tensor_tensor(out=den_sb[:], in0=den, scalar=-1.0, in1=enm_t[:, tile, :, h],
                                                 op0=ALU.mult, op1=ALU.max))
                    v.tensor_tensor(den_sb[:], den, den_sb[:], ALU.max).then_inc(den_read, 1)
                    v.wait_ge(den_read, 5 * h + u + 1)
                    v.reciprocal(rec[:], den_sb[:]).then_inc(rec_ok, 1)
                    v.wait_ge(rec_ok, 5 * h + u + 1)
                    v.wait_ge(hf_ok, 5 * h + u + 1)
                    v.scalar_tensor_tensor(out=h_sb[:], in0=psum[:, 6, :], scalar=rec[:, 1:2], in1=h_sb[:],
                                           op0=ALU.mult, op1=ALU.add).then_inc(num_free, 1)
                    v.wait_ge(num_free, 5 * h + u + 1)
                    chain(v.bn_stats(stats[:, 0, 0, :], h_sb[:]))
                    v.sem_inc(stats_seen, 1)
                    chain(v.bn_aggr(mv[:, 0, :], stats[:, 0, 0, :]))
                    chain(v.tensor_scalar(nt_v[:], mv[:, 0, 1:2], EPS, None, ALU.add))
                    chain(v.tensor_scalar(nt_a[:].bitcast(I32), nt_v[:].bitcast(I32), 1, None,
                                          ALU.logical_shift_right))
                    chain(v.tensor_scalar(nt_y[:].bitcast(I32), nt_a[:].bitcast(I32), -1.0, MAGIC,
                                          ALU.mult, ALU.add))
                    for _n in range(4):
                        chain(v.scalar_tensor_tensor(out=nt_a[:], in0=nt_y[:], scalar=nt_v[:, 0:1], in1=nt_y[:],
                                                     op0=ALU.mult, op1=ALU.mult))
                        chain(v.tensor_scalar(nt_a[:], nt_a[:], -0.5, 1.5, ALU.mult, ALU.add))
                        chain(v.tensor_tensor(nt_y[:], nt_y[:], nt_a[:], ALU.mult))
                    if u >= 1:
                        v.wait_ge(t_done, 5 * h + u)
                    v.tensor_scalar(hn_sb[:], h_sb[:], mv[:, 0, 0:1], nt_y[:, 0:1], ALU.subtract, ALU.mult)\
                        .then_inc(hn_ok, 1)

                def gated(u):
                    tok = wlat(u) if u < LT else slice(0, NC)
                    v.wait_ge(t_done, 5 * h + u + 1)
                    v.wait_ge(taken[0], A + 5)
                    v.wait_ge(taken[1], A + 5)
                    v.wait_ge(yg_stored, 80 * h + 16 * u + 16)
                    v.scalar_tensor_tensor(out=yg_sb[:], in0=og[:, :, tok], scalar=1.0,
                                           in1=psum[:, 7, :].rearrange("p (v t) -> p v t", t=P),
                                           op0=ALU.add, op1=ALU.mult).then_inc(yg_ok, 1)

                v.tensor_scalar(r_head[:], r_rows[:], onehot[:, bass.ds(h, 1)], None, ALU.mult).then_inc(rh_ok, 1)
                for n in range(4):
                    v.wait_ge(qk_hi_ok, 4 * h + n + 1)
                    src = joined(n % 2)
                    if n < 2:
                        v.tensor_copy(q_f[:, n, :], src[:, NC:NT])
                        sub(q_lo[:, n, :], src, q_hi[:, n, :]).then_inc(taken[n % 2], 1)
                    else:
                        v.tensor_scalar(k_c[:, n % 2, :], src[:, 0:NC], QSCALE, None, ALU.mult)
                        v.scalar_tensor_tensor(out=k_lo[:, n % 2, :], in0=src, scalar=QSCALE,
                                               in1=k_hi[:, n % 2, :].bitcast(F32), op0=ALU.mult,
                                               op1=ALU.subtract).then_inc(taken[n % 2], 1)
                v.wait_ge(c_hi_ok, h + 1)
                sub(c_lo[:], c_raw[:], c_hi[:]).then_inc(c_ok, 1)
                diag(0)
                for tt in range(TT):
                    v.wait_ge(v_hi_ok, 5 * h + tt + 1)
                    sub(v_lo[:, tt, :], psum[:, (0, 4, 5, 6, 7)[tt], :], v_hi[:, tt, :]).then_inc(v_ok, 1)
                probs(0)
                p_rest(0)
                diag(1)
                probs(1)
                p_rest(1)
                combine(0)
                diag(2)
                probs(2)
                p_rest(2)
                combine(1)
                gated(0)
                diag(3)
                probs(3)
                p_rest(3)
                combine(2)
                gated(1)
                diag(4)
                probs(4)
                p_rest(4)
                v.wait_ge(kt_done, h + 1)
                v.tensor_scalar(kw_f[:, 0, :], psum[:, 2, 0:DQK], wg[:, 0:1], None, ALU.mult)
                v.tensor_scalar(kw_f[:, 1, :], psum[:, 2, 0:DQK], wg[:, 1:2], None, ALU.mult).then_inc(taken[1], 1)
                v.wait_ge(kw_hi_ok, h + 1)
                sub(kw_lo[:], kw_f[:], kw_hi[:]).then_inc(kw_ok, 1)
                combine(3)
                gated(2)
                combine(4)
                gated(3)
                gated(4)
                assert steps[0] == PER_HEAD
            steps[0] = base + H * PER_HEAD

            with v.Fori(0, H * KV // 4) as i:
                for r in range(4):
                    v.wait_ge(ygs_hi_ok, 4 * i + r + 1)
                    v.scalar_tensor_tensor(out=yg_lo[:, 4 * i + r, :], in0=yg_st[:, r, :],
                                           scalar=gain_h[:, bass.ds(4 * i + r, 1)],
                                           in1=yg_hi[:, 4 * i + r, :].bitcast(F32),
                                           op0=ALU.mult, op1=ALU.subtract).then_inc(ygs_ok, 1)
            base2 = steps[0]
            with v.Fori(0, KD // 2) as i:
                for p in range(2):
                    j = 2 * i + p
                    v.wait_ge(units_done, U_MIX + 4 * i + 2 * p + 2)
                    v.wait_ge(zg_in[p], 32 * i + 32)
                    v.wait_ge(m_ok, j + 2)
                    v.tensor_tensor(two(m_sb[:]), halves(p), two(g_st[:, p, :]), ALU.mult).then_inc(taken[p], 1)
                    v.wait_ge(taken[p], A_MIX + i + 2)
                    v.tensor_tensor(m_sb[:], m_sb[:], z_st[:, p, :], ALU.add).then_inc(m_f_ok, 1)
                    v.wait_ge(m_hi_ok, j + 1)
                    sub(mg_lo[:, j, :], m_sb[:], mg_hi[:, j, :]).then_inc(m_ok, 1)

            def residual(i, p, unit, a_first, landed, st, rt, gcol):
                j = 2 * i + p
                v.wait_ge(units_done, unit)
                v.wait_ge(landed[p], 16 * i + 16)
                src = joined(p)
                for g, span in enumerate((slice(0, NC), slice(NC, NT))):
                    ins = v.scalar_tensor_tensor(out=rt[:, p, span], in0=src[:, span],
                                                 scalar=mod_sb[:, gcol + j, g:g + 1],
                                                 in1=st[:, p, span], op0=ALU.mult, op1=ALU.add)
                ins.then_inc(taken[p], 1)

            with v.Fori(0, KD // 2) as i:
                for p in range(2):
                    j = 2 * i + p
                    v.wait_ge(xs_in[p], 16 * i + 16)
                    ins = v.tensor_scalar(x_st[:, p, :], x_st[:, p, :], ALPHA, None, ALU.mult)
                    ins.then_inc(dve, 1)
                    v.wait_ge(dve, 2 * i + (base2 + p + 1))
                    residual(i, p, U_OUT + 2 * i + p + 1, A_OUT, xs_in, x_st, r_t, 2 * KD)
            steps[0] = base2 + KD

            def norm_rows(src, ok, var_sem, sd_sem, done, gains=None):
                v.wait_ge(ok, KD + 2)
                for tt in range(TT):
                    for b in range(2):
                        own(v.bn_stats(stats[:, tt, b, :], src[:, tt, b * 512:(b + 1) * 512]))
                    own(v.bn_aggr(mv[:, tt, :], stats[:, tt, :, :]))
                v.tensor_scalar(sd[:], mv[:, :, 1], EPS, None, ALU.add).then_inc(var_sem, 1)
                v.wait_ge(sd_sem, 1)
                own(v.reciprocal(rstd[:], sd[:]))
                for tt in range(TT):
                    ins = v.tensor_scalar(src[:, tt, :], src[:, tt, :], mv[:, tt, 0:1], rstd[:, tt:tt + 1],
                                          ALU.subtract, ALU.mult)
                    if gains is None:
                        ins.then_inc(done, 1)
                        continue
                    own(ins)
                    own(v.tensor_tensor(src[:, tt, :], src[:, tt, :], gains[:, 0, :], ALU.mult))
                    v.tensor_tensor(src[:, tt, :], src[:, tt, :], gains[:, 1, :], ALU.add).then_inc(done, 1)

            norm_rows(rows, rows_ok, var_ok, sd_ok, xn_ok)
            with v.Fori(0, KD // 2) as i:
                for p in range(2):
                    j = 2 * i + p
                    v.wait_ge(xt_done, j + 1)
                    v.wait_ge(x1_stored, 32 * i + 16 * p + 16)
                    v.wait_ge(h2_hi_ok, j + 1)
                    v.tensor_scalar(x1_sb[:], joined(p), aln[:, 0, bass.ds(j, 1)], aln[:, 1, bass.ds(j, 1)],
                                    ALU.mult, ALU.add).then_inc(x1_ok, 1)
                    v.wait_ge(x1_ok, j + 1)
                    sub(h2_lo[:, j, :], h2_f[:], h2_hi[:, j, :]).then_inc(taken[p], 1)

            with v.Fori(0, KF) as i:
                v.wait_ge(taken[0], A_FF1 + i + 2)
                v.wait_ge(units_done, U_FF1 + 2 * i + 2)
                v.wait_ge(f_ok, i + 1)
                v.tensor_tensor(two(ff_sb[:]), halves(1), two(s_sb[:]), ALU.mult).then_inc(taken[1], 1)
                v.wait_ge(f_hi_ok, i + 1)
                sub(f_lo[:, i, :], ff_sb[:], f_hi[:, i, :]).then_inc(f_ok, 1)
            with v.Fori(0, KD // 2) as i:
                for p in range(2):
                    residual(i, p, U_FF2 + 4 * i + 2 * p + 2, A_FF2, x1s_in, x2_st, r2_t, 5 * KD)
            v.wait_ge(lnr_in, 16)
            norm_rows(rows2, rows2_ok, var2_ok, sd2_ok, y_ok, ln_row)


_OUTS = [("y_prompt", (NC, DMODEL)), ("y_sample", (NL, DMODEL)), ("new_C", (2, H, DV, DQK)),
         ("new_n", (2, H, DQK)), ("new_m", (2, H, 1))]


def dft_constants():
    c = np.arange(DG)
    ang = 2 * np.pi * np.outer(c, c) / DG
    cos, sin = np.cos(ang) / np.sqrt(DG), np.sin(ang) / np.sqrt(DG)
    chan = np.zeros((DG, XW))
    chan[:, 0:P] = cos[:, 0:P]
    chan[:, 0] = (cos[:, 0] + cos[:, P]) / 2
    chan[:, P:2 * P] = sin[:, 0:P]
    chan[:, 2 * P] = (cos[:, P] - cos[:, 0]) / 2
    t = np.arange(NC)
    a = 2 * np.pi * np.outer(t, t) / NC
    pos_c = np.stack([np.cos(a), np.sin(a)]) / np.sqrt(NC)
    r, w = np.arange(NL) // GRID_W, np.arange(NL) % GRID_W
    a = 2 * np.pi * (np.outer(r, r) * GRID_W / NL + np.outer(w, w) / GRID_W)
    pos_l = np.stack([np.cos(a), np.sin(a)]) / np.sqrt(NL)
    f = np.float32
    return (np.ascontiguousarray(pos_c.transpose(1, 0, 2), f).reshape(P, 2 * NC),
            np.ascontiguousarray(pos_l.reshape(2, LT, P, NL).transpose(2, 0, 1, 3), f).reshape(P, 2 * LT * NL),
            np.ascontiguousarray(chan.reshape(2, P, XW).transpose(1, 0, 2), f).reshape(P, 2 * XW))


def const_block():
    s, t = np.arange(P)[:, None], np.arange(P)[None, :]
    out = np.zeros((P, 5 * P + H), np.float32)
    out[:, 0:P] = np.eye(P)
    out[:, P:2 * P] = np.where(s <= t, 0.0, -1e30)
    out[:, 2 * P:3 * P] = np.where(s >= t, 0.0, -1e30)
    out[0:H, 3 * P:4 * P] = 1.0
    out[32:32 + H, 4 * P:5 * P] = 1.0
    for h in range(H):
        out[h, 5 * P + h] = out[32 + h, 5 * P + h] = 1.0
    return out


def blocks(w):
    k, n = w.shape
    return w.reshape(k // P, P, n // P, P).transpose(2, 1, 0, 3).reshape(n // P, P, k)


def kernel(**inputs):
    import concourse.bacc as _bacc
    from concourse.bass_utils import run_bass_kernel_spmd as _run

    a = {k: np.asarray(v) for k, v in inputs.items()}
    w_in = a["w_in"][0]
    cuts = [0, H * DQK, 2 * H * DQK, 2 * H * DQK + DM, 2 * H * DQK + 2 * DM]
    g_end = cuts[4] + 4 * H
    wq, wk, wv, wo = (w_in[:, cuts[i]:cuts[i + 1]] for i in range(4))
    wg = w_in[:, cuts[4]:g_end]
    wf, wga, wgb = (w_in[:, g_end + i * DMODEL:g_end + (i + 1) * DMODEL] for i in range(3))
    wb = a["w_branch_b"][0].reshape(NG, DG, KD, P)
    low = wb[:, 0:P]
    high = np.concatenate([wb[:, P:P + 1], wb[:, :P:-1]], axis=1)
    ub = np.stack([low, high]).transpose(3, 2, 0, 1, 4).reshape(KD, P, UW)
    gb = blocks(wgb)
    q, k, o = blocks(wq), blocks(wk), blocks(wo)
    vv = wv.reshape(4, 2, P, H, DV).transpose(3, 0, 2, 1, 4).reshape(H, 4, P, 2 * DV)
    wa = blocks(a["w_branch_a"][0]).reshape(KD, P, 2, UW).transpose(0, 2, 1, 3)
    ffi = blocks(a["w_ffn_in"][0])
    parts = [blocks(wf), np.stack([gb, ub], axis=1).reshape(2 * KD, P, UW), blocks(wga)]
    for h in range(H):
        parts += [q[2 * h:2 * h + 2], k[2 * h:2 * h + 2], vv[h], o[4 * h:4 * h + 4]]
    parts += [wa.reshape(2 * KD, P, UW), blocks(a["w_out"][0]),
              np.stack([ffi[:KF], ffi[KF:]], axis=1).reshape(2 * KF, P, UW)]
    wunits = np.concatenate(parts)
    wffo = blocks(a["w_ffn_out"][0]).reshape(KD, P, 2, FW).transpose(0, 2, 1, 3).reshape(2 * KD, P, FW)
    gates = np.zeros((KD, P, P), np.float32)
    gbias = np.zeros((P, 1), np.float32)
    for d in range(2):
        for kind in range(2):
            row, col = 64 * kind + 32 * d, (2 * d + kind) * H
            gates[:, :, row:row + H] = wg[:, col:col + H].reshape(KD, P, H)
            gbias[row:row + H, 0] = a["b_gate"][0][col:col + H]
    x = np.concatenate([a["x_prompt"][0], a["x_sample"][0]])
    cc = np.stack([a["c_ctx"], a["c"][0]])
    sm = a["state_m"][0, 0]
    sn = a["state_n"][0, 0].reshape(2, H, KQ, P).transpose(3, 1, 0, 2)
    pos_c, pos_l, chan = dft_constants()
    ln = np.stack([a["ln_gain"][0], a["ln_bias"][0]], axis=1)
    arrays = {
        "wunits": wunits, "wffo": wffo, "wmod": blocks(a["w_mod"][0]),
        "xT": x.reshape(NT, KD, P).transpose(2, 1, 0), "cT": cc.reshape(2, KD, P).transpose(2, 1, 0),
        "bmod": np.repeat(a["b_mod"][0].reshape(NMOD, P).T[:, :, None], 2, axis=2),
        "consts": const_block(), "dft_c": pos_c, "dft_l": pos_l, "dft_x": chan,
        "wgate": gates.transpose(1, 0, 2).reshape(P, UW), "gate_bias": gbias,
        "stateC": a["state_C"][0, 0].reshape(2, H, DV, KQ, P).transpose(1, 4, 0, 3, 2),
        "state_n": np.repeat(sn[..., None], 2, axis=4), "m0_rows": sm.T,
        "m0_bcast": np.repeat(sm[None], P, axis=0), "gainT": a["mh_gain"][0].reshape(H * KV, P).T,
        "lnT": ln[0].reshape(2, KD, P).transpose(2, 0, 1), "ln_rows": np.repeat(ln[1][None], P, axis=0),
    }
    nc = _bacc.Bacc("TRN2", target_bir_lowering=False, num_devices=1)
    args, host = [], {}
    for name, value in arrays.items():
        value = np.ascontiguousarray(value)
        host[f"in_{name}"] = value
        args.append(nc.dram_tensor(f"in_{name}", value.shape, F32, kind="ExternalInput").ap())
    for name, shape in _OUTS:
        args.append(nc.dram_tensor(f"out_{name}", shape, F32, kind="ExternalOutput").ap())
    build(nc, *args)
    r = _run(nc, [host], core_ids=[0]).results[0]
    return (r["out_y_prompt"][None], r["out_y_sample"][None], r["out_new_C"][None, None],
            r["out_new_n"][None, None], r["out_new_m"][None, None, :, :, 0])
```

```python
from contextlib import ExitStack

import numpy as np

import concourse.bass as bass
from concourse import mybir

F32 = mybir.dt.float32
F32R = mybir.dt.float32r
I32 = mybir.dt.int32
ALU = mybir.AluOpType
ACT = mybir.ActivationFunctionType

P = 128
DMODEL = 1024
NC = 128
NL = 512
NT = NC + NL
TT = NT // P
LT = NL // P
GRID_W = 64
H = 4
DM = 2 * DMODEL
DV = DM // H
DQK = DV // 2
KD = DMODEL // P
KQ = DQK // P
KV = DV // P
NG = 4
DG = DMODEL // NG
CUT = 256
XW = DG + 2
DFF = ((8 * DMODEL // 3 + 255) // 256) * 256
KF = DFF // P
ALPHA = float(np.float32(2.0 ** 0.25))
EPS = 1e-5
QSCALE = DQK ** -0.5
UB = 8
UW = UB * P
FB = KF // 2
FW = FB * P

U_PASS1 = 0
U_B = 2 * NG
U_HEAD = U_B + 2 * KD
HU = 2 * KQ + 4 + KV
U_GA = U_HEAD + H * HU
U_MIX = U_GA + KD
U_OUT = U_MIX + 2 * KD
U_FF1 = U_OUT + KD
U_FF2 = U_FF1 + 2 * KF
U_END = U_FF2 + 2 * KD
NMOD = 6 * KD
MOD1 = 2 * KD

A_F = 0
A_B = A_F + 2 * NG
A_HEAD = A_B + KD
HA = 7
A_GA = A_HEAD + HA * H
A_MIX = A_GA + 3 + KD // 2
A_OUT = A_MIX + KD // 2
A_XT = A_OUT + KD // 2
A_FF1 = A_XT + KD // 2
A_FF2 = A_FF1 + KF
MAGIC = float(0x5F3759DF)


def build(nc, wunits, wffo, wmod, xT, cT, bmod, consts, dft_c, dft_l, dft_x, wgate, gate_bias,
          stateC, state_n, m0_rows, m0_bcast, gainT, lnT, ln_rows,
          y_prompt, y_sample, new_C, new_n, new_m):
    ctx = ExitStack()
    with ctx:
        sem = lambda name: ctx.enter_context(nc.semaphore(name))
        psum = ctx.enter_context(nc.psum_tensor("psum", [P, 8, 512], F32))
        flat = psum[:, :, :].rearrange("p b c -> p (b c)")

        z_dram = nc.dram_tensor("z_dram", [KD, P, NT], F32, kind="Internal").ap()
        yg_dram = nc.dram_tensor("yg_dram", [H, KV, P, NT], F32, kind="Internal").ap()
        x1_dram = nc.dram_tensor("x1_dram", [KD, P, NT], F32, kind="Internal").ap()

        top = [(nc.sbuf_base + 63) // 64 * 64]

        def at(name, shape, dt, cursor):
            t = nc.alloc_sbuf_tensor_at(name, shape, dt, offset=cursor[0])
            size = int(np.prod(shape[1:])) * 4
            cursor[0] += (size + 63) // 64 * 64
            assert cursor[0] <= nc.sbuf_usable_end, (name, cursor[0])
            return t

        keep = lambda name, shape, dt=F32: at(name, shape, dt, top)
        const_sb = keep("const_sb", [P, 5 * P + H])
        ident, mask_f, mask_b, sel_f, sel_b = (const_sb[:, i * P:(i + 1) * P] for i in range(5))
        onehot = const_sb[:, 5 * P:5 * P + H]
        ones_r = keep("ones_r", [P, P], F32R)
        c_sb = keep("c_sb", [P, KD, 2])
        c_silu = keep("c_silu", [P, KD, 2])
        bmod_sb = keep("bmod_sb", [P, NMOD, 2])
        mod_sb = keep("mod_sb", [P, NMOD, 2])
        gbias = keep("gbias", [P, 1])
        zero = keep("zero", [P, 1])
        em_t = keep("em_t", [P, TT, 4, 32])
        enm_t = keep("enm_t", [P, TT, 2, 32])
        r_rows = keep("r_rows", [P, NT])
        r_head = keep("r_head", [P, NT])
        m0r = keep("m0r", [H, 2])
        m0b = keep("m0b", [P, 2, H])
        n0_sb = keep("n0_sb", [P, H, 2, KQ, 2])
        n0_hi = keep("n0_hi", [P, H, 2, KQ, 2], F32R)
        n0_lo = keep("n0_lo", [P, H, 2, KQ, 2], F32R)
        gain_sb = keep("gain_sb", [P, H * KV])
        gain_h = keep("gain_h", [P, H * KV])
        ln_sb = keep("ln_sb", [P, 2, KD])
        aln = keep("aln", [P, 2, KD])
        h2_s = keep("h2_s", [P, KD, 2])
        h2_b = keep("h2_b", [P, KD, 2])
        stats = keep("stats", [P, TT, 2, 6])
        mv = keep("mv", [P, TT, 2])
        rstd = keep("rstd", [P, TT])
        sd = keep("sd", [P, TT])
        den_sb = keep("den_sb", [P, 2])
        rec = keep("rec", [P, 2])
        wg = keep("wg", [P, 2])
        nt_v = keep("nt_v", [P, 1])
        nt_y = keep("nt_y", [P, 1])
        nt_a = keep("nt_a", [P, 1])

        c1 = [top[0]]
        raw = at("raw", [P, 2, UW], F32, c1)
        w_hi = at("w_hi", [P, 2, UW], F32R, c1)
        w_lo = at("w_lo", [P, 2, UW], F32R, c1)
        ring_end = c1[0]
        h_hi = at("h_hi", [P, KD, NT], F32R, c1)
        h_lo = at("h_lo", [P, KD, NT], F32R, c1)
        h_end = c1[0]
        c0 = [h_end]
        x_sb = at("x_sb", [P, KD, NT], F32, c0)
        mod_first = at("mod_first", [P, 8, UW], F32, c0)
        sum_first = at("sum_first", [P, 2, UW], F32, c0)
        prod = at("prod", [P, 4, UW // 2], F32, c0)
        cs = [h_end + 4 * KD * NT]
        dl_st = at("dl_st", [P, 2 * LT * NL], F32, cs)
        dc_st = at("dc_st", [P, 2 * NC], F32, cs)
        dx_st = at("dx_st", [P, 2 * XW], F32, cs)
        assert cs[0] <= h_end + 2 * 4 * 2 * NG * NT
        cp = [h_end]
        ft_hi = at("ft_hi", [P, 2 * NG, NT], F32R, cp)
        ft_lo = at("ft_lo", [P, 2 * NG, NT], F32R, cp)
        uf_hi = at("uf_hi", [P, 2, NT], F32R, cp)
        uf_lo = at("uf_lo", [P, 2, NT], F32R, cp)
        x_hi = at("xch_hi", [P, TT, XW], F32R, cp)
        x_lo = at("xch_lo", [P, TT, XW], F32R, cp)
        dl_hi = at("dl_hi", [P, 2, LT, NL], F32R, cp)
        dl_lo = at("dl_lo", [P, 2, LT, NL], F32R, cp)
        dc_hi = at("dc_hi", [P, 2, NC], F32R, cp)
        dc_lo = at("dc_lo", [P, 2, NC], F32R, cp)
        dx_hi = at("dx_hi", [P, 2, XW], F32R, cp)
        dx_lo = at("dx_lo", [P, 2, XW], F32R, cp)
        cp_end = cp[0]
        wb_sum = at("wb_sum", [P, UW], F32, cp)
        mod_ring = at("mod_ring", [P, 2, UW], F32, cp)
        mod_sum = at("mod_sum", [P, 2, UW], F32, cp)
        gate_w = wb_sum
        gw_hi = at("gw_hi", [P, UW], F32R, cp)
        gw_lo = at("gw_lo", [P, UW], F32R, cp)
        cq = [uf_hi_off := h_end + 2 * 2 * NG * NT * 4]
        gb_sb = at("gb_sb", [P, NT], F32, cq)
        z_sb = at("z_sb", [P, NT], F32, cq)
        gt = at("gt", [P, NT], F32, cq)
        gt_e = at("gt_e", [P, NT], F32, cq)
        gt_m = at("gt_m", [P, NT], F32, cq)
        igs = at("igs", [H, 2, NT], F32, cq)
        lfs = at("lfs", [H, 2, NT], F32, cq)
        bs = at("bs", [H, 2, NT], F32, cq)
        ms = at("ms", [H, 2, NT], F32, cq)
        one4 = at("one4", [H, NT], F32, cq)
        em_rows = at("em_rows", [P, NT], F32, cq)
        assert cq[0] <= cp_end
        ch = [h_end]
        q_hi = at("q_hi", [P, KQ, NT], F32R, ch)
        q_lo = at("q_lo", [P, KQ, NT], F32R, ch)
        k_hi = at("k_hi", [P, KQ, NT], F32R, ch)
        k_lo = at("k_lo", [P, KQ, NT], F32R, ch)
        q_f = at("q_f", [P, KQ, NL], F32, ch)
        k_c = at("k_c", [P, KQ, NC], F32, ch)
        v_hi = at("v_hi", [P, TT, DV], F32R, ch)
        v_lo = at("v_lo", [P, TT, DV], F32R, ch)
        og = at("og", [P, KV, NT], F32, ch)
        r_sb = at("r_sb", [P, 2, NT], F32, ch)
        w_sb = at("w_sb", [P, 2, LT + 1, P], F32, ch)
        i_sb = at("i_sb", [P, 2, 2, P], F32, ch)
        qi_f = at("qi_f", [P, 2, KQ, P], F32, ch)
        p_hi = at("p_hi", [P, 2, LT + 1, P], F32R, ch)
        p_lo = at("p_lo", [P, 2, LT + 1, P], F32R, ch)
        qi_hi = at("qi_hi", [P, 2, 2, KQ, P], F32R, ch)
        qi_lo = at("qi_lo", [P, 2, 2, KQ, P], F32R, ch)
        c_raw = at("c_raw", [P, 2, KQ, DV], F32, ch)
        c_hi = at("c_hi", [P, 2, KQ, DV], F32R, ch)
        c_lo = at("c_lo", [P, 2, KQ, DV], F32R, ch)
        kw_f = at("kw_f", [P, 2, DQK], F32, ch)
        kw_hi = at("kw_hi", [P, 2, DQK], F32R, ch)
        kw_lo = at("kw_lo", [P, 2, DQK], F32R, ch)
        h_sb = at("h_sb", [P, DV], F32, ch)
        hn_sb = at("hn_sb", [P, DV], F32, ch)
        yg_sb = at("yg_sb", [P, KV, P], F32, ch)
        st_sb = at("st_sb", [P, 2, 2 * DQK], F32, ch)
        nn_sb = at("nn_sb", [1, 2 * DQK], F32, ch)
        cm = [h_end]
        yg_hi = at("yg_hi", [P, H * KV, NT], F32R, cm)
        yg_lo = at("yg_lo", [P, H * KV, NT], F32R, cm)
        ga_sb = at("ga_sb", [P, KD, NT], F32, cm)
        z_st = at("z_st", [P, 2, NT], F32, cm)
        m_sb = at("m_sb", [P, NT], F32, cm)
        yg_st = at("yg_st", [P, 4, NT], F32, cm)
        cg = [ring_end]
        mg_hi = at("mg_hi", [P, KD, NT], F32R, cg)
        mg_lo = at("mg_lo", [P, KD, NT], F32R, cg)
        assert cg[0] <= h_end
        co = [h_end]
        x_st = at("x_st", [P, 2, NT], F32, co)
        r_t = at("r_t", [P, 2, NT], F32, co)
        rows = at("rows", [P, TT, DMODEL], F32, co)
        assert co[0] <= h_end + 4 * 2 * H * KV * NT
        cf = [ring_end]
        f_hi = at("f_hi", [P, KF, NT], F32R, cf)
        f_lo = at("f_lo", [P, KF, NT], F32R, cf)
        h2_hi = at("h2_hi", [P, KD, NT], F32R, cf)
        h2_lo = at("h2_lo", [P, KD, NT], F32R, cf)
        s_sb = at("s_sb", [P, NT], F32, cf)
        ff_sb = at("ff_sb", [P, NT], F32, cf)
        cx = [co[0]]
        x1_sb = at("x1_sb", [P, NT], F32, cx)
        h2_f = at("h2_f", [P, NT], F32, cx)
        assert cx[0] <= ring_end + 4 * 2 * KF * NT
        c2 = [ring_end + 4 * 2 * KF * NT]
        raw2 = at("raw2", [P, 2, FW], F32, c2)
        w2_hi = at("w2_hi", [P, 2, FW], F32R, c2)
        w2_lo = at("w2_lo", [P, 2, FW], F32R, c2)
        x2_st = at("x2_st", [P, 2, NT], F32, c2)
        r2_t = at("r2_t", [P, 2, NT], F32, c2)
        rows2 = at("rows2", [P, TT, DMODEL], F32, [top[0]])
        ln_row = at("ln_row", [P, 2, DMODEL], F32, c2)
        assert top[0] + 4 * TT * DMODEL <= ring_end

        small_in = sem("small_in")
        c_sb_in = sem("c_sb_in")
        const_in = sem("const_in")
        gw_in = sem("gw_in")
        mod_ready = sem("mod_ready")
        x_mod_c = sem("x_mod_c")
        zero_ok = sem("zero_ok")
        x_in = sem("x_in")
        dft_in = sem("dft_in")
        raw_in = [sem(f"raw_in{r}") for r in range(2)]
        mod_in = [sem(f"mod_in{r}") for r in range(8)]
        mod2_in = [sem(f"mod2_in{r}") for r in range(2)]
        c_in = sem("c_in")
        w_half = sem("w_half")
        w_split = sem("w_split")
        units_done = sem("units_done")
        mod_sum0 = sem("mod_sum0")
        mod_sum1 = sem("mod_sum1")
        prod_ok = sem("prod_ok")
        mod_sum_p = sem("mod_sum_p")
        mod_done = sem("mod_done")
        taken = [sem("taken_a"), sem("taken_b")]
        once = sem("once")
        once_v = sem("once_v")
        x_mod = sem("x_mod")
        h_hi_ok = sem("h_hi_ok")
        h_ok = sem("h_ok")
        dft_hi_ok = sem("dft_hi_ok")
        dft_ok = sem("dft_ok")
        dl_ok = sem("dl_ok")
        uf_hi_ok = sem("uf_hi_ok")
        xch_done = sem("xch_done")
        xch_hi_ok = sem("xch_hi_ok")
        xch_ok = sem("xch_ok")
        pos_done = sem("pos_done")
        ft_hi_ok = sem("ft_hi_ok")
        z_stored = sem("z_stored")
        gate_acc = sem("gate_acc")
        gate_act = sem("gate_act")
        gates_ok = sem("gates_ok")
        em_acc = sem("em_acc")
        em_ok = sem("em_ok")
        m_stored = sem("m_stored")
        dve = sem("dve")
        rh_ok = sem("rh_ok")
        r_done = sem("r_done")
        r_ok = sem("r_ok")
        qk_hi_ok = sem("qk_hi_ok")
        c_hi_ok = sem("c_hi_ok")
        c_ok = sem("c_ok")
        v_hi_ok = sem("v_hi_ok")
        v_ok = sem("v_ok")
        diag_ok = sem("diag_ok")
        e_ok = sem("e_ok")
        s_done = sem("s_done")
        s_free = sem("s_free")
        p_f_ok = sem("p_f_ok")
        p_hi_ok = sem("p_hi_ok")
        p_ok = sem("p_ok")
        den_done = sem("den_done")
        den_read = sem("den_read")
        num_done = sem("num_done")
        rec_ok = sem("rec_ok")
        hf_ok = sem("hf_ok")
        num_free = sem("num_free")
        hn_ok = sem("hn_ok")
        t_done = sem("t_done")
        yg_ok = sem("yg_ok")
        yg_stored = sem("yg_stored")
        kt_done = sem("kt_done")
        kw_hi_ok = sem("kw_hi_ok")
        kw_ok = sem("kw_ok")
        st_done = sem("st_done")
        st_stored = [sem("st_stored0"), sem("st_stored1")]
        nn_stored = sem("nn_stored")
        ygs_in = [sem(f"ygs_in{r}") for r in range(4)]
        ygs_hi_ok = sem("ygs_hi_ok")
        ygs_ok = sem("ygs_ok")
        z_in = [sem("z_in0"), sem("z_in1")]
        m_f_ok = sem("m_f_ok")
        m_hi_ok = sem("m_hi_ok")
        m_ok = sem("m_ok")
        xs_in = [sem("xs_in0"), sem("xs_in1")]
        rt_done = sem("rt_done")
        rows_ok = sem("rows_ok")
        stats_seen = sem("stats_seen")
        var_ok = sem("var_ok")
        sd_ok = sem("sd_ok")
        xn_ok = sem("xn_ok")
        xt_done = sem("xt_done")
        x1_ok = sem("x1_ok")
        x1_stored = sem("x1_stored")
        h2f_ok = sem("h2f_ok")
        h2_hi_ok = sem("h2_hi_ok")
        f_hi_ok = sem("f_hi_ok")
        f_ok = sem("f_ok")
        x1s_in = [sem("x1s_in0"), sem("x1s_in1")]
        lnr_in = sem("lnr_in")
        rt2_done = sem("rt2_done")
        rows2_ok = sem("rows2_ok")
        var2_ok = sem("var2_ok")
        sd2_ok = sem("sd2_ok")
        y_ok = sem("y_ok")
        y_stored = sem("y_stored")

        def joined(pair):
            a = 2 * pair * 512 + 512 - CUT
            return flat[:, a:a + NT]

        def grids(pair):
            a = 2 * pair * 512 + 512 - NC
            return flat[:, a:a + NT]

        def two(ap):
            return ap.rearrange("p (a b) -> p a b", a=2)

        O_PAIR = (1, 0, 0, 1)

        def den_at(u):
            return psum[:, (3, 1, 1, 1, 3)[u], 0:4]

        def wlat(tt):
            return slice(NC + P * tt, NC + P * tt + P)

        N_SMALL = 12
        block = ctx.enter_context(nc.Block())

        @block.sync
        def _(sp):
            for m in range(4):
                sp.dma_start(mod_first[:, m, :], wmod[m]).then_inc(mod_in[m], 16)
            for dst, src in ((bmod_sb[:], bmod), (gbias[:], gate_bias),
                             (m0r[:], m0_rows), (m0b[:], m0_bcast), (n0_sb[:], state_n), (gain_sb[:], gainT),
                             (ln_sb[:], lnT)):
                sp.dma_start(dst, src).then_inc(small_in, 16)
            for m in range(4, 8):
                sp.dma_start(mod_first[:, m, :], wmod[m]).then_inc(mod_in[m], 16)
            for r in range(2):
                sp.dma_start(raw[:, r, :], wunits[r]).then_inc(raw_in[r], 16)
            for m in range(8):
                sp.wait_ge(mod_sum1, m + 1)
                sp.wait_ge(prod_ok, m + 1)
                sp.dma_start(mod_first[:, m, :], wmod[8 + m]).then_inc(mod_in[m], 16)
            sp.dma_start(x_sb[:], xT).then_inc(x_in, 16)
            sp.wait_ge(mod_sum1, MOD1)
            sp.wait_ge(prod_ok, MOD1)
            for dst, src in ((dl_st, dft_l), (dc_st, dft_c), (dx_st, dft_x)):
                sp.dma_start(dst[:], src).then_inc(dft_in, 16)
            for r in range(2):
                sp.dma_start(mod_ring[:, r, :], wmod[MOD1 + r]).then_inc(mod2_in[r], 16)
            with sp.Fori(0, NG) as g:
                for r in range(2):
                    sp.wait_ge(w_split, 2 * g + r + 1)
                    sp.dma_start(raw[:, r, :], wunits[2 * g + r + 2]).then_inc(raw_in[r], 16)
                for q in range(2):
                    for r in range(2):
                        sp.wait_ge(mod_sum1, 4 * g + 2 * q + r + MOD1 + 1)
                        sp.dma_start(mod_ring[:, r, :], wmod[4 * g + 2 * q + r + MOD1 + 2]).then_inc(mod2_in[r], 16)
            with sp.Fori(0, KD - 1) as j:
                for r in range(2):
                    sp.wait_ge(w_split, 2 * j + r + U_B + 1)
                    sp.dma_start(raw[:, r, :], wunits[2 * j + r + U_B + 2]).then_inc(raw_in[r], 16)
                for r in range(2):
                    sp.wait_ge(mod_sum1, 2 * j + r + MOD1 + 4 * NG + 1)
                    sp.dma_start(mod_ring[:, r, :], wmod[2 * j + r + MOD1 + 4 * NG + 2]).then_inc(mod2_in[r], 16)
            for r in range(2):
                sp.wait_ge(w_split, U_HEAD + r - 1)
                sp.dma_start(raw[:, r, :], wunits[U_HEAD + r]).then_inc(raw_in[r], 16)
            with sp.Fori(0, H) as h:
                for r in range(HU):
                    if r == 2:
                        sp.wait_ge(c_ok, h + 1)
                        sp.wait_ge(em_ok, 2)
                        sp.wait_ge(m_stored, 32)
                        sp.wait_ge(z_stored, 16 * (KD + 1))
                        sp.dma_start(c_raw[:], stateC[h]).then_inc(c_in, 16)
                    sp.wait_ge(w_split, U_HEAD + HU * h + r + 1)
                    sp.dma_start(raw[:, r % 2, :], wunits[U_HEAD + HU * h + r + 2]).then_inc(raw_in[r % 2], 16)
            for r in range(2):
                sp.wait_ge(w_split, U_GA + r + 1)
                sp.dma_start(raw[:, r, :], wunits[U_GA + r + 2]).then_inc(raw_in[r], 16)
            sp.wait_ge(yg_stored, 16 * (H * TT + 1))
            for r in range(2):
                sp.wait_ge(st_stored[r], 16 * (2 * H + 1))
            sp.wait_ge(nn_stored, 16 * (H + 1))
            yg_tiles = yg_dram.rearrange("h v p t -> (h v) p t")
            with sp.Fori(0, H * KV // 8) as i:
                for q in range(2):
                    for r in range(4):
                        sp.wait_ge(ygs_ok, 8 * i + 4 * q + r + 1)
                        sp.dma_start(yg_st[:, r, :], yg_tiles[8 * i + 4 * q + r]).then_inc(ygs_in[r], 16)
                    sp.wait_ge(w_split, U_GA + 2 * i + q + 3)
                    sp.dma_start(raw[:, q, :], wunits[U_GA + 2 * i + q + 4]).then_inc(raw_in[q], 16)
            for r in range(2):
                sp.wait_ge(w_split, U_MIX + r - 1)
                sp.dma_start(raw[:, r, :], wunits[U_MIX + r]).then_inc(raw_in[r], 16)
            with sp.Fori(0, KD // 2) as i:
                for r in range(2):
                    sp.wait_ge(m_ok, 2 * i + r + 1)
                    sp.dma_start(z_st[:, r, :], z_dram[2 * i + r]).then_inc(z_in[r], 16)
                    for q in range(2):
                        sp.wait_ge(w_split, U_MIX + 4 * i + 2 * r + q + 1)
                        sp.dma_start(raw[:, q, :], wunits[U_MIX + 2 + 4 * i + 2 * r + q]).then_inc(raw_in[q], 16)
            sp.wait_ge(units_done, U_OUT)
            with sp.Fori(0, KD // 2) as i:
                for r in range(2):
                    sp.wait_ge(taken[r], A_OUT + i + 1)
                    sp.dma_start(x_st[:, r, :], xT[:, 2 * i + r, :]).then_inc(xs_in[r], 16)
                for r in range(2):
                    sp.wait_ge(w_split, U_OUT + 2 * i + r + 1)
                    sp.dma_start(raw[:, r, :], wunits[U_OUT + 2 + 2 * i + r]).then_inc(raw_in[r], 16)
            with sp.Fori(1, KF) as i:
                for r in range(2):
                    sp.wait_ge(w_split, U_FF1 + 2 * i + r - 1)
                    sp.dma_start(raw[:, r, :], wunits[U_FF1 + 2 * i + r]).then_inc(raw_in[r], 16)
            sp.wait_ge(units_done, U_FF2)
            for r in range(2):
                sp.dma_start(raw2[:, r, :], wffo[r]).then_inc(raw_in[r], 16)
            sp.wait_ge(f_ok, KF + 1)
            sp.dma_start(ln_row[:], ln_rows).then_inc(lnr_in, 16)
            sp.wait_ge(x1_stored, 16 * (KD + 1))
            for r in range(2):
                sp.dma_start(x2_st[:, r, :], x1_dram[r]).then_inc(x1s_in[r], 16)
            with sp.Fori(0, KD // 2 - 1) as i:
                for r in range(2):
                    for q in range(2):
                        sp.wait_ge(w_split, U_FF2 + 4 * i + 2 * r + q + 1)
                        sp.dma_start(raw2[:, q, :], wffo[4 * i + 2 * r + q + 2]).then_inc(raw_in[q], 16)
                for r in range(2):
                    sp.wait_ge(taken[r], A_FF2 + i + 2)
                    sp.dma_start(x2_st[:, r, :], x1_dram[2 * i + r + 2]).then_inc(x1s_in[r], 16)
            for q in range(2):
                sp.wait_ge(w_split, U_END - 4 + q + 1)
                sp.dma_start(raw2[:, q, :], wffo[2 * KD - 2 + q]).then_inc(raw_in[q], 16)
            for tt in range(TT):
                sp.wait_ge(y_ok, tt + 1)
                dst = y_prompt if tt == 0 else y_sample[(tt - 1) * P:tt * P, :]
                sp.dma_start(dst, rows2[:, tt, :]).then_inc(y_stored, 16)
            sp.wait_ge(y_stored, 16 * TT)
            sp.wait_ge(m_stored, 32)

        @block.gpsimd
        def _(pool):
            def split(u, slot, first, combine=False, ring=(raw, w_hi, w_lo), n_in=None):
                src, hi, lo = (t[:, slot, :] for t in ring)
                pool.wait_ge(raw_in[slot], n_in)
                if not first:
                    pool.wait_ge(units_done, u - 1)
                if combine:
                    half = UW // 2
                    pool.tensor_tensor(wb_sum[:, 0:half], src[:, 0:half], src[:, half:UW], ALU.add)
                    pool.tensor_tensor(wb_sum[:, half:UW], src[:, half:UW], src[:, 0:half], ALU.subtract)\
                        .then_inc(w_half, 1)
                return src, hi, lo

            def rounded(src, hi):
                pool.tensor_tensor(hi, src, zero[:, 0:1].broadcast_to([P, src.shape[1]]), ALU.add)\
                    .then_inc(w_half, 1)

            def rest(src, hi, lo):
                pool.tensor_tensor(lo, src, hi.bitcast(F32), ALU.subtract).then_inc(w_split, 1)

            pool.memset(zero[:], 0.0).then_inc(zero_ok, 1)
            pool.wait_ge(zero_ok, 1)
            for u in range(2):
                for k in range(1, KD):
                    acc = (mod_sum, sum_first)[u][:, 0, UW // 2:]
                    pool.wait_ge(prod_ok, KD * u + k + 1)
                    if u or k > 1:
                        pool.wait_ge(mod_sum_p, (KD - 1) * u + k - 1)
                    pool.tensor_tensor(acc, acc, prod[:, k % 4, :], ALU.add).then_inc(mod_sum_p, 1)
                src, hi, lo = split(u, u, True, n_in=16)
                rounded(src, hi)
                pool.wait_ge(w_half, u + 1)
                rest(src, hi, lo)
            def units_f(i):
                for r in range(2):
                    src, hi, lo = split(2 * i + r, r, False, n_in=16 * i + 16)
                    rounded(src, hi)
                    pool.wait_ge(w_half, 2 * i + r + 1)
                    rest(src, hi, lo)

            units_f(1)
            pool.wait_ge(dft_hi_ok, 3)
            pool.tensor_tensor(dl_lo[:].rearrange("p a b c -> p (a b c)"), dl_st[:],
                               dl_hi[:].rearrange("p a b c -> p (a b c)").bitcast(F32), ALU.subtract)\
                .then_inc(dl_ok, 1)
            pool.wait_ge(gate_act, 1)
            pool.tensor_tensor(gw_lo[:], gate_w[:], gw_hi[:].bitcast(F32), ALU.subtract).then_inc(gates_ok, 1)
            with pool.Fori(2, NG) as i:
                units_f(i)
            pool.wait_ge(gates_ok, 1)
            with pool.Fori(0, KD) as j:
                src, hi, lo = split(U_B + 2 * j, 0, False, n_in=16 * j + 16 * (NG + 1))
                rounded(src, hi)
                pool.wait_ge(w_half, U_B + 3 * j + 1)
                rest(src, hi, lo)
                src, hi, lo = split(U_B + 2 * j + 1, 1, False, True, n_in=16 * j + 16 * (NG + 1))
                pool.wait_ge(w_half, U_B + 3 * j + 2)
                rounded(wb_sum[:], hi)
                pool.wait_ge(w_half, U_B + 3 * j + 3)
                rest(wb_sum[:], hi, lo)
            half0 = U_HEAD + KD
            with pool.Fori(0, (U_FF2 - U_HEAD) // 2) as i:
                for r in range(2):
                    src, hi, lo = split(U_HEAD + 2 * i + r, r, False, n_in=16 * i + 16 * (U_HEAD // 2 + 1))
                    rounded(src, hi)
                    pool.wait_ge(w_half, half0 + 2 * i + r + 1)
                    rest(src, hi, lo)
            half1 = half0 + U_FF2 - U_HEAD
            with pool.Fori(0, KD) as i:
                for r in range(2):
                    src, hi, lo = split(U_FF2 + 2 * i + r, r, False, ring=(raw2, w2_hi, w2_lo),
                                        n_in=16 * i + 16 * (U_FF2 // 2 + 1))
                    if r == 0:
                        pool.wait_ge(units_done, U_FF2)
                    rounded(src, hi)
                    pool.wait_ge(w_half, half1 + 2 * i + r + 1)
                    rest(src, hi, lo)

        @block.tensor
        def _(pe):
            mm = pe.matmul

            def unit_cols(out, u, slot, act_hi, act_lo, k0=0, last=True, first=True, nb=UB,
                          ring=(w_hi, w_lo), k_ready=None):
                pe.wait_ge(w_split, u + 1)
                for b in range(nb):
                    if k_ready is not None:
                        pe.wait_ge(k_ready, b + 1)
                    cols = slice(b * P, (b + 1) * P)
                    terms = ((ring[0], act_hi), (ring[0], act_lo), (ring[1], act_hi))
                    for n, (w, x) in enumerate(terms):
                        for a, z in ((0, CUT), (CUT, NT)):
                            ins = mm(out[:, a:z], w[:, slot, cols], x[:, k0 + b, a:z],
                                     start=(first and b == 0 and n == 0),
                                     stop=(last and b == nb - 1 and n == 2))
                ins.then_inc(units_done, 1)

            def mod_chunk(c, acc):
                pe.wait_ge(mod_sum1, KD * c + KD)
                for m in range(KD):
                    for g in range(2):
                        ins = mm(psum[:, 7, bass.ds(2 * KD * c + (2 * m + g), 1)], acc[:, g, m * P:(m + 1) * P],
                                 ones_r[:, 0:1].bitcast(F32), start=True, stop=True)
                ins.then_inc(mod_done, 1)

            for p in range(2):
                pe.sem_inc(taken[p], 1)
            pe.wait_ge(once, 2)
            for c in range(2):
                pe.wait_ge(mod_sum_p, (KD - 1) * (c + 1))
                mod_chunk(c, (mod_sum, sum_first)[c])

            def group(g, odd):
                for p in range(2):
                    pe.wait_ge(taken[p], A_F + 2 * g + 1)
                    unit_cols(joined(p), U_PASS1 + 2 * g + p, p, h_hi, h_lo, k_ready=h_ok if p == 0 else None)
                pe.wait_ge(dft_ok, 2)
                for p in range(2):
                    if p == 1 and odd is not None:
                        mod_chunk(odd, mod_sum)
                    pe.wait_ge(taken[p], A_F + 2 * g + 2)
                for tt in range(TT):
                    if tt >= 3:
                        pe.wait_ge(xch_ok, 5 * g + tt - 2)
                    n = 0
                    for k in range(2):
                        for u, d in ((uf_hi, dx_hi), (uf_lo, dx_hi), (uf_hi, dx_lo)):
                            ins = mm(psum[:, 4 + tt % 3, 0:XW], u[:, k, tt * P:(tt + 1) * P], d[:, k, :],
                                     start=(n == 0), stop=(n == 5))
                            n += 1
                    ins.then_inc(xch_done, 1)
                pe.wait_ge(xch_ok, 5 * g + 5)
                pe.wait_ge(dl_ok, 1)
                for kind in range(2):
                    out = grids(kind)
                    cols = slice(kind * P, kind * P + P)
                    for span, tiles, dh, dl in ((slice(0, NC), range(1), dc_hi, dc_lo),
                                                (slice(NC, NT), range(1, TT), dl_hi, dl_lo)):
                        for t in tiles:
                            pos = (lambda d, c: d[:, c, :]) if t == 0 else (lambda d, c, t=t: d[:, c, t - 1, :])
                            jobs = [(x_hi, cols, pos(dh, kind)), (x_lo, cols, pos(dh, kind)),
                                    (x_hi, cols, pos(dl, kind))]
                            if kind == 1:
                                nyq = slice(2 * P, 2 * P + 2)
                                jobs += [(x_hi, nyq, pos(dh, 0)), (x_lo, nyq, pos(dh, 0)), (x_hi, nyq, pos(dl, 0))]
                            for n, (x, cc, d) in enumerate(jobs):
                                m = cc.stop - cc.start
                                ins = mm(out[0:m, span], x[:, t, cc], d,
                                         start=(t == tiles[0] and n == 0),
                                         stop=(t == tiles[-1] and n == len(jobs) - 1), skip_group_check=True)
                    ins.then_inc(pos_done, 1)

            with pe.Fori(0, NG // 2) as gg:
                group(2 * gg, None)
                group(2 * gg + 1, gg + 2)

            pe.wait_ge(gates_ok, 1)
            for k in range(KD):
                for n, (w, x) in enumerate(((gw_hi, h_hi), (gw_hi, h_lo), (gw_lo, h_hi))):
                    for half in range(2):
                        ins = mm(psum[:, 5 + half, 0:NT // 2], w[:, k * P:(k + 1) * P],
                                 x[:, k, half * NT // 2:(half + 1) * NT // 2],
                                 start=(k == 0 and n == 0), stop=(k == KD - 1 and n == 2))
            ins.then_inc(gate_acc, 1)

            with pe.Fori(0, 2) as jj:
                for jr in range(KD // 2):
                    j = jj * (KD // 2) + jr
                    pe.wait_ge(taken[0], A_B + j + 1)
                    unit_cols(joined(0), U_B + 2 * j, 0, h_hi, h_lo)
                    pe.wait_ge(taken[1], A_B + j + 1)
                    unit_cols(joined(1), U_B + 2 * j + 1, 1, ft_hi, ft_lo)
                mod_chunk(jj + 4, mod_sum)

            pe.wait_ge(gates_ok, 2)
            for tt in range(TT):
                ins = pe.transpose(flat[:, 5 * 512 + tt * P:5 * 512 + (tt + 1) * P],
                                   em_rows[:, tt * P:(tt + 1) * P], ident)
            ins.then_inc(em_acc, 1)

            def turn(h, u):
                pe.wait_ge(hn_ok, 5 * h + u + 1)
                if u >= 1:
                    pe.wait_ge(yg_ok, 5 * h + u + 1)
                for v in range(KV):
                    ins = pe.transpose(psum[:, 7, v * P:(v + 1) * P], hn_sb[:, v * P:(v + 1) * P], ident)
                ins.then_inc(t_done, 1)

            def final_states(h, A):
                pe.wait_ge(kw_ok, h + 1)
                for v in range(KV + 1):
                    p, tile = v % 2, 1 + v // 2
                    pe.wait_ge(taken[p], A + tile + 1)
                    if v < KV:
                        cc = slice(v * P, (v + 1) * P)
                        jobs = [(v_hi[:, 0, cc], kw_hi), (v_lo[:, 0, cc], kw_hi), (v_hi[:, 0, cc], kw_lo)]
                    else:
                        jobs = [(ones_r[:, :], kw_hi), (ones_r[:, :], kw_lo)]
                    for n, (a, b) in enumerate(jobs):
                        ins = mm(psum[:, 2 * p, :], a, b[:, :, :].rearrange("p a b -> p (a b)"),
                                 start=(n == 0), stop=(n == len(jobs) - 1))
                    ins.then_inc(st_done, 1)

            def head(h, tail):
                U = U_HEAD + HU * h
                A = A_HEAD + HA * h

                def project(pair, tile, unit, slot):
                    pe.wait_ge(taken[pair], A + tile + 1)
                    unit_cols(joined(pair), U + unit, slot, h_hi, h_lo)

                def scores(u):
                    if u == 0:
                        pe.wait_ge(v_ok, 5 * h + 2)
                    else:
                        pe.wait_ge(s_free, 5 * h + u)
                    srcs = range(LT) if u < LT else range(1)
                    tq = wlat(u) if u < LT else slice(0, NC)
                    for s in srcs:
                        sk = wlat(s) if u < LT else slice(0, NC)
                        n = 0
                        for d in range(KQ):
                            for a, b in ((k_hi, q_hi), (k_hi, q_lo), (k_lo, q_hi)):
                                ins = mm(psum[:, 4, s * P:(s + 1) * P], a[:, d, sk], b[:, d, tq],
                                         start=(n == 0), stop=(n == 3 * KQ - 1))
                                n += 1
                    ins.then_inc(s_done, 1)

                def numer(u):
                    buf = u % 2
                    if u == 0:
                        pe.wait_ge(v_ok, 5 * h + 5)
                        pe.wait_ge(c_ok, h + 2)
                    else:
                        pe.wait_ge(num_free, 5 * h + u)
                    if u < 2:
                        pe.wait_ge(taken[1 - u], A + 6 + 2 * u)
                    pe.wait_ge(p_ok, 5 * h + u + 1)
                    blocks = [list(range(u + 1)), list(range(u, LT))] if u < LT else [[0], [0]]
                    starts = [0, u + 1] if u < LT else [0, 1]
                    for part in range(2):
                        for d in range(2):
                            jobs = []
                            for n, s in enumerate(blocks[d]):
                                pos = starts[d] + n
                                hi, lo = p_hi[:, buf, pos, :], p_lo[:, buf, pos, :]
                                if part == 0:
                                    jobs += [(hi, ones_r[:, 0:2]), (lo, ones_r[:, 0:2])]
                                else:
                                    vt = s + 1 if u < LT else 0
                                    jobs += [(hi, v_hi[:, vt, :]), (lo, v_hi[:, vt, :]), (hi, v_lo[:, vt, :])]
                            if u < LT:
                                for k in range(KQ):
                                    hi, lo = qi_hi[:, buf, d, k, :], qi_lo[:, buf, d, k, :]
                                    a, b = ((n0_hi[:, h, d, k, :], n0_lo[:, h, d, k, :]) if part == 0
                                            else (c_hi[:, d, k, :], c_lo[:, d, k, :]))
                                    jobs += [(hi, a), (lo, a), (hi, b)]
                            out = den_at(u)[:, 2 * d:2 * d + 2] if part == 0 else psum[:, 5 + d, :]
                            for n, (a, b) in enumerate(jobs):
                                ins = mm(out, a, b, start=(n == 0), stop=(n == len(jobs) - 1))
                        ins.then_inc(num_done if part else den_done, 1)

                project(0, 0, 0, 0)
                if tail:
                    turn(h - 1, 3)
                    pe.wait_ge(den_read, 5 * h)
                project(1, 0, 1, 1)
                if tail:
                    turn(h - 1, 4)
                    final_states(h - 1, A)
                else:
                    for p in range(2):
                        pe.wait_ge(taken[p], A + 2)
                        pe.sem_inc(taken[p], 3 - p)
                project(0, 4, 2, 0)
                pe.wait_ge(rh_ok, h + 1)
                pe.wait_ge(em_ok, 1)
                pe.wait_ge(yg_ok, 5 * h + 1)
                for d, s in enumerate((sel_f, sel_b)):
                    dst = joined(2 + d)
                    mm(dst[:, 0:CUT], s[0:64, :], r_head[0:64, 0:CUT], start=True, stop=True)
                    mm(dst[:, CUT:NT], s[0:64, :], r_head[0:64, CUT:NT], start=True, stop=True).then_inc(r_done, 1)
                project(1, 3, 3, 1)
                pe.wait_ge(taken[0], A + 6)
                pe.wait_ge(r_ok, 2 * h + 2)
                v_banks = [0, 4, 5, 6, 7]
                for q in range(4):
                    pe.wait_ge(w_split, U + 4 + q + 1)
                    for kk in range(2):
                        k = 2 * q + kk
                        cols = slice(kk * DV, (kk + 1) * DV)
                        for tt in range(TT):
                            for n, (x, w) in enumerate(((h_hi, w_hi), (h_lo, w_hi), (h_hi, w_lo))):
                                ins = mm(psum[:, v_banks[tt], :], x[:, k, tt * P:(tt + 1) * P],
                                         w[:, q % 2, cols], start=(k == 0 and n == 0),
                                         stop=(k == KD - 1 and n == 2))
                    ins.then_inc(units_done, 1)
                project(1, 4, 8, 0)
                scores(0)
                pe.wait_ge(v_ok, 5 * h + 1)
                project(0, 5, 9, 1)
                scores(1)
                numer(0)
                project(0, 6, 10, 0)
                scores(2)
                numer(1)
                turn(h, 0)
                project(1, 5, 11, 1)
                pe.wait_ge(taken[1], A + 7)
                for k in range(KQ):
                    ins = pe.transpose(psum[:, 2, k * P:(k + 1) * P], k_c[:, k, :], ident)
                ins.then_inc(kt_done, 1)
                scores(3)
                numer(2)
                scores(4)
                turn(h, 1)
                numer(3)
                turn(h, 2)
                numer(4)

            head(0, False)
            with pe.Fori(1, H) as h:
                head(h, True)

            pe.wait_ge(taken[0], A_GA + 1)
            unit_cols(joined(0), U_GA, 0, h_hi, h_lo)
            turn(H - 1, 3)
            pe.wait_ge(den_read, 5 * H)
            pe.wait_ge(taken[1], A_GA + 1)
            unit_cols(joined(1), U_GA + 1, 1, h_hi, h_lo)
            turn(H - 1, 4)
            final_states(H - 1, A_GA)
            with pe.Fori(1, KD // 2) as i:
                for p in range(2):
                    pe.wait_ge(taken[p], A_GA + i + (4 - p))
                    unit_cols(joined(p), U_GA + 2 * i + p, p, h_hi, h_lo)
            pe.wait_ge(taken[1], A_MIX)
            pe.sem_inc(taken[1], 1)

            with pe.Fori(0, KD // 2) as i:
                for p in range(2):
                    pe.wait_ge(taken[p], A_MIX + i + 1)
                    for q in range(2):
                        u = U_MIX + 4 * i + 2 * p + q
                        pe.wait_ge(ygs_ok, 4 + 8 * q + 8)
                        unit_cols(joined(p), u, q, yg_hi, yg_lo, k0=8 * q, first=(q == 0), last=(q == 1))

            with pe.Fori(0, KD // 2) as i:
                for p in range(2):
                    pe.wait_ge(taken[p], A_OUT + i + 1)
                    if p == 0:
                        pe.wait_ge(m_ok, 2 + KD)
                    unit_cols(joined(p), U_OUT + 2 * i + p, p, mg_hi, mg_lo)
                for p in range(2):
                    pe.wait_ge(taken[p], A_OUT + i + 2)
                    pe.wait_ge(rows_ok, 2 * i + p + 1)
                    for tt in range(TT):
                        a = (4 + 2 * p) * 512 + tt * P
                        ins = pe.transpose(flat[:, a:a + P], r_t[:, p, tt * P:(tt + 1) * P], ident)
                    ins.then_inc(rt_done, 1)
            pe.wait_ge(xn_ok, TT)
            for j in range(KD):
                p = j % 2
                pe.wait_ge(taken[p], A_XT + j // 2 + 1)
                for tt in range(TT):
                    ins = pe.transpose(joined(p)[:, tt * P:(tt + 1) * P], rows[:, tt, j * P:(j + 1) * P], ident)
                ins.then_inc(xt_done, 1)

            pe.wait_ge(taken[1], A_FF1 + 1)
            with pe.Fori(0, KF) as i:
                for p in range(2):
                    pe.wait_ge(taken[p], A_FF1 + i + 1)
                    unit_cols(joined(p), U_FF1 + 2 * i + p, p, h2_hi, h2_lo)
            pe.wait_ge(f_ok, KF + 1)
            with pe.Fori(0, KD // 2) as i:
                for p in range(2):
                    pe.wait_ge(taken[p], A_FF2 + i + 1)
                    for q in range(2):
                        unit_cols(joined(p), U_FF2 + 4 * i + 2 * p + q, q, f_hi, f_lo, k0=FB * q, nb=FB,
                                  first=(q == 0), last=(q == 1), ring=(w2_hi, w2_lo))
                for p in range(2):
                    pe.wait_ge(taken[p], A_FF2 + i + 2)
                    pe.wait_ge(rows2_ok, 2 * i + p + 1)
                    for tt in range(TT):
                        a = (4 + 2 * p) * 512 + tt * P
                        ins = pe.transpose(flat[:, a:a + P], r2_t[:, p, tt * P:(tt + 1) * P], ident)
                    ins.then_inc(rt2_done, 1)

        @block.scalar
        def _(act):
            A_ = act.activation
            act.sem_inc(z_stored, 16)
            for r in range(2):
                act.sem_inc(st_stored[r], 16)
                act.sem_inc(rows_ok, 1)
                act.sem_inc(rows2_ok, 1)
            act.sem_inc(nn_stored, 16)
            act.sem_inc(yg_stored, 16)
            act.sem_inc(x1_stored, 16)
            act.dma_start(c_sb[:], cT).then_inc(c_sb_in, 16)
            act.dma_start(const_sb[:], consts).then_inc(const_in, 16)
            act.wait_ge(c_sb_in, 16)
            A_(c_silu[:], c_sb[:], ACT.Silu).then_inc(once, 1)
            act.wait_ge(once, 1)
            for n in range(MOD1):
                if n == 2:
                    act.wait_ge(const_in, 16)
                    A_(ones_r[:], ident, ACT.Identity, bias=1.0, scale=0.0).then_inc(once, 1)
                c, k = divmod(n, KD)
                act.wait_ge(mod_in[k], 16 * (c + 1))
                if n > 4 and (n - 4) % KD:
                    act.wait_ge(mod_sum_p, (KD - 1) * ((n - 4) // KD) + (n - 4) % KD)
                dst = (mod_sum, sum_first)[c][:, 0, UW // 2:] if k == 0 else prod[:, k % 4, :]
                A_(dst, mod_first[:, k, UW // 2:], ACT.Copy, scale=c_silu[:, k, 0:1]).then_inc(prod_ok, 1)
            act.dma_start(gate_w[:], wgate).then_inc(gw_in, 16)
            act.wait_ge(small_in, 16 * 7)
            A_(n0_hi[:], n0_sb[:], ACT.Copy).then_inc(once, 1)
            act.wait_ge(mod_ready, 1)
            act.wait_ge(x_in, 16)
            for k in range(KD):
                A_(x_sb[:, k, 0:NC], x_sb[:, k, 0:NC], ACT.Identity, scale=mod_sb[:, KD + k, 0:1],
                   bias=mod_sb[:, k, 0:1]).then_inc(x_mod_c, 1)
                act.wait_ge(x_mod_c, k + 1)
                act.wait_ge(x_mod, k + 1)
                A_(h_hi[:, k, :], x_sb[:, k, :], ACT.Copy).then_inc(h_hi_ok, 1)
            act.wait_ge(dft_in, 48)
            for hi, st in ((dx_hi[:].rearrange("p a b -> p (a b)"), dx_st),
                           (dc_hi[:].rearrange("p a b -> p (a b)"), dc_st),
                           (dl_hi[:].rearrange("p a b c -> p (a b c)"), dl_st)):
                A_(hi, st[:], ACT.Copy).then_inc(dft_hi_ok, 1)
            act.wait_ge(gw_in, 16)
            A_(gw_hi[:], gate_w[:], ACT.Copy).then_inc(gate_act, 1)

            with act.Fori(0, NG) as g:
                for p in range(2):
                    act.wait_ge(units_done, U_PASS1 + 2 * g + p + 1)
                    A_(uf_hi[:, p, :], joined(p), ACT.Copy).then_inc(uf_hi_ok, 1)
                for tt in range(TT):
                    act.wait_ge(xch_done, 5 * g + tt + 1)
                    A_(x_hi[:, tt, :], psum[:, 4 + tt % 3, 0:XW], ACT.Copy).then_inc(xch_hi_ok, 1)
                for kind in range(2):
                    act.wait_ge(pos_done, 2 * g + kind + 1)
                    A_(ft_hi[:, NG * kind + g, :], grids(kind), ACT.Copy).then_inc(ft_hi_ok, 1)

            act.wait_ge(gate_acc, 1)
            A_(two(gt[:]), psum[:, 5:7, 0:NT // 2], ACT.Identity, bias=gbias[:, 0:1]).then_inc(gate_act, 1)
            act.wait_ge(gate_act, 2)
            A_(gt_e[:], gt[:], ACT.Abs).then_inc(gate_act, 1)
            act.wait_ge(gate_act, 3)
            A_(gt_e[:], gt_e[:], ACT.Exp, scale=-1.0).then_inc(gate_act, 1)
            act.wait_ge(gate_act, 4)
            A_(gt_e[:], gt_e[:], ACT.Ln, bias=1.0).then_inc(gate_act, 1)
            with act.Fori(0, KD) as j:
                act.wait_ge(units_done, U_B + 2 * j + 1)
                A_(gb_sb[:], joined(0), ACT.Sigmoid).then_inc(taken[0], 1)
                act.wait_ge(taken[1], A_B + j + 2)
                act.dma_start(z_dram[j], z_sb[:]).then_inc(z_stored, 16)
            act.wait_ge(gates_ok, 2)
            act.dma_start(new_m[0], em_rows[64:64 + H, NC - 1:NC]).then_inc(m_stored, 16)
            act.dma_start(new_m[1], em_rows[96:96 + H, 0:1]).then_inc(m_stored, 16)
            act.wait_ge(em_acc, 1)
            em_flat = em_t[:].rearrange("p t g c -> p (t g c)")
            A_(em_flat, flat[:, 5 * 512:5 * 512 + NT], ACT.Copy).then_inc(em_ok, 1)
            act.wait_ge(em_ok, 1)
            A_(enm_t[:], em_t[:, :, 2:4, :], ACT.Exp, scale=-1.0).then_inc(em_ok, 1)

            act.wait_ge(m_stored, 32)
            act.wait_ge(z_stored, 16 * (KD + 1))
            def turned(h, u):
                tok = wlat(u) if u < LT else slice(0, NC)
                act.wait_ge(yg_ok, 5 * h + u + 2)
                act.dma_start(yg_dram[h, :, :, tok].rearrange("v p t -> p v t"), yg_sb[:]).then_inc(yg_stored, 16)

            def forward(h, u):
                act.wait_ge(rec_ok, 5 * h + u + 1)
                act.wait_ge(num_done, 5 * h + u + 1)
                A_(h_sb[:], psum[:, 5, :], ACT.Copy, scale=rec[:, 0:1]).then_inc(hf_ok, 1)

            def final_states(h, A):
                for v in range(KV + 1):
                    p, tile = v % 2, 1 + v // 2
                    if v < KV:
                        if p == 0:
                            act.wait_ge(st_done, 5 * h + v + 1)
                            act.wait_ge(st_stored[p], 32 * h + 16 * (v // 2) + 16)
                            A_(st_sb[:, p, :], psum[:, 2 * p, :], ACT.Copy).then_inc(taken[p], 1)
                        act.wait_ge(taken[p], A + tile + 2)
                        act.dma_start(new_C[:, h, v * P:(v + 1) * P, :].rearrange("a p d -> p a d"),
                                      st_sb[:, p, :].rearrange("p (a d) -> p a d", a=2)).then_inc(st_stored[p], 16)
                    else:
                        act.wait_ge(st_done, 5 * h + v + 1)
                        act.wait_ge(nn_stored, 16 * h + 16)
                        A_(nn_sb[:], psum[0:1, 2 * p, :], ACT.Copy).then_inc(taken[p], 1)
                        act.wait_ge(taken[p], A + tile + 2)
                        act.dma_start(new_n[:, h, :].unsqueeze(0),
                                      nn_sb[:, :].rearrange("p (a d) -> p a d", a=2)).then_inc(nn_stored, 16)

            def head(h, tail):
                U = U_HEAD + HU * h
                A = A_HEAD + HA * h

                def gate(v):
                    pair = O_PAIR[v]
                    act.wait_ge(units_done, U + 8 + v + 1)
                    A_(og[:, v, :], joined(pair), ACT.Tanh, scale=0.5).then_inc(taken[pair], 1)

                def weights(u):
                    act.wait_ge(diag_ok, 5 * h + u + 1)
                    w, inter = w_sb[:, u % 2], i_sb[:, u % 2]
                    if u == LT:
                        A_(w[:, 0:2, :], w[:, 0:2, :], ACT.Exp).then_inc(e_ok, 1)
                        return
                    A_(w[:, u:u + 2, :], w[:, u:u + 2, :], ACT.Exp)
                    for s in range(u):
                        A_(w[:, s, :], r_sb[:, 0, wlat(u)], ACT.Exp, bias=em_t[:, 1 + s, 0, bass.ds(h, 1)])
                    for s in range(u + 1, LT):
                        A_(w[:, s + 1, :], r_sb[:, 1, wlat(u)], ACT.Exp, bias=em_t[:, 1 + s, 1, bass.ds(h, 1)])
                    for d in range(2):
                        ins = A_(inter[:, d, :], r_sb[:, d, wlat(u)], ACT.Exp, bias=m0b[:, d, bass.ds(h, 1)])
                    ins.then_inc(e_ok, 1)

                def p_round(u):
                    act.wait_ge(p_f_ok, 5 * h + u + 1)
                    if u >= 2:
                        act.wait_ge(num_done, 5 * h + u - 1)
                    if u < LT:
                        A_(p_hi[:, u % 2, :, :], w_sb[:, u % 2, :, :], ACT.Copy)
                        A_(qi_hi[:, u % 2, :, :, :], qi_f[:], ACT.Copy).then_inc(p_hi_ok, 1)
                    else:
                        A_(p_hi[:, u % 2, 0:2, :], w_sb[:, u % 2, 0:2, :], ACT.Copy).then_inc(p_hi_ok, 1)

                def qk(n, dst, scale):
                    act.wait_ge(units_done, U + n + 1)
                    A_(dst[:, n % 2, :], joined(n % 2), ACT.Copy, scale=scale).then_inc(qk_hi_ok, 1)

                if tail:
                    forward(h - 1, 4)
                qk(0, q_hi, 1.0)
                if tail:
                    turned(h - 1, 3)
                qk(1, q_hi, 1.0)
                if tail:
                    final_states(h - 1, A)
                    turned(h - 1, 4)
                qk(2, k_hi, QSCALE)
                for d in range(2):
                    act.wait_ge(r_done, 2 * h + d + 1)
                    A_(r_sb[:, d, :], joined(2 + d), ACT.Copy).then_inc(r_ok, 1)
                weights(0)
                weights(1)
                qk(3, k_hi, QSCALE)
                act.wait_ge(c_in, 16 * h + 16)
                A_(c_hi[:], c_raw[:], ACT.Copy).then_inc(c_hi_ok, 1)
                act.wait_ge(units_done, U + 8)
                for tt in range(TT):
                    A_(v_hi[:, tt, :], psum[:, (0, 4, 5, 6, 7)[tt], :], ACT.Copy).then_inc(v_hi_ok, 1)
                gate(0)
                p_round(0)
                gate(1)
                weights(2)
                p_round(1)
                forward(h, 0)
                weights(3)
                gate(2)
                p_round(2)
                forward(h, 1)
                weights(4)
                gate(3)
                turned(h, 0)
                p_round(3)
                forward(h, 2)
                turned(h, 1)
                p_round(4)
                act.wait_ge(taken[1], A + 8)
                A_(kw_hi[:], kw_f[:], ACT.Copy).then_inc(kw_hi_ok, 1)
                forward(h, 3)
                turned(h, 2)

            head(0, False)
            with act.Fori(1, H) as h:
                head(h, True)

            def gate_a(j, pair):
                act.wait_ge(units_done, j + (U_GA + 1))
                A_(ga_sb[:, j, :], joined(pair), ACT.Sigmoid).then_inc(taken[pair], 1)

            forward(H - 1, 4)
            gate_a(0, 0)
            turned(H - 1, 3)
            gate_a(1, 1)
            final_states(H - 1, A_GA)
            turned(H - 1, 4)
            with act.Fori(0, H * KV // 8) as i:
                for p in range(2):
                    gate_a(2 * i + 2 + p, p)
                    for r in range(4):
                        t = 8 * i + (4 * p + r)
                        act.wait_ge(ygs_in[r], 32 * i + 16 * (p + 1))
                        A_(yg_hi[:, t, :], yg_st[:, r, :], ACT.Copy,
                           scale=gain_h[:, bass.ds(t, 1)]).then_inc(ygs_hi_ok, 1)
            for p in range(2):
                gate_a(KD - 2 + p, p)
            with act.Fori(0, KD) as j:
                act.wait_ge(m_f_ok, j + 1)
                A_(mg_hi[:, j, :], m_sb[:], ACT.Copy).then_inc(m_hi_ok, 1)
            with act.Fori(0, KD // 2) as i:
                for p in range(2):
                    act.wait_ge(rt_done, 2 * i + p + 1)
                    dst = rows[:, :, :].rearrange("p t (j c) -> p t j c", c=P)[:, :, 2 * i + p, :]
                    a = (4 + 2 * p) * 512
                    A_(dst, flat[:, a:a + NT].rearrange("p (t c) -> p t c", c=P), ACT.Copy).then_inc(rows_ok, 1)
            act.wait_ge(var_ok, 1)
            A_(sd[:], sd[:], ACT.Sqrt).then_inc(sd_ok, 1)
            with act.Fori(0, KD // 2) as i:
                for p in range(2):
                    j = 2 * i + p
                    act.wait_ge(xt_done, j + 1)
                    src = joined(p)
                    A_(h2_f[:, 0:NC], src[:, 0:NC], ACT.Identity, scale=h2_s[:, j, 0:1], bias=h2_b[:, j, 0:1])
                    A_(h2_f[:, NC:NT], src[:, NC:NT], ACT.Identity, scale=h2_s[:, j, 1:2],
                       bias=h2_b[:, j, 1:2]).then_inc(h2f_ok, 1)
                    act.wait_ge(h2f_ok, j + 1)
                    A_(h2_hi[:, j, :], h2_f[:], ACT.Copy).then_inc(h2_hi_ok, 1)
                    act.wait_ge(taken[p], A_XT + i + 2)
                    act.dma_start(x1_dram[j], x1_sb[:]).then_inc(x1_stored, 16)

            act.wait_ge(x1_stored, 16 * (KD + 1))
            with act.Fori(0, KF) as i:
                act.wait_ge(units_done, U_FF1 + 2 * i + 1)
                A_(s_sb[:], joined(0), ACT.Silu).then_inc(taken[0], 1)
                act.wait_ge(taken[1], A_FF1 + i + 2)
                A_(f_hi[:, i, :], ff_sb[:], ACT.Copy).then_inc(f_hi_ok, 1)
            act.wait_ge(w_split, U_FF2 + 1)
            with act.Fori(0, KD // 2) as i:
                for p in range(2):
                    act.wait_ge(rt2_done, 2 * i + p + 1)
                    dst = rows2[:, :, :].rearrange("p t (j c) -> p t j c", c=P)[:, :, 2 * i + p, :]
                    a = (4 + 2 * p) * 512
                    A_(dst, flat[:, a:a + NT].rearrange("p (t c) -> p t c", c=P), ACT.Copy).then_inc(rows2_ok, 1)
            act.wait_ge(var2_ok, 1)
            A_(sd[:], sd[:], ACT.Sqrt).then_inc(sd2_ok, 1)

        @block.vector
        def _(v):
            steps = [0]

            def own(ins, value=None):
                steps[0] += 1
                ins.then_inc(dve, 1)
                v.wait_ge(dve, steps[0] if value is None else value(steps[0]))

            def sub(out, a, b):
                return v.tensor_tensor(out, a, b.bitcast(F32), ALU.subtract)

            v.sem_inc(yg_ok, 1)
            v.sem_inc(c_ok, 1)
            v.sem_inc(f_ok, 1)
            for _i in range(2):
                v.sem_inc(m_ok, 1)
            for _i in range(4):
                v.sem_inc(ygs_ok, 1)
            def mod_add(n, k, ring, slot, acc, first):
                for g, done in enumerate((mod_sum0, mod_sum1)):
                    part = slice(0, UW // 2 if first and g == 0 else UW)
                    w, a, c = ring[:, slot, part], acc[:, g, part], c_silu[:, k, g:g + 1]
                    if not (first and n == 0):
                        v.wait_ge(done, n)
                    if k == 0:
                        v.tensor_scalar(a, w, c, None, ALU.mult).then_inc(done, 1)
                    else:
                        v.scalar_tensor_tensor(out=a, in0=w, scalar=c, in1=a, op0=ALU.mult, op1=ALU.add)\
                            .then_inc(done, 1)

            def mod_adds(c, ks):
                for k in ks:
                    v.wait_ge(mod2_in[k % 2], 64 * c + (16 * (k // 2 + 1) - 128))
                    if k == 0:
                        v.wait_ge(mod_done, c)
                    mod_add(KD * c + k, k, mod_ring, k % 2, mod_sum, False)

            v.wait_ge(once, 1)
            for n in range(MOD1):
                v.wait_ge(mod_in[n % KD], 16 * (n // KD + 1))
                mod_add(n, n % KD, mod_first, n % KD, (mod_sum, sum_first)[n // KD], True)
            v.wait_ge(small_in, 16 * 7)
            own(v.tensor_scalar(gain_h[:], gain_sb[:], 0.5, None, ALU.mult))
            own(v.tensor_scalar(aln[:], ln_sb[:], ALPHA, None, ALU.mult))
            v.wait_ge(once, 3)
            sub(n0_lo[:], n0_sb[:], n0_hi[:]).then_inc(once_v, 1)
            v.wait_ge(mod_done, 2)
            ps_mod = psum[:, 7, 0:2 * NMOD].rearrange("p (m g) -> p m g", g=2)
            own(v.tensor_tensor(mod_sb[:, 0:MOD1, :], ps_mod[:, 0:MOD1, :], bmod_sb[:, 0:MOD1, :], ALU.add))
            v.tensor_scalar(mod_sb[:, KD:MOD1, :], mod_sb[:, KD:MOD1, :], 1.0, None, ALU.add).then_inc(mod_ready, 1)
            v.wait_ge(mod_ready, 1)
            v.wait_ge(x_in, 16)

            def h_rest(k):
                v.wait_ge(h_hi_ok, k + 1)
                sub(h_lo[:, k, :], x_sb[:, k, :], h_hi[:, k, :]).then_inc(h_ok, 1)

            for k in range(KD):
                v.tensor_scalar(x_sb[:, k, NC:NT], x_sb[:, k, NC:NT], mod_sb[:, KD + k, 1:2], mod_sb[:, k, 1:2],
                                ALU.mult, ALU.add).then_inc(x_mod, 1)
                if k >= 1:
                    h_rest(k - 1)
            h_rest(KD - 1)
            for n, (lo, hi, st) in enumerate(((dx_lo, dx_hi, dx_st), (dc_lo, dc_hi, dc_st))):
                v.wait_ge(dft_hi_ok, n + 1)
                sub(lo[:].rearrange("p a b -> p (a b)"), st[:], hi[:].rearrange("p a b -> p (a b)"))\
                    .then_inc(dft_ok, 1)

            def group(g):
                for p in range(2):
                    v.wait_ge(uf_hi_ok, 2 * g + p + 1)
                    sub(uf_lo[:, p, :], joined(p), uf_hi[:, p, :]).then_inc(taken[p], 1)
                for tt in range(TT):
                    v.wait_ge(xch_hi_ok, 5 * g + tt + 1)
                    sub(x_lo[:, tt, :], psum[:, 4 + tt % 3, 0:XW], x_hi[:, tt, :]).then_inc(xch_ok, 1)
                for kind in range(2):
                    v.wait_ge(ft_hi_ok, 2 * g + kind + 1)
                    sub(ft_lo[:, NG * kind + g, :], grids(kind), ft_hi[:, NG * kind + g, :])\
                        .then_inc(taken[kind], 1)

            with v.Fori(0, NG // 2) as gg:
                for odd in range(2):
                    mod_adds(gg + 2, range(4 * odd, 4 * odd + 4))
                    group(2 * gg + odd)

            own(v.memset(one4[:], 1.0))
            own(v.memset(r_rows[:], 0.0))
            own(v.memset(em_rows[:], 0.0))
            v.wait_ge(gate_act, 2)
            own(v.tensor_scalar(gt_m[:], gt[:], 0.0, None, ALU.min))
            v.wait_ge(gate_act, 5)
            own(v.tensor_tensor(gt_m[:], gt_m[:], gt_e[:], ALU.subtract))
            spans = (slice(0, NC), slice(NC, NT))
            backs = (slice(NC - 1, None, -1), slice(NT - 1, NC - 1, -1))
            for src, dst, row in ((gt, igs, 0), (gt_m, lfs, 64)):
                own(v.tensor_copy(dst[:, 0, :], src[row:row + H, :]))
                for s, b in zip(spans, backs):
                    own(v.tensor_copy(dst[:, 1, s], src[row + 32:row + 32 + H, b]))
            for d in range(2):
                for n, s in enumerate(spans):
                    own(v.tensor_tensor_scan(bs[:, d, s], one4[:, s], lfs[:, d, s], 0.0, ALU.mult, ALU.add))
                    own(v.tensor_tensor_scan(ms[:, d, s], lfs[:, d, s], igs[:, d, s],
                                             m0r[:, d:d + 1] if n else 0.0, ALU.add, ALU.max))
            own(v.tensor_tensor(r_rows[0:H, :], bs[:, 0, :], ms[:, 0, :], ALU.subtract))
            own(v.tensor_tensor(em_rows[0:H, :], igs[:, 0, :], bs[:, 0, :], ALU.subtract))
            own(v.tensor_copy(em_rows[64:64 + H, :], ms[:, 0, :]))
            for s, b in zip(spans, backs):
                own(v.tensor_tensor(r_rows[32:32 + H, s], bs[:, 1, b], ms[:, 1, b], ALU.subtract))
                own(v.tensor_tensor(em_rows[32:32 + H, s], igs[:, 1, b], bs[:, 1, b], ALU.subtract))
                if s is spans[0]:
                    own(v.tensor_copy(em_rows[96:96 + H, s], ms[:, 1, b]))
                else:
                    v.tensor_copy(em_rows[96:96 + H, s], ms[:, 1, b]).then_inc(gates_ok, 1)
            with v.Fori(0, 2) as jj:
                for jr in range(KD // 2):
                    j = jj * (KD // 2) + jr
                    mod_adds(jj + 4, range(2 * jr, 2 * jr + 2))
                    v.wait_ge(taken[0], A_B + j + 2)
                    v.wait_ge(units_done, U_B + 2 * j + 2)
                    v.wait_ge(z_stored, 16 * j + 16)
                    v.tensor_tensor(z_sb[:], joined(1), gb_sb[:], ALU.mult).then_inc(taken[1], 1)
            v.wait_ge(mod_done, 6)
            own(v.tensor_tensor(mod_sb[:, MOD1:NMOD, :], ps_mod[:, MOD1:NMOD, :], bmod_sb[:, MOD1:NMOD, :], ALU.add))
            own(v.tensor_scalar(mod_sb[:, 4 * KD:5 * KD, :], mod_sb[:, 4 * KD:5 * KD, :], 1.0, None, ALU.add))
            lg = ln_sb[:, 0, :].unsqueeze(2).broadcast_to([P, KD, 2])
            lb = ln_sb[:, 1, :].unsqueeze(2).broadcast_to([P, KD, 2])
            own(v.tensor_tensor(h2_s[:], mod_sb[:, 4 * KD:5 * KD, :], lg, ALU.mult))
            own(v.tensor_tensor(h2_b[:], mod_sb[:, 4 * KD:5 * KD, :], lb, ALU.mult))
            own(v.tensor_tensor(h2_b[:], h2_b[:], mod_sb[:, 3 * KD:4 * KD, :], ALU.add))

            base = steps[0]
            COMBINE = 15
            PER_HEAD = 2 + TT * COMBINE

            def combine(h, u, chain):
                tile = 1 + u if u < LT else 0
                v.wait_ge(den_done, 5 * h + u + 1)
                den = den_at(u).rearrange("p (a b) -> p a b", b=2)[:, :, 0]
                chain(v.scalar_tensor_tensor(out=den_sb[:], in0=den, scalar=-1.0, in1=enm_t[:, tile, :, h],
                                             op0=ALU.mult, op1=ALU.max))
                v.tensor_tensor(den_sb[:], den, den_sb[:], ALU.max).then_inc(den_read, 1)
                v.wait_ge(den_read, 5 * h + u + 1)
                v.reciprocal(rec[:], den_sb[:]).then_inc(rec_ok, 1)
                v.wait_ge(rec_ok, 5 * h + u + 1)
                v.wait_ge(hf_ok, 5 * h + u + 1)
                v.scalar_tensor_tensor(out=h_sb[:], in0=psum[:, 6, :], scalar=rec[:, 1:2], in1=h_sb[:],
                                       op0=ALU.mult, op1=ALU.add).then_inc(num_free, 1)
                v.wait_ge(num_free, 5 * h + u + 1)
                chain(v.bn_stats(stats[:, 0, 0, :], h_sb[:]))
                v.sem_inc(stats_seen, 1)
                chain(v.bn_aggr(mv[:, 0, :], stats[:, 0, 0, :]))
                chain(v.tensor_scalar(nt_v[:], mv[:, 0, 1:2], EPS, None, ALU.add))
                chain(v.tensor_scalar(nt_a[:].bitcast(I32), nt_v[:].bitcast(I32), 1, None,
                                      ALU.logical_shift_right))
                chain(v.tensor_scalar(nt_y[:].bitcast(I32), nt_a[:].bitcast(I32), -1.0, MAGIC,
                                      ALU.mult, ALU.add))
                for _n in range(3):
                    chain(v.scalar_tensor_tensor(out=nt_a[:], in0=nt_y[:], scalar=nt_v[:, 0:1], in1=nt_y[:],
                                                 op0=ALU.mult, op1=ALU.mult))
                    chain(v.tensor_scalar(nt_a[:], nt_a[:], -0.5, 1.5, ALU.mult, ALU.add))
                    chain(v.tensor_tensor(nt_y[:], nt_y[:], nt_a[:], ALU.mult))
                if u >= 1:
                    v.wait_ge(t_done, 5 * h + u)
                v.tensor_scalar(hn_sb[:], h_sb[:], mv[:, 0, 0:1], nt_y[:, 0:1], ALU.subtract, ALU.mult)\
                    .then_inc(hn_ok, 1)

            def gated(h, u):
                tok = wlat(u) if u < LT else slice(0, NC)
                v.wait_ge(t_done, 5 * h + u + 1)
                v.wait_ge(taken[0], A_HEAD + HA * h + 8)
                v.wait_ge(taken[1], A_HEAD + HA * h + 7)
                v.wait_ge(yg_stored, 80 * h + 16 * u + 16)
                v.scalar_tensor_tensor(out=yg_sb[:], in0=og[:, :, tok], scalar=1.0,
                                       in1=psum[:, 7, :].rearrange("p (v t) -> p v t", t=P),
                                       op0=ALU.add, op1=ALU.mult).then_inc(yg_ok, 1)

            def odd_state(h, tile):
                v.wait_ge(st_done, 5 * h + tile + 1)
                v.wait_ge(st_stored[1], 32 * h + 16 * (tile // 2) + 16)
                v.tensor_copy(st_sb[:, 1, :], psum[:, 2, :]).then_inc(taken[1], 1)

            def head(h, tail):
                U = U_HEAD + HU * h
                A = A_HEAD + HA * h
                steps[0] = base - (COMBINE if tail else 0)

                def chain(ins):
                    steps[0] += 1
                    ins.then_inc(dve, 1)
                    v.wait_ge(dve, h * PER_HEAD + steps[0])

                def diag(u):
                    if u == 0:
                        v.wait_ge(r_ok, 2 * h + 2)
                        v.wait_ge(em_ok, 2)
                    elif u >= 2:
                        v.wait_ge(p_ok, 5 * h + u - 1)
                    w = w_sb[:, u % 2]
                    pos, tile, tok = (u, 1 + u, wlat(u)) if u < LT else (0, 0, slice(0, NC))
                    v.scalar_tensor_tensor(out=w[:, pos, :], in0=r_sb[:, 0, tok],
                                           scalar=em_t[:, tile, 0, bass.ds(h, 1)], in1=mask_f,
                                           op0=ALU.add, op1=ALU.add)
                    v.scalar_tensor_tensor(out=w[:, pos + 1, :], in0=r_sb[:, 1, tok],
                                           scalar=em_t[:, tile, 1, bass.ds(h, 1)], in1=mask_b,
                                           op0=ALU.add, op1=ALU.add).then_inc(diag_ok, 1)

                def probs(u):
                    w = w_sb[:, u % 2]
                    v.wait_ge(e_ok, 5 * h + u + 1)
                    if u == LT:
                        chain(v.tensor_copy(wg[:, 0:1], w[:, 0, NC - 1:NC]))
                        chain(v.tensor_copy(wg[:, 1:2], w[:, 1, 0:1]))
                    v.wait_ge(s_done, 5 * h + u + 1)
                    if u < LT:
                        s4 = psum[:, 4, :].rearrange("p (s t) -> p s t", t=P)
                        v.tensor_tensor(w[:, 0:u + 1, :], w[:, 0:u + 1, :], s4[:, 0:u + 1, :], ALU.mult)
                        v.tensor_tensor(w[:, u + 1:, :], w[:, u + 1:, :], s4[:, u:, :], ALU.mult)\
                            .then_inc(s_free, 1)
                        for d in range(2):
                            ins = v.tensor_tensor(qi_f[:, d, :, :], q_f[:, :, u * P:(u + 1) * P],
                                                  i_sb[:, u % 2, d, :].unsqueeze(1).broadcast_to([P, KQ, P]), ALU.mult)
                        ins.then_inc(p_f_ok, 1)
                    else:
                        s1 = psum[:, 4, 0:P]
                        v.tensor_tensor(w[:, 0, :], w[:, 0, :], s1, ALU.mult)
                        v.tensor_tensor(w[:, 1, :], w[:, 1, :], s1, ALU.mult).then_inc(s_free, 1)
                        v.wait_ge(s_free, 5 * h + 5)
                        v.sem_inc(p_f_ok, 1)

                def p_rest(u):
                    v.wait_ge(p_hi_ok, 5 * h + u + 1)
                    if u < LT:
                        sub(p_lo[:, u % 2, :, :], w_sb[:, u % 2, :, :], p_hi[:, u % 2, :, :])
                        sub(qi_lo[:, u % 2, :, :, :], qi_f[:], qi_hi[:, u % 2, :, :, :]).then_inc(p_ok, 1)
                    else:
                        sub(p_lo[:, u % 2, 0:2, :], w_sb[:, u % 2, 0:2, :], p_hi[:, u % 2, 0:2, :]).then_inc(p_ok, 1)

                v.tensor_scalar(r_head[:], r_rows[:], onehot[:, bass.ds(h, 1)], None, ALU.mult).then_inc(rh_ok, 1)

                def qk_rest(n):
                    v.wait_ge(qk_hi_ok, 4 * h + n + 1)
                    src = joined(n % 2)
                    if n < 2:
                        v.tensor_copy(q_f[:, n, :], src[:, NC:NT])
                        sub(q_lo[:, n, :], src, q_hi[:, n, :]).then_inc(taken[n % 2], 1)
                    else:
                        v.tensor_scalar(k_c[:, n % 2, :], src[:, 0:NC], QSCALE, None, ALU.mult)
                        v.scalar_tensor_tensor(out=k_lo[:, n % 2, :], in0=src, scalar=QSCALE,
                                               in1=k_hi[:, n % 2, :].bitcast(F32), op0=ALU.mult,
                                               op1=ALU.subtract).then_inc(taken[n % 2], 1)

                if tail:
                    combine(h - 1, 4, chain)
                qk_rest(0)
                if tail:
                    gated(h - 1, 3)
                qk_rest(1)
                if tail:
                    gated(h - 1, 4)
                    odd_state(h - 1, 1)
                    odd_state(h - 1, 3)
                qk_rest(2)
                diag(0)
                diag(1)
                qk_rest(3)
                v.wait_ge(c_hi_ok, h + 1)
                sub(c_lo[:], c_raw[:], c_hi[:]).then_inc(c_ok, 1)
                for tt in range(TT):
                    v.wait_ge(v_hi_ok, 5 * h + tt + 1)
                    sub(v_lo[:, tt, :], psum[:, (0, 4, 5, 6, 7)[tt], :], v_hi[:, tt, :]).then_inc(v_ok, 1)
                probs(0)
                p_rest(0)
                diag(2)
                probs(1)
                p_rest(1)
                diag(3)
                combine(h, 0, chain)
                probs(2)
                p_rest(2)
                diag(4)
                combine(h, 1, chain)
                gated(h, 0)
                probs(3)
                p_rest(3)
                combine(h, 2, chain)
                gated(h, 1)
                probs(4)
                p_rest(4)
                v.wait_ge(kt_done, h + 1)
                v.tensor_scalar(kw_f[:, 0, :], psum[:, 2, 0:DQK], wg[:, 0:1], None, ALU.mult)
                v.tensor_scalar(kw_f[:, 1, :], psum[:, 2, 0:DQK], wg[:, 1:2], None, ALU.mult).then_inc(taken[1], 1)
                v.wait_ge(kw_hi_ok, h + 1)
                sub(kw_lo[:], kw_f[:], kw_hi[:]).then_inc(kw_ok, 1)
                combine(h, 3, chain)
                gated(h, 2)
                assert steps[0] == base + PER_HEAD - COMBINE

            head(0, False)
            with v.Fori(1, H) as h:
                head(h, True)
            steps[0] = base + H * PER_HEAD - COMBINE
            combine(H - 1, 4, own)
            gated(H - 1, 3)
            gated(H - 1, 4)
            odd_state(H - 1, 1)
            odd_state(H - 1, 3)

            with v.Fori(0, H * KV // 4) as i:
                for r in range(4):
                    v.wait_ge(ygs_hi_ok, 4 * i + r + 1)
                    v.scalar_tensor_tensor(out=yg_lo[:, 4 * i + r, :], in0=yg_st[:, r, :],
                                           scalar=gain_h[:, bass.ds(4 * i + r, 1)],
                                           in1=yg_hi[:, 4 * i + r, :].bitcast(F32),
                                           op0=ALU.mult, op1=ALU.subtract).then_inc(ygs_ok, 1)
            base2 = steps[0]
            with v.Fori(0, KD // 2) as i:
                for p in range(2):
                    j = 2 * i + p
                    v.wait_ge(units_done, U_MIX + 4 * i + 2 * p + 2)
                    v.wait_ge(z_in[p], 16 * i + 16)
                    v.wait_ge(m_ok, j + 2)
                    v.tensor_tensor(m_sb[:], joined(p), ga_sb[:, j, :], ALU.mult).then_inc(taken[p], 1)
                    v.wait_ge(taken[p], A_MIX + i + 2)
                    v.tensor_tensor(m_sb[:], m_sb[:], z_st[:, p, :], ALU.add).then_inc(m_f_ok, 1)
                    v.wait_ge(m_hi_ok, j + 1)
                    sub(mg_lo[:, j, :], m_sb[:], mg_hi[:, j, :]).then_inc(m_ok, 1)

            def residual(i, p, unit, a_first, landed, st, rt, gcol):
                j = 2 * i + p
                v.wait_ge(units_done, unit)
                v.wait_ge(landed[p], 16 * i + 16)
                src = joined(p)
                for g, span in enumerate((slice(0, NC), slice(NC, NT))):
                    ins = v.scalar_tensor_tensor(out=rt[:, p, span], in0=src[:, span],
                                                 scalar=mod_sb[:, gcol + j, g:g + 1],
                                                 in1=st[:, p, span], op0=ALU.mult, op1=ALU.add)
                ins.then_inc(taken[p], 1)

            with v.Fori(0, KD // 2) as i:
                for p in range(2):
                    j = 2 * i + p
                    v.wait_ge(xs_in[p], 16 * i + 16)
                    ins = v.tensor_scalar(x_st[:, p, :], x_st[:, p, :], ALPHA, None, ALU.mult)
                    ins.then_inc(dve, 1)
                    v.wait_ge(dve, 2 * i + (base2 + p + 1))
                    residual(i, p, U_OUT + 2 * i + p + 1, A_OUT, xs_in, x_st, r_t, 2 * KD)
            steps[0] = base2 + KD

            def norm_rows(src, ok, var_sem, sd_sem, done, gains=None):
                v.wait_ge(ok, KD + 2)
                for tt in range(TT):
                    for b in range(2):
                        own(v.bn_stats(stats[:, tt, b, :], src[:, tt, b * 512:(b + 1) * 512]))
                    own(v.bn_aggr(mv[:, tt, :], stats[:, tt, :, :]))
                v.tensor_scalar(sd[:], mv[:, :, 1], EPS, None, ALU.add).then_inc(var_sem, 1)
                v.wait_ge(sd_sem, 1)
                own(v.reciprocal(rstd[:], sd[:]))
                for tt in range(TT):
                    ins = v.tensor_scalar(src[:, tt, :], src[:, tt, :], mv[:, tt, 0:1], rstd[:, tt:tt + 1],
                                          ALU.subtract, ALU.mult)
                    if gains is None:
                        ins.then_inc(done, 1)
                        continue
                    own(ins)
                    own(v.tensor_tensor(src[:, tt, :], src[:, tt, :], gains[:, 0, :], ALU.mult))
                    v.tensor_tensor(src[:, tt, :], src[:, tt, :], gains[:, 1, :], ALU.add).then_inc(done, 1)

            norm_rows(rows, rows_ok, var_ok, sd_ok, xn_ok)
            with v.Fori(0, KD // 2) as i:
                for p in range(2):
                    j = 2 * i + p
                    v.wait_ge(xt_done, j + 1)
                    v.wait_ge(x1_stored, 32 * i + 16 * p + 16)
                    v.wait_ge(h2_hi_ok, j + 1)
                    v.tensor_scalar(x1_sb[:], joined(p), aln[:, 0, bass.ds(j, 1)], aln[:, 1, bass.ds(j, 1)],
                                    ALU.mult, ALU.add).then_inc(x1_ok, 1)
                    v.wait_ge(x1_ok, j + 1)
                    sub(h2_lo[:, j, :], h2_f[:], h2_hi[:, j, :]).then_inc(taken[p], 1)

            with v.Fori(0, KF) as i:
                v.wait_ge(taken[0], A_FF1 + i + 2)
                v.wait_ge(units_done, U_FF1 + 2 * i + 2)
                v.wait_ge(f_ok, i + 1)
                v.tensor_tensor(ff_sb[:], joined(1), s_sb[:], ALU.mult).then_inc(taken[1], 1)
                v.wait_ge(f_hi_ok, i + 1)
                sub(f_lo[:, i, :], ff_sb[:], f_hi[:, i, :]).then_inc(f_ok, 1)
            with v.Fori(0, KD // 2) as i:
                for p in range(2):
                    residual(i, p, U_FF2 + 4 * i + 2 * p + 2, A_FF2, x1s_in, x2_st, r2_t, 5 * KD)
            v.wait_ge(lnr_in, 16)
            norm_rows(rows2, rows2_ok, var2_ok, sd2_ok, y_ok, ln_row)


_OUTS = [("y_prompt", (NC, DMODEL)), ("y_sample", (NL, DMODEL)), ("new_C", (2, H, DV, DQK)),
         ("new_n", (2, H, DQK)), ("new_m", (2, H, 1))]


def dft_constants():
    c = np.arange(DG)
    ang = 2 * np.pi * np.outer(c, c) / DG
    cos, sin = np.cos(ang) / np.sqrt(DG), np.sin(ang) / np.sqrt(DG)
    chan = np.zeros((DG, XW))
    chan[:, 0:P] = cos[:, 0:P]
    chan[:, 0] = (cos[:, 0] + cos[:, P]) / 2
    chan[:, P:2 * P] = sin[:, 0:P]
    chan[:, 2 * P] = (cos[:, P] - cos[:, 0]) / 2
    t = np.arange(NC)
    a = 2 * np.pi * np.outer(t, t) / NC
    pos_c = np.stack([np.cos(a), np.sin(a)]) / np.sqrt(NC)
    r, w = np.arange(NL) // GRID_W, np.arange(NL) % GRID_W
    a = 2 * np.pi * (np.outer(r, r) * GRID_W / NL + np.outer(w, w) / GRID_W)
    pos_l = np.stack([np.cos(a), np.sin(a)]) / np.sqrt(NL)
    f = np.float32
    return (np.ascontiguousarray(pos_c.transpose(1, 0, 2), f).reshape(P, 2 * NC),
            np.ascontiguousarray(pos_l.reshape(2, LT, P, NL).transpose(2, 0, 1, 3), f).reshape(P, 2 * LT * NL),
            np.ascontiguousarray(chan.reshape(2, P, XW).transpose(1, 0, 2), f).reshape(P, 2 * XW))


def const_block():
    s, t = np.arange(P)[:, None], np.arange(P)[None, :]
    out = np.zeros((P, 5 * P + H), np.float32)
    out[:, 0:P] = np.eye(P)
    out[:, P:2 * P] = np.where(s <= t, 0.0, -1e30)
    out[:, 2 * P:3 * P] = np.where(s >= t, 0.0, -1e30)
    out[0:H, 3 * P:4 * P] = 1.0
    out[32:32 + H, 4 * P:5 * P] = 1.0
    for h in range(H):
        out[h, 5 * P + h] = out[32 + h, 5 * P + h] = 1.0
    return out


def blocks(w):
    k, n = w.shape
    return w.reshape(k // P, P, n // P, P).transpose(2, 1, 0, 3).reshape(n // P, P, k)


def kernel(**inputs):
    import concourse.bacc as _bacc
    from concourse.bass_utils import run_bass_kernel_spmd as _run

    a = {k: np.asarray(v) for k, v in inputs.items()}
    w_in = a["w_in"][0]
    cuts = [0, H * DQK, 2 * H * DQK, 2 * H * DQK + DM, 2 * H * DQK + 2 * DM]
    g_end = cuts[4] + 4 * H
    wq, wk, wv, wo = (w_in[:, cuts[i]:cuts[i + 1]] for i in range(4))
    wg = w_in[:, cuts[4]:g_end]
    wf, wga, wgb = (w_in[:, g_end + i * DMODEL:g_end + (i + 1) * DMODEL] for i in range(3))
    wb = a["w_branch_b"][0].reshape(NG, DG, KD, P)
    low = wb[:, 0:P]
    high = np.concatenate([wb[:, P:P + 1], wb[:, :P:-1]], axis=1)
    ub = np.stack([low, high]).transpose(3, 2, 0, 1, 4).reshape(KD, P, UW)
    gb = blocks(wgb)
    q, k, o = blocks(wq), blocks(wk), blocks(wo)
    vv = wv.reshape(4, 2, P, H, DV).transpose(3, 0, 2, 1, 4).reshape(H, 4, P, 2 * DV)
    wa = blocks(a["w_branch_a"][0]).reshape(KD, P, 2, UW).transpose(0, 2, 1, 3)
    ffi = blocks(a["w_ffn_in"][0])
    parts = [blocks(wf), np.stack([gb, ub], axis=1).reshape(2 * KD, P, UW)]
    for h in range(H):
        parts += [q[2 * h:2 * h + 2], k[2 * h:2 * h + 2], vv[h], o[4 * h:4 * h + 4]]
    parts += [blocks(wga), wa.reshape(2 * KD, P, UW), blocks(a["w_out"][0]),
              np.stack([ffi[:KF], ffi[KF:]], axis=1).reshape(2 * KF, P, UW)]
    wunits = np.concatenate(parts)
    wffo = blocks(a["w_ffn_out"][0]).reshape(KD, P, 2, FW).transpose(0, 2, 1, 3).reshape(2 * KD, P, FW)
    gates = np.zeros((KD, P, P), np.float32)
    gbias = np.zeros((P, 1), np.float32)
    for d in range(2):
        for kind in range(2):
            row, col = 64 * kind + 32 * d, (2 * d + kind) * H
            gates[:, :, row:row + H] = wg[:, col:col + H].reshape(KD, P, H)
            gbias[row:row + H, 0] = a["b_gate"][0][col:col + H]
    x = np.concatenate([a["x_prompt"][0], a["x_sample"][0]])
    cc = np.stack([a["c_ctx"], a["c"][0]])
    sm = a["state_m"][0, 0]
    sn = a["state_n"][0, 0].reshape(2, H, KQ, P).transpose(3, 1, 0, 2)
    pos_c, pos_l, chan = dft_constants()
    ln = np.stack([a["ln_gain"][0], a["ln_bias"][0]], axis=1)
    arrays = {
        "wunits": wunits, "wffo": wffo, "wmod": a["w_mod"][0].reshape(KD, P, 6, UW).transpose(2, 0, 1, 3).reshape(NMOD, P, UW),
        "xT": x.reshape(NT, KD, P).transpose(2, 1, 0), "cT": cc.reshape(2, KD, P).transpose(2, 1, 0),
        "bmod": np.repeat(a["b_mod"][0].reshape(NMOD, P).T[:, :, None], 2, axis=2),
        "consts": const_block(), "dft_c": pos_c, "dft_l": pos_l, "dft_x": chan,
        "wgate": gates.transpose(1, 0, 2).reshape(P, UW), "gate_bias": gbias,
        "stateC": a["state_C"][0, 0].reshape(2, H, DV, KQ, P).transpose(1, 4, 0, 3, 2),
        "state_n": np.repeat(sn[..., None], 2, axis=4), "m0_rows": sm.T,
        "m0_bcast": np.repeat(sm[None], P, axis=0), "gainT": a["mh_gain"][0].reshape(H * KV, P).T,
        "lnT": ln[0].reshape(2, KD, P).transpose(2, 0, 1), "ln_rows": np.repeat(ln[1][None], P, axis=0),
    }
    nc = _bacc.Bacc("TRN2", target_bir_lowering=False, num_devices=1)
    args, host = [], {}
    for name, value in arrays.items():
        value = np.ascontiguousarray(value)
        host[f"in_{name}"] = value
        args.append(nc.dram_tensor(f"in_{name}", value.shape, F32, kind="ExternalInput").ap())
    for name, shape in _OUTS:
        args.append(nc.dram_tensor(f"out_{name}", shape, F32, kind="ExternalOutput").ap())
    build(nc, *args)
    r = _run(nc, [host], core_ids=[0]).results[0]
    return (r["out_y_prompt"][None], r["out_y_sample"][None], r["out_new_C"][None, None],
            r["out_new_n"][None, None], r["out_new_m"][None, None, :, :, 0])
```

```python
from contextlib import ExitStack

import numpy as np

import concourse.bass as bass
from concourse import mybir

F32 = mybir.dt.float32
F32R = mybir.dt.float32r
I32 = mybir.dt.int32
ALU = mybir.AluOpType
ACT = mybir.ActivationFunctionType

P = 128
DMODEL = 1024
NC = 128
NL = 512
NT = NC + NL
TT = NT // P
LT = NL // P
GRID_W = 64
H = 4
DM = 2 * DMODEL
DV = DM // H
DQK = DV // 2
KD = DMODEL // P
KQ = DQK // P
KV = DV // P
NG = 4
DG = DMODEL // NG
CUT = 256
XW = DG + 2
DFF = ((8 * DMODEL // 3 + 255) // 256) * 256
KF = DFF // P
ALPHA = float(np.float32(2.0 ** 0.25))
EPS = 1e-5
QSCALE = DQK ** -0.5
UB = 8
UW = UB * P
FQ = (UB, UB, KF - 2 * UB)

U_PASS1 = 0
U_B = 2 * NG
U_HEAD = U_B + 2 * KD
HU = 2 * KQ + 4 + KV
U_GA = U_HEAD + H * HU
U_MIX = U_GA + KD
U_OUT = U_MIX + 2 * KD
U_FF1 = U_OUT + KD
U_FF2 = U_FF1 + 2 * KF
U_END = U_FF2 + len(FQ) * KD
NMOD = 6 * KD
MOD1 = 2 * KD

A_F = 0
A_B = A_F + 2 * NG
A_HEAD = A_B + KD
HA = 7
A_GA = A_HEAD + HA * H
A_MIX = A_GA + 3 + KD // 2
A_OUT = A_MIX + KD // 2
A_FF1 = A_OUT + KD // 2
A_FF2 = A_FF1 + KF
MAGIC = float(0x5F3759DF)


def build(nc, wunits, wmod, xT, cT, bmod, consts, dft_c, dft_l, dft_x, wgate, gate_bias,
          stateC, state_n, m0_rows, m0_bcast, gainT, lnT, ln_rows,
          y_prompt, y_sample, new_C, new_n, new_m):
    ctx = ExitStack()
    with ctx:
        sem = lambda name: ctx.enter_context(nc.semaphore(name))
        psum = ctx.enter_context(nc.psum_tensor("psum", [P, 8, 512], F32))
        flat = psum[:, :, :].rearrange("p b c -> p (b c)")

        z_dram = nc.dram_tensor("z_dram", [KD, P, NT], F32, kind="Internal").ap()
        yg_dram = nc.dram_tensor("yg_dram", [H, KV, P, NT], F32, kind="Internal").ap()
        x1_dram = nc.dram_tensor("x1_dram", [P, KD, NT], F32, kind="Internal").ap()

        top = [(nc.sbuf_base + 63) // 64 * 64]

        def at(name, shape, dt, cursor):
            t = nc.alloc_sbuf_tensor_at(name, shape, dt, offset=cursor[0])
            size = int(np.prod(shape[1:])) * 4
            cursor[0] += (size + 63) // 64 * 64
            assert cursor[0] <= nc.sbuf_usable_end, (name, cursor[0])
            return t

        keep = lambda name, shape, dt=F32: at(name, shape, dt, top)
        const_sb = keep("const_sb", [P, 5 * P + H])
        ident, mask_f, mask_b, sel_f, sel_b = (const_sb[:, i * P:(i + 1) * P] for i in range(5))
        onehot = const_sb[:, 5 * P:5 * P + H]
        ones_r = keep("ones_r", [P, P], F32R)
        c_sb = keep("c_sb", [P, KD, 2])
        c_silu = keep("c_silu", [P, KD, 2])
        bmod_sb = keep("bmod_sb", [P, NMOD, 2])
        mod_sb = keep("mod_sb", [P, NMOD, 2])
        gbias = keep("gbias", [P, 1])
        zero = keep("zero", [P, 1])
        em_t = keep("em_t", [P, TT, 4, 32])
        enm_t = keep("enm_t", [P, TT, 2, 32])
        r_rows = keep("r_rows", [P, NT])
        r_head = keep("r_head", [P, NT])
        m0r = keep("m0r", [H, 2])
        m0b = keep("m0b", [P, 2, H])
        n0_sb = keep("n0_sb", [P, H, 2, KQ, 2])
        n0_hi = keep("n0_hi", [P, H, 2, KQ, 2], F32R)
        n0_lo = keep("n0_lo", [P, H, 2, KQ, 2], F32R)
        gain_sb = keep("gain_sb", [P, H * KV])
        gain_h = keep("gain_h", [P, H * KV])
        ln_sb = keep("ln_sb", [P, 2, KD])
        aln = keep("aln", [P, 2, KD])
        h2_s = keep("h2_s", [P, KD, 2])
        h2_b = keep("h2_b", [P, KD, 2])
        stats = keep("stats", [P, 6])
        eps_sb = keep("eps_sb", [P, 1])
        mv = keep("mv", [P, TT, 2])
        rstd = keep("rstd", [P, TT])
        sd = keep("sd", [P, TT])
        nmr = keep("nmr", [P, TT])
        den_sb = keep("den_sb", [P, 2])
        rec = keep("rec", [P, 2])
        wg = keep("wg", [P, 2])
        nt_v = keep("nt_v", [P, 1])
        nt_y = keep("nt_y", [P, 1])
        nt_a = keep("nt_a", [P, 1])

        c1 = [top[0]]
        raw = at("raw", [P, 2, UW], F32, c1)
        w_hi = at("w_hi", [P, 2, UW], F32R, c1)
        w_lo = at("w_lo", [P, 2, UW], F32R, c1)
        ring_end = c1[0]
        h_hi = at("h_hi", [P, KD, NT], F32R, c1)
        h_lo = at("h_lo", [P, KD, NT], F32R, c1)
        h_end = c1[0]
        c0 = [h_end]
        x_sb = at("x_sb", [P, KD, NT], F32, c0)
        mod_first = at("mod_first", [P, 8, UW], F32, c0)
        sum_first = at("sum_first", [P, 2, UW], F32, c0)
        prod = at("prod", [P, 4, UW // 2], F32, c0)
        cs = [h_end + 4 * KD * NT]
        dl_st = at("dl_st", [P, 2 * LT * NL], F32, cs)
        dc_st = at("dc_st", [P, 2 * NC], F32, cs)
        dx_st = at("dx_st", [P, 2 * XW], F32, cs)
        assert cs[0] <= h_end + 2 * 4 * 2 * NG * NT
        cp = [h_end]
        ft_hi = at("ft_hi", [P, 2 * NG, NT], F32R, cp)
        ft_lo = at("ft_lo", [P, 2 * NG, NT], F32R, cp)
        uf_hi = at("uf_hi", [P, 2, NT], F32R, cp)
        uf_lo = at("uf_lo", [P, 2, NT], F32R, cp)
        x_hi = at("xch_hi", [P, TT, XW], F32R, cp)
        x_lo = at("xch_lo", [P, TT, XW], F32R, cp)
        dl_hi = at("dl_hi", [P, 2, LT, NL], F32R, cp)
        dl_lo = at("dl_lo", [P, 2, LT, NL], F32R, cp)
        dc_hi = at("dc_hi", [P, 2, NC], F32R, cp)
        dc_lo = at("dc_lo", [P, 2, NC], F32R, cp)
        dx_hi = at("dx_hi", [P, 2, XW], F32R, cp)
        dx_lo = at("dx_lo", [P, 2, XW], F32R, cp)
        cp_end = cp[0]
        wb_sum = at("wb_sum", [P, UW], F32, cp)
        mod_ring = at("mod_ring", [P, 2, UW], F32, cp)
        mod_sum = at("mod_sum", [P, 2, UW], F32, cp)
        gate_w = wb_sum
        gw_hi = at("gw_hi", [P, UW], F32R, cp)
        gw_lo = at("gw_lo", [P, UW], F32R, cp)
        cq = [uf_hi_off := h_end + 2 * 2 * NG * NT * 4]
        gb_sb = at("gb_sb", [P, NT], F32, cq)
        z_sb = at("z_sb", [P, NT], F32, cq)
        gt = at("gt", [P, NT], F32, cq)
        gt_e = at("gt_e", [P, NT], F32, cq)
        gt_m = at("gt_m", [P, NT], F32, cq)
        igs = at("igs", [H, 2, NT], F32, cq)
        lfs = at("lfs", [H, 2, NT], F32, cq)
        bs = at("bs", [H, 2, NT], F32, cq)
        ms = at("ms", [H, 2, NT], F32, cq)
        one4 = at("one4", [H, NT], F32, cq)
        em_rows = at("em_rows", [P, NT], F32, cq)
        assert cq[0] <= cp_end
        ch = [h_end]
        q_hi = at("q_hi", [P, KQ, NT], F32R, ch)
        q_lo = at("q_lo", [P, KQ, NT], F32R, ch)
        k_hi = at("k_hi", [P, KQ, NT], F32R, ch)
        k_lo = at("k_lo", [P, KQ, NT], F32R, ch)
        q_f = at("q_f", [P, KQ, NL], F32, ch)
        k_c = at("k_c", [P, KQ, NC], F32, ch)
        v_hi = at("v_hi", [P, TT, DV], F32R, ch)
        v_lo = at("v_lo", [P, TT, DV], F32R, ch)
        og = at("og", [P, KV, NT], F32, ch)
        r_sb = at("r_sb", [P, 2, NT], F32, ch)
        w_sb = at("w_sb", [P, 2, LT + 1, P], F32, ch)
        i_sb = at("i_sb", [P, 2, 2, P], F32, ch)
        qi_f = at("qi_f", [P, 2, KQ, P], F32, ch)
        p_hi = at("p_hi", [P, 2, LT + 1, P], F32R, ch)
        p_lo = at("p_lo", [P, 2, LT + 1, P], F32R, ch)
        qi_hi = at("qi_hi", [P, 2, 2, KQ, P], F32R, ch)
        qi_lo = at("qi_lo", [P, 2, 2, KQ, P], F32R, ch)
        c_raw = at("c_raw", [P, 2, KQ, DV], F32, ch)
        c_hi = at("c_hi", [P, 2, KQ, DV], F32R, ch)
        c_lo = at("c_lo", [P, 2, KQ, DV], F32R, ch)
        kw_f = at("kw_f", [P, 2, DQK], F32, ch)
        kw_hi = at("kw_hi", [P, 2, DQK], F32R, ch)
        kw_lo = at("kw_lo", [P, 2, DQK], F32R, ch)
        h_sb = at("h_sb", [P, DV], F32, ch)
        hn_sb = at("hn_sb", [P, DV], F32, ch)
        yg_sb = at("yg_sb", [P, KV, P], F32, ch)
        st_sb = at("st_sb", [P, 2, 2 * DQK], F32, ch)
        nn_sb = at("nn_sb", [1, 2 * DQK], F32, ch)
        cm = [h_end]
        yg_hi = at("yg_hi", [P, H * KV, NT], F32R, cm)
        yg_lo = at("yg_lo", [P, H * KV, NT], F32R, cm)
        ga_sb = at("ga_sb", [P, KD, NT], F32, cm)
        z_st = at("z_st", [P, 2, NT], F32, cm)
        m_sb = at("m_sb", [P, NT], F32, cm)
        yg_st = at("yg_st", [P, 4, NT], F32, cm)
        cg = [ring_end]
        mg_hi = at("mg_hi", [P, KD, NT], F32R, cg)
        mg_lo = at("mg_lo", [P, KD, NT], F32R, cg)
        assert cg[0] <= h_end
        cf = [ring_end]
        f_hi = at("f_hi", [P, KF, NT], F32R, cf)
        f_lo = at("f_lo", [P, KF, NT], F32R, cf)
        f_end = cf[0]
        h2_hi = at("h2_hi", [P, KD, NT], F32R, cf)
        h2_lo = at("h2_lo", [P, KD, NT], F32R, cf)
        r2_t = at("r2_t", [P, 2, NT], F32, [cf[0]])
        s_sb = at("s_sb", [P, NT], F32, cf)
        ff_sb = at("ff_sb", [P, NT], F32, cf)
        ln_row = at("ln_row", [P, 2, DMODEL], F32, cf)
        stats2 = at("stats2", [P, TT, KD, 6], F32, cf)
        r_all = at("r_all", [P, KD, NT], F32, [f_end - 4 * KD * NT])
        co = [h_end]
        r_hi = at("r_hi", [P, 2, NT], F32R, co)
        r_lo = at("r_lo", [P, 2, NT], F32R, co)
        sq_f = at("sq_f", [P, 2, NT], F32, co)
        sq_hi = at("sq_hi", [P, 2, NT], F32R, co)
        sq_lo = at("sq_lo", [P, 2, NT], F32R, co)
        mu = at("mu", [P, NT], F32, co)
        musq = at("musq", [P, NT], F32, co)
        var_b = at("var_b", [P, NT], F32, co)
        rstd_b = at("rstd_b", [P, NT], F32, co)
        h2_f = at("h2_f", [P, 2, NT], F32, co)
        assert co[0] <= f_end - 4 * KD * NT
        c2 = [f_end]
        x2_all = at("x2_all", [P, KD, NT], F32, c2)
        rows2 = at("rows2", [P, TT, DMODEL], F32, c2)
        assert c2[0] <= f_end + 4 * 2 * KD * NT

        small_in = sem("small_in")
        c_sb_in = sem("c_sb_in")
        const_in = sem("const_in")
        gw_in = sem("gw_in")
        mod_ready = sem("mod_ready")
        x_mod_c = sem("x_mod_c")
        zero_ok = sem("zero_ok")
        x_in = sem("x_in")
        dft_in = sem("dft_in")
        raw_in = [sem(f"raw_in{r}") for r in range(2)]
        mod_in = [sem(f"mod_in{r}") for r in range(8)]
        mod2_in = [sem(f"mod2_in{r}") for r in range(2)]
        c_in = sem("c_in")
        w_half = sem("w_half")
        w_split = sem("w_split")
        units_done = sem("units_done")
        mod_sum0 = sem("mod_sum0")
        mod_sum1 = sem("mod_sum1")
        prod_ok = sem("prod_ok")
        mod_sum_p = sem("mod_sum_p")
        mod_done = sem("mod_done")
        taken = [sem("taken_a"), sem("taken_b")]
        once = sem("once")
        once_v = sem("once_v")
        x_mod = sem("x_mod")
        h_hi_ok = sem("h_hi_ok")
        h_ok = sem("h_ok")
        dft_hi_ok = sem("dft_hi_ok")
        dft_ok = sem("dft_ok")
        dl_ok = sem("dl_ok")
        uf_hi_ok = sem("uf_hi_ok")
        xch_done = sem("xch_done")
        xch_hi_ok = sem("xch_hi_ok")
        xch_ok = sem("xch_ok")
        pos_done = sem("pos_done")
        ft_hi_ok = sem("ft_hi_ok")
        z_stored = sem("z_stored")
        gate_acc = sem("gate_acc")
        gate_act = sem("gate_act")
        gates_ok = sem("gates_ok")
        em_acc = sem("em_acc")
        em_ok = sem("em_ok")
        m_stored = sem("m_stored")
        dve = sem("dve")
        rh_ok = sem("rh_ok")
        r_done = sem("r_done")
        r_ok = sem("r_ok")
        qk_hi_ok = sem("qk_hi_ok")
        c_hi_ok = sem("c_hi_ok")
        c_ok = sem("c_ok")
        v_hi_ok = sem("v_hi_ok")
        v_ok = sem("v_ok")
        diag_ok = sem("diag_ok")
        e_ok = sem("e_ok")
        s_done = sem("s_done")
        s_free = sem("s_free")
        p_f_ok = sem("p_f_ok")
        p_hi_ok = sem("p_hi_ok")
        p_ok = sem("p_ok")
        den_done = sem("den_done")
        den_read = sem("den_read")
        num_done = sem("num_done")
        rec_ok = sem("rec_ok")
        hf_ok = sem("hf_ok")
        num_free = sem("num_free")
        hn_ok = sem("hn_ok")
        t_done = sem("t_done")
        yg_ok = sem("yg_ok")
        yg_stored = sem("yg_stored")
        kt_done = sem("kt_done")
        kw_hi_ok = sem("kw_hi_ok")
        kw_ok = sem("kw_ok")
        st_done = sem("st_done")
        st_stored = [sem("st_stored0"), sem("st_stored1")]
        nn_stored = sem("nn_stored")
        ygs_in = [sem(f"ygs_in{r}") for r in range(4)]
        ygs_hi_ok = sem("ygs_hi_ok")
        ygs_ok = sem("ygs_ok")
        z_in = [sem("z_in0"), sem("z_in1")]
        m_f_ok = sem("m_f_ok")
        m_hi_ok = sem("m_hi_ok")
        m_ok = sem("m_ok")
        xs_in = [sem("xs_in0"), sem("xs_in1")]
        r_split = sem("r_split")
        sq_f_ok = sem("sq_f_ok")
        sq_split = sem("sq_split")
        st_in = sem("st_in")
        stats_done = sem("stats_done")
        stats_seen = sem("stats_seen")
        mu_ok = sem("mu_ok")
        var_b_ok = sem("var_b_ok")
        sd_b_ok = sem("sd_b_ok")
        centred = sem("centred")
        t2_ok = sem("t2_ok")
        x1_ok = sem("x1_ok")
        x1_stored = sem("x1_stored")
        h2f_ok = sem("h2f_ok")
        h2_ok = sem("h2_ok")
        h2_hi_ok = sem("h2_hi_ok")
        f_hi_ok = sem("f_hi_ok")
        f_ok = sem("f_ok")
        x1s_in = [sem("x1s_in0"), sem("x1s_in1")]
        lnr_in = sem("lnr_in")
        rt2_done = sem("rt2_done")
        rows2_ok = sem("rows2_ok")
        var2_ok = sem("var2_ok")
        sd2_ok = sem("sd2_ok")
        norm_ok = sem("norm_ok")
        gain_ok = sem("gain_ok")
        y_ok = sem("y_ok")
        y_ok_p = sem("y_ok_p")
        y_stored = sem("y_stored")

        def joined(pair):
            a = 2 * pair * 512 + 512 - CUT
            return flat[:, a:a + NT]

        def grids(pair):
            a = 2 * pair * 512 + 512 - NC
            return flat[:, a:a + NT]

        def two(ap):
            return ap.rearrange("p (a b) -> p a b", a=2)

        O_PAIR = (1, 0, 0, 1)

        def den_at(u):
            return psum[:, (3, 1, 1, 1, 3)[u], 0:4]

        def wlat(tt):
            return slice(NC + P * tt, NC + P * tt + P)

        N_SMALL = 12
        block = ctx.enter_context(nc.Block())

        @block.sync
        def _(sp):
            for m in range(4):
                sp.dma_start(mod_first[:, m, :], wmod[m]).then_inc(mod_in[m], 16)
            for dst, src in ((bmod_sb[:], bmod), (gbias[:], gate_bias),
                             (m0r[:], m0_rows), (m0b[:], m0_bcast), (n0_sb[:], state_n), (gain_sb[:], gainT),
                             (ln_sb[:], lnT)):
                sp.dma_start(dst, src).then_inc(small_in, 16)
            for m in range(4, 8):
                sp.dma_start(mod_first[:, m, :], wmod[m]).then_inc(mod_in[m], 16)
            for r in range(2):
                sp.dma_start(raw[:, r, :], wunits[r]).then_inc(raw_in[r], 16)
            for m in range(8):
                sp.wait_ge(mod_sum1, m + 1)
                sp.wait_ge(prod_ok, m + 1)
                sp.dma_start(mod_first[:, m, :], wmod[8 + m]).then_inc(mod_in[m], 16)
            sp.dma_start(x_sb[:], xT).then_inc(x_in, 16)
            sp.wait_ge(mod_sum1, MOD1)
            sp.wait_ge(prod_ok, MOD1)
            for dst, src in ((dl_st, dft_l), (dc_st, dft_c), (dx_st, dft_x)):
                sp.dma_start(dst[:], src).then_inc(dft_in, 16)
            for r in range(2):
                sp.dma_start(mod_ring[:, r, :], wmod[MOD1 + r]).then_inc(mod2_in[r], 16)
            with sp.Fori(0, NG) as g:
                for r in range(2):
                    sp.wait_ge(w_split, 2 * g + r + 1)
                    sp.dma_start(raw[:, r, :], wunits[2 * g + r + 2]).then_inc(raw_in[r], 16)
                for q in range(2):
                    for r in range(2):
                        sp.wait_ge(mod_sum1, 4 * g + 2 * q + r + MOD1 + 1)
                        sp.dma_start(mod_ring[:, r, :], wmod[4 * g + 2 * q + r + MOD1 + 2]).then_inc(mod2_in[r], 16)
            with sp.Fori(0, KD - 1) as j:
                for r in range(2):
                    sp.wait_ge(w_split, 2 * j + r + U_B + 1)
                    sp.dma_start(raw[:, r, :], wunits[2 * j + r + U_B + 2]).then_inc(raw_in[r], 16)
                for r in range(2):
                    sp.wait_ge(mod_sum1, 2 * j + r + MOD1 + 4 * NG + 1)
                    sp.dma_start(mod_ring[:, r, :], wmod[2 * j + r + MOD1 + 4 * NG + 2]).then_inc(mod2_in[r], 16)
            for r in range(2):
                sp.wait_ge(w_split, U_HEAD + r - 1)
                sp.dma_start(raw[:, r, :], wunits[U_HEAD + r]).then_inc(raw_in[r], 16)
            with sp.Fori(0, H) as h:
                for r in range(HU):
                    if r == 2:
                        sp.wait_ge(c_ok, h + 1)
                        sp.wait_ge(em_ok, 2)
                        sp.wait_ge(m_stored, 32)
                        sp.wait_ge(z_stored, 16 * (KD + 1))
                        sp.dma_start(c_raw[:], stateC[h]).then_inc(c_in, 16)
                    sp.wait_ge(w_split, U_HEAD + HU * h + r + 1)
                    sp.dma_start(raw[:, r % 2, :], wunits[U_HEAD + HU * h + r + 2]).then_inc(raw_in[r % 2], 16)
            for r in range(2):
                sp.wait_ge(w_split, U_GA + r + 1)
                sp.dma_start(raw[:, r, :], wunits[U_GA + r + 2]).then_inc(raw_in[r], 16)
            sp.wait_ge(yg_stored, 16 * (H * TT + 1))
            for r in range(2):
                sp.wait_ge(st_stored[r], 16 * (2 * H + 1))
            sp.wait_ge(nn_stored, 16 * (H + 1))
            yg_tiles = yg_dram.rearrange("h v p t -> (h v) p t")
            with sp.Fori(0, H * KV // 8) as i:
                for q in range(2):
                    for r in range(4):
                        sp.wait_ge(ygs_ok, 8 * i + 4 * q + r + 1)
                        sp.dma_start(yg_st[:, r, :], yg_tiles[8 * i + 4 * q + r]).then_inc(ygs_in[r], 16)
                    sp.wait_ge(w_split, U_GA + 2 * i + q + 3)
                    sp.dma_start(raw[:, q, :], wunits[U_GA + 2 * i + q + 4]).then_inc(raw_in[q], 16)
            for r in range(2):
                sp.wait_ge(w_split, U_MIX + r - 1)
                sp.dma_start(raw[:, r, :], wunits[U_MIX + r]).then_inc(raw_in[r], 16)
            with sp.Fori(0, KD // 2) as i:
                for r in range(2):
                    sp.wait_ge(m_ok, 2 * i + r + 1)
                    sp.dma_start(z_st[:, r, :], z_dram[2 * i + r]).then_inc(z_in[r], 16)
                    for q in range(2):
                        sp.wait_ge(w_split, U_MIX + 4 * i + 2 * r + q + 1)
                        sp.dma_start(raw[:, q, :], wunits[U_MIX + 2 + 4 * i + 2 * r + q]).then_inc(raw_in[q], 16)
            sp.wait_ge(units_done, U_OUT)
            for n, part in enumerate((slice(0, 2), slice(2, KD))):
                sp.dma_start(r_all[:, part, :], xT[:, part, :]).then_inc(xs_in[n], 16)
            with sp.Fori(0, KD // 2) as i:
                for r in range(2):
                    sp.wait_ge(w_split, U_OUT + 2 * i + r + 1)
                    sp.dma_start(raw[:, r, :], wunits[U_OUT + 2 + 2 * i + r]).then_inc(raw_in[r], 16)
            for r in range(2):
                sp.wait_ge(w_split, U_FF1 + r + 1)
                sp.dma_start(raw[:, r, :], wunits[U_FF1 + 2 + r]).then_inc(raw_in[r], 16)
            sp.wait_ge(x1_ok, KD)
            sp.dma_start(x1_dram, r_all[:]).then_inc(x1_stored, 16)
            with sp.Fori(2, KF) as i:
                for r in range(2):
                    sp.wait_ge(w_split, U_FF1 + 2 * i + r - 1)
                    sp.dma_start(raw[:, r, :], wunits[U_FF1 + 2 * i + r]).then_inc(raw_in[r], 16)

            def last_units(i, qs):
                for q in qs:
                    u, w = U_FF2 + 2 * len(FQ) * i + q, FQ[q % len(FQ)] * P
                    sp.wait_ge(w_split, u - 1)
                    sp.dma_start(raw[:, q % 2, 0:w], wunits[u][:, 0:w]).then_inc(raw_in[q % 2], 16)

            last_units(0, range(2))
            sp.wait_ge(units_done, U_FF2)
            sp.wait_ge(x1_stored, 16)
            sp.dma_start(x2_all[:, 0:2, :], x1_dram[:, 0:2, :]).then_inc(x1s_in[0], 16)
            last_units(0, range(2, 4))
            sp.dma_start(x2_all[:, 2:KD, :], x1_dram[:, 2:KD, :]).then_inc(x1s_in[1], 16)
            sp.dma_start(ln_row[:], ln_rows).then_inc(lnr_in, 16)
            last_units(0, range(4, 6))
            with sp.Fori(1, KD // 2) as i:
                last_units(i, range(2 * len(FQ)))
            for tt in range(TT):
                sp.wait_ge(*((y_ok_p, tt // 2 + 1) if tt in (0, 2) else (y_ok, {1: 1, 3: 2, 4: 3}[tt])))
                dst = y_prompt if tt == 0 else y_sample[(tt - 1) * P:tt * P, :]
                sp.dma_start(dst, rows2[:, tt, :]).then_inc(y_stored, 16)
            sp.wait_ge(y_stored, 16 * TT)
            sp.wait_ge(m_stored, 32)

        @block.gpsimd
        def _(pool):
            def split(u, slot, first, combine=False, width=UW, n_in=None):
                src, hi, lo = (t[:, slot, 0:width] for t in (raw, w_hi, w_lo))
                pool.wait_ge(raw_in[slot], n_in)
                if not first:
                    pool.wait_ge(units_done, u - 1)
                if combine:
                    half = UW // 2
                    pool.tensor_tensor(wb_sum[:, 0:half], src[:, 0:half], src[:, half:UW], ALU.add)
                    pool.tensor_tensor(wb_sum[:, half:UW], src[:, half:UW], src[:, 0:half], ALU.subtract)\
                        .then_inc(w_half, 1)
                return src, hi, lo

            def rounded(src, hi):
                pool.tensor_tensor(hi, src, zero[:, 0:1].broadcast_to([P, src.shape[1]]), ALU.add)\
                    .then_inc(w_half, 1)

            def rest(src, hi, lo):
                pool.tensor_tensor(lo, src, hi.bitcast(F32), ALU.subtract).then_inc(w_split, 1)

            pool.memset(zero[:], 0.0).then_inc(zero_ok, 1)
            pool.wait_ge(zero_ok, 1)
            for u in range(2):
                for k in range(1, KD):
                    acc = (mod_sum, sum_first)[u][:, 0, UW // 2:]
                    pool.wait_ge(prod_ok, KD * u + k + 1)
                    if u or k > 1:
                        pool.wait_ge(mod_sum_p, (KD - 1) * u + k - 1)
                    pool.tensor_tensor(acc, acc, prod[:, k % 4, :], ALU.add).then_inc(mod_sum_p, 1)
                src, hi, lo = split(u, u, True, n_in=16)
                rounded(src, hi)
                pool.wait_ge(w_half, u + 1)
                rest(src, hi, lo)
            def units_f(i):
                for r in range(2):
                    src, hi, lo = split(2 * i + r, r, False, n_in=16 * i + 16)
                    rounded(src, hi)
                    pool.wait_ge(w_half, 2 * i + r + 1)
                    rest(src, hi, lo)

            units_f(1)
            pool.wait_ge(dft_hi_ok, 3)
            pool.tensor_tensor(dl_lo[:].rearrange("p a b c -> p (a b c)"), dl_st[:],
                               dl_hi[:].rearrange("p a b c -> p (a b c)").bitcast(F32), ALU.subtract)\
                .then_inc(dl_ok, 1)
            pool.wait_ge(gate_act, 1)
            pool.tensor_tensor(gw_lo[:], gate_w[:], gw_hi[:].bitcast(F32), ALU.subtract).then_inc(gates_ok, 1)
            with pool.Fori(2, NG) as i:
                units_f(i)
            pool.wait_ge(gates_ok, 1)
            with pool.Fori(0, KD) as j:
                src, hi, lo = split(U_B + 2 * j, 0, False, n_in=16 * j + 16 * (NG + 1))
                rounded(src, hi)
                pool.wait_ge(w_half, U_B + 3 * j + 1)
                rest(src, hi, lo)
                src, hi, lo = split(U_B + 2 * j + 1, 1, False, True, n_in=16 * j + 16 * (NG + 1))
                pool.wait_ge(w_half, U_B + 3 * j + 2)
                rounded(wb_sum[:], hi)
                pool.wait_ge(w_half, U_B + 3 * j + 3)
                rest(wb_sum[:], hi, lo)
            half0 = U_HEAD + KD

            def pair(i):
                for r in range(2):
                    src, hi, lo = split(U_HEAD + 2 * i + r, r, False, n_in=16 * i + 16 * (U_HEAD // 2 + 1))
                    rounded(src, hi)
                    pool.wait_ge(w_half, half0 + 2 * i + r + 1)
                    rest(src, hi, lo)

            before_norm = (U_FF1 + 2 - U_HEAD) // 2
            with pool.Fori(0, before_norm) as i:
                pair(i)
            pool.wait_ge(mu_ok, 1)
            for j in range(1, KD, 2):
                pool.tensor_tensor(r_all[:, j, :], r_all[:, j, :], mu[:], ALU.subtract).then_inc(centred, 1)
            for j in range(KD):
                pool.wait_ge(h2f_ok, j + 1)
                pool.tensor_scalar(r_all[:, j, :], r_all[:, j, :], aln[:, 0, j:j + 1], aln[:, 1, j:j + 1],
                                   ALU.mult, ALU.add).then_inc(x1_ok, 1)
            with pool.Fori(before_norm, (U_FF2 - U_HEAD) // 2) as i:
                pair(i)
            half1 = half0 + U_FF2 - U_HEAD
            with pool.Fori(0, KD // 2) as i:
                for q in range(2 * len(FQ)):
                    n = 2 * len(FQ) * i + q
                    src, hi, lo = split(U_FF2 + n, q % 2, False, width=FQ[q % len(FQ)] * P,
                                        n_in=16 * len(FQ) * i + 16 * (U_FF2 // 2 + q // 2 + 1))
                    rounded(src, hi)
                    pool.wait_ge(w_half, half1 + n + 1)
                    rest(src, hi, lo)
            for n, tt in enumerate((0, 2)):
                pool.wait_ge(gain_ok, (1, 3)[n])
                pool.tensor_tensor(rows2[:, tt, :], rows2[:, tt, :], ln_row[:, 1, :], ALU.add).then_inc(y_ok_p, 1)

        @block.tensor
        def _(pe):
            mm = pe.matmul

            def block(out, slot, b, x_hi_, x_lo_, k, start, stop):
                cols = slice(b * P, (b + 1) * P)
                for n, (w, x) in enumerate(((w_hi, x_hi_), (w_hi, x_lo_), (w_lo, x_hi_))):
                    for a, z in ((0, CUT), (CUT, NT)):
                        ins = mm(out[:, a:z], w[:, slot, cols], x[:, k, a:z],
                                 start=(start and n == 0), stop=(stop and n == 2))
                return ins

            def unit_cols(out, u, slot, act_hi, act_lo, k0=0, last=True, first=True, nb=UB, k_ready=None):
                pe.wait_ge(w_split, u + 1)
                for b in range(nb):
                    if k_ready is not None:
                        pe.wait_ge(k_ready, b + 1)
                    ins = block(out, slot, b, act_hi, act_lo, k0 + b, first and b == 0, last and b == nb - 1)
                ins.then_inc(units_done, 1)

            def two_units(u, act_hi, act_lo, ready, given):
                pe.wait_ge(w_split, u + 2)
                for b in range(UB):
                    pe.wait_ge(ready, given + b + 1)
                    for p in range(2):
                        ins = block(joined(p), p, b, act_hi, act_lo, b, b == 0, b == UB - 1)
                        if b == UB - 1:
                            ins.then_inc(units_done, 1)

            def mod_chunk(c, acc):
                pe.wait_ge(mod_sum1, KD * c + KD)
                for m in range(KD):
                    for g in range(2):
                        ins = mm(psum[:, 7, bass.ds(2 * KD * c + (2 * m + g), 1)], acc[:, g, m * P:(m + 1) * P],
                                 ones_r[:, 0:1].bitcast(F32), start=True, stop=True)
                ins.then_inc(mod_done, 1)

            for p in range(2):
                pe.sem_inc(taken[p], 1)
            pe.wait_ge(once, 2)
            for c in range(2):
                pe.wait_ge(mod_sum_p, (KD - 1) * (c + 1))
                mod_chunk(c, (mod_sum, sum_first)[c])

            def group(g, odd):
                for p in range(2):
                    pe.wait_ge(taken[p], A_F + 2 * g + 1)
                    unit_cols(joined(p), U_PASS1 + 2 * g + p, p, h_hi, h_lo, k_ready=h_ok if p == 0 else None)
                pe.wait_ge(dft_ok, 2)
                for p in range(2):
                    if p == 1 and odd is not None:
                        mod_chunk(odd, mod_sum)
                    pe.wait_ge(taken[p], A_F + 2 * g + 2)
                for tt in range(TT):
                    if tt >= 3:
                        pe.wait_ge(xch_ok, 5 * g + tt - 2)
                    n = 0
                    for k in range(2):
                        for u, d in ((uf_hi, dx_hi), (uf_lo, dx_hi), (uf_hi, dx_lo)):
                            ins = mm(psum[:, 4 + tt % 3, 0:XW], u[:, k, tt * P:(tt + 1) * P], d[:, k, :],
                                     start=(n == 0), stop=(n == 5))
                            n += 1
                    ins.then_inc(xch_done, 1)
                pe.wait_ge(xch_ok, 5 * g + 5)
                pe.wait_ge(dl_ok, 1)
                for kind in range(2):
                    out = grids(kind)
                    cols = slice(kind * P, kind * P + P)
                    for span, tiles, dh, dl in ((slice(0, NC), range(1), dc_hi, dc_lo),
                                                (slice(NC, NT), range(1, TT), dl_hi, dl_lo)):
                        for t in tiles:
                            pos = (lambda d, c: d[:, c, :]) if t == 0 else (lambda d, c, t=t: d[:, c, t - 1, :])
                            jobs = [(x_hi, cols, pos(dh, kind)), (x_lo, cols, pos(dh, kind)),
                                    (x_hi, cols, pos(dl, kind))]
                            if kind == 1:
                                nyq = slice(2 * P, 2 * P + 2)
                                jobs += [(x_hi, nyq, pos(dh, 0)), (x_lo, nyq, pos(dh, 0)), (x_hi, nyq, pos(dl, 0))]
                            for n, (x, cc, d) in enumerate(jobs):
                                m = cc.stop - cc.start
                                ins = mm(out[0:m, span], x[:, t, cc], d,
                                         start=(t == tiles[0] and n == 0),
                                         stop=(t == tiles[-1] and n == len(jobs) - 1), skip_group_check=True)
                    ins.then_inc(pos_done, 1)

            with pe.Fori(0, NG // 2) as gg:
                group(2 * gg, None)
                group(2 * gg + 1, gg + 2)

            pe.wait_ge(gates_ok, 1)
            for k in range(KD):
                for n, (w, x) in enumerate(((gw_hi, h_hi), (gw_hi, h_lo), (gw_lo, h_hi))):
                    for half in range(2):
                        ins = mm(psum[:, 5 + half, 0:NT // 2], w[:, k * P:(k + 1) * P],
                                 x[:, k, half * NT // 2:(half + 1) * NT // 2],
                                 start=(k == 0 and n == 0), stop=(k == KD - 1 and n == 2))
            ins.then_inc(gate_acc, 1)

            with pe.Fori(0, 2) as jj:
                for jr in range(KD // 2):
                    j = jj * (KD // 2) + jr
                    pe.wait_ge(taken[0], A_B + j + 1)
                    unit_cols(joined(0), U_B + 2 * j, 0, h_hi, h_lo)
                    pe.wait_ge(taken[1], A_B + j + 1)
                    unit_cols(joined(1), U_B + 2 * j + 1, 1, ft_hi, ft_lo)
                mod_chunk(jj + 4, mod_sum)

            pe.wait_ge(gates_ok, 2)
            for tt in range(TT):
                ins = pe.transpose(flat[:, 5 * 512 + tt * P:5 * 512 + (tt + 1) * P],
                                   em_rows[:, tt * P:(tt + 1) * P], ident)
            ins.then_inc(em_acc, 1)

            def turn(h, u):
                pe.wait_ge(hn_ok, 5 * h + u + 1)
                if u >= 1:
                    pe.wait_ge(yg_ok, 5 * h + u + 1)
                for v in range(KV):
                    ins = pe.transpose(psum[:, 7, v * P:(v + 1) * P], hn_sb[:, v * P:(v + 1) * P], ident)
                ins.then_inc(t_done, 1)

            def final_states(h, A):
                pe.wait_ge(kw_ok, h + 1)
                for v in range(KV + 1):
                    p, tile = v % 2, 1 + v // 2
                    pe.wait_ge(taken[p], A + tile + 1)
                    if v < KV:
                        cc = slice(v * P, (v + 1) * P)
                        jobs = [(v_hi[:, 0, cc], kw_hi), (v_lo[:, 0, cc], kw_hi), (v_hi[:, 0, cc], kw_lo)]
                    else:
                        jobs = [(ones_r[:, :], kw_hi), (ones_r[:, :], kw_lo)]
                    for n, (a, b) in enumerate(jobs):
                        ins = mm(psum[:, 2 * p, :], a, b[:, :, :].rearrange("p a b -> p (a b)"),
                                 start=(n == 0), stop=(n == len(jobs) - 1))
                    ins.then_inc(st_done, 1)

            def head(h, tail):
                U = U_HEAD + HU * h
                A = A_HEAD + HA * h

                def project(pair, tile, unit, slot):
                    pe.wait_ge(taken[pair], A + tile + 1)
                    unit_cols(joined(pair), U + unit, slot, h_hi, h_lo)

                def scores(u):
                    if u == 0:
                        pe.wait_ge(v_ok, 5 * h + 2)
                    else:
                        pe.wait_ge(s_free, 5 * h + u)
                    srcs = range(LT) if u < LT else range(1)
                    tq = wlat(u) if u < LT else slice(0, NC)
                    for s in srcs:
                        sk = wlat(s) if u < LT else slice(0, NC)
                        n = 0
                        for d in range(KQ):
                            for a, b in ((k_hi, q_hi), (k_hi, q_lo), (k_lo, q_hi)):
                                ins = mm(psum[:, 4, s * P:(s + 1) * P], a[:, d, sk], b[:, d, tq],
                                         start=(n == 0), stop=(n == 3 * KQ - 1))
                                n += 1
                    ins.then_inc(s_done, 1)

                def numer(u):
                    buf = u % 2
                    if u == 0:
                        pe.wait_ge(v_ok, 5 * h + 5)
                        pe.wait_ge(c_ok, h + 2)
                    else:
                        pe.wait_ge(num_free, 5 * h + u)
                    if u < 2:
                        pe.wait_ge(taken[1 - u], A + 6 + 2 * u)
                    pe.wait_ge(p_ok, 5 * h + u + 1)
                    blocks = [list(range(u + 1)), list(range(u, LT))] if u < LT else [[0], [0]]
                    starts = [0, u + 1] if u < LT else [0, 1]
                    for part in range(2):
                        for d in range(2):
                            jobs = []
                            for n, s in enumerate(blocks[d]):
                                pos = starts[d] + n
                                hi, lo = p_hi[:, buf, pos, :], p_lo[:, buf, pos, :]
                                if part == 0:
                                    jobs += [(hi, ones_r[:, 0:2]), (lo, ones_r[:, 0:2])]
                                else:
                                    vt = s + 1 if u < LT else 0
                                    jobs += [(hi, v_hi[:, vt, :]), (lo, v_hi[:, vt, :]), (hi, v_lo[:, vt, :])]
                            if u < LT:
                                for k in range(KQ):
                                    hi, lo = qi_hi[:, buf, d, k, :], qi_lo[:, buf, d, k, :]
                                    a, b = ((n0_hi[:, h, d, k, :], n0_lo[:, h, d, k, :]) if part == 0
                                            else (c_hi[:, d, k, :], c_lo[:, d, k, :]))
                                    jobs += [(hi, a), (lo, a), (hi, b)]
                            out = den_at(u)[:, 2 * d:2 * d + 2] if part == 0 else psum[:, 5 + d, :]
                            for n, (a, b) in enumerate(jobs):
                                ins = mm(out, a, b, start=(n == 0), stop=(n == len(jobs) - 1))
                        ins.then_inc(num_done if part else den_done, 1)

                project(0, 0, 0, 0)
                if tail:
                    turn(h - 1, 3)
                    pe.wait_ge(den_read, 5 * h)
                project(1, 0, 1, 1)
                if tail:
                    turn(h - 1, 4)
                    final_states(h - 1, A)
                else:
                    for p in range(2):
                        pe.wait_ge(taken[p], A + 2)
                        pe.sem_inc(taken[p], 3 - p)
                project(0, 4, 2, 0)
                pe.wait_ge(rh_ok, h + 1)
                pe.wait_ge(em_ok, 1)
                pe.wait_ge(yg_ok, 5 * h + 1)
                for d, s in enumerate((sel_f, sel_b)):
                    dst = joined(2 + d)
                    mm(dst[:, 0:CUT], s[0:64, :], r_head[0:64, 0:CUT], start=True, stop=True)
                    mm(dst[:, CUT:NT], s[0:64, :], r_head[0:64, CUT:NT], start=True, stop=True).then_inc(r_done, 1)
                project(1, 3, 3, 1)
                pe.wait_ge(taken[0], A + 6)
                pe.wait_ge(r_ok, 2 * h + 2)
                v_banks = [0, 4, 5, 6, 7]
                for q in range(4):
                    pe.wait_ge(w_split, U + 4 + q + 1)
                    for kk in range(2):
                        k = 2 * q + kk
                        cols = slice(kk * DV, (kk + 1) * DV)
                        for tt in range(TT):
                            for n, (x, w) in enumerate(((h_hi, w_hi), (h_lo, w_hi), (h_hi, w_lo))):
                                ins = mm(psum[:, v_banks[tt], :], x[:, k, tt * P:(tt + 1) * P],
                                         w[:, q % 2, cols], start=(k == 0 and n == 0),
                                         stop=(k == KD - 1 and n == 2))
                    ins.then_inc(units_done, 1)
                project(1, 4, 8, 0)
                scores(0)
                pe.wait_ge(v_ok, 5 * h + 1)
                project(0, 5, 9, 1)
                scores(1)
                numer(0)
                project(0, 6, 10, 0)
                scores(2)
                numer(1)
                turn(h, 0)
                project(1, 5, 11, 1)
                pe.wait_ge(taken[1], A + 7)
                for k in range(KQ):
                    ins = pe.transpose(psum[:, 2, k * P:(k + 1) * P], k_c[:, k, :], ident)
                ins.then_inc(kt_done, 1)
                scores(3)
                numer(2)
                scores(4)
                turn(h, 1)
                numer(3)
                turn(h, 2)
                numer(4)

            head(0, False)
            with pe.Fori(1, H) as h:
                head(h, True)

            pe.wait_ge(taken[0], A_GA + 1)
            unit_cols(joined(0), U_GA, 0, h_hi, h_lo)
            turn(H - 1, 3)
            pe.wait_ge(den_read, 5 * H)
            pe.wait_ge(taken[1], A_GA + 1)
            unit_cols(joined(1), U_GA + 1, 1, h_hi, h_lo)
            turn(H - 1, 4)
            final_states(H - 1, A_GA)
            with pe.Fori(1, KD // 2) as i:
                for p in range(2):
                    pe.wait_ge(taken[p], A_GA + i + (4 - p))
                    unit_cols(joined(p), U_GA + 2 * i + p, p, h_hi, h_lo)
            pe.wait_ge(taken[1], A_MIX)
            pe.sem_inc(taken[1], 1)

            with pe.Fori(0, KD // 2) as i:
                for p in range(2):
                    pe.wait_ge(taken[p], A_MIX + i + 1)
                    for q in range(2):
                        u = U_MIX + 4 * i + 2 * p + q
                        pe.wait_ge(ygs_ok, 4 + 8 * q + 8)
                        unit_cols(joined(p), u, q, yg_hi, yg_lo, k0=8 * q, first=(q == 0), last=(q == 1))

            def column_sums(p, start, stop):
                for out, parts in ((joined(2), (r_hi, r_lo)), (joined(3), (sq_hi, sq_lo))):
                    for n, x in enumerate(parts):
                        for a, z in ((0, CUT), (CUT, NT)):
                            ins = mm(out[:, a:z], ones_r[:], x[:, p, a:z], start=(start and n == 0),
                                     stop=(stop and n == 1))
                ins.then_inc(stats_done, 1)

            for p in range(2):
                pe.sem_inc(stats_done, 1)
                pe.wait_ge(taken[p], A_OUT + 1)
            two_units(U_OUT, mg_hi, mg_lo, m_ok, 2)
            pe.wait_ge(st_in, 1)
            column_sums(0, True, False)
            with pe.Fori(1, KD // 2) as i:
                for p in range(2):
                    pe.wait_ge(taken[p], A_OUT + i + 1)
                    unit_cols(joined(p), U_OUT + 2 * i + p, p, mg_hi, mg_lo)
                    pe.wait_ge(st_in, 2 * i + p)
                    column_sums(1 - p, False, False)
            pe.wait_ge(st_in, KD)
            column_sums(1, False, True)

            for p in range(2):
                pe.wait_ge(taken[p], A_FF1 + 1)
            two_units(U_FF1, h2_hi, h2_lo, h2_ok, 0)
            with pe.Fori(1, KF) as i:
                for p in range(2):
                    pe.wait_ge(taken[p], A_FF1 + i + 1)
                    unit_cols(joined(p), U_FF1 + 2 * i + p, p, h2_hi, h2_lo)
            pe.wait_ge(f_ok, KF + 1)

            def last_tile(i, p):
                pe.wait_ge(taken[p], A_FF2 + i + 1)
                for q, nb in enumerate(FQ):
                    unit_cols(joined(p), U_FF2 + 2 * len(FQ) * i + (len(FQ) * p + q), (p + q) % 2, f_hi, f_lo,
                              k0=UB * q, nb=nb, first=(q == 0), last=(q == 2))

            def to_rows(i, p):
                pe.wait_ge(taken[p], A_FF2 + i + 2)
                pe.wait_ge(rows2_ok, 2 * i + p + 1)
                for tt in range(TT):
                    a = (4 + 2 * p) * 512 + tt * P
                    ins = pe.transpose(flat[:, a:a + P], r2_t[:, p, tt * P:(tt + 1) * P], ident)
                ins.then_inc(rt2_done, 1)

            last_tile(0, 0)
            last_tile(0, 1)
            to_rows(0, 0)
            with pe.Fori(1, KD // 2) as i:
                last_tile(i, 0)
                to_rows(i - 1, 1)
                last_tile(i, 1)
                to_rows(i, 0)
            to_rows(KD // 2 - 1, 1)

        @block.scalar
        def _(act):
            A_ = act.activation
            act.sem_inc(z_stored, 16)
            for r in range(2):
                act.sem_inc(st_stored[r], 16)
                act.sem_inc(rows2_ok, 1)
            act.sem_inc(nn_stored, 16)
            act.sem_inc(yg_stored, 16)
            act.dma_start(c_sb[:], cT).then_inc(c_sb_in, 16)
            act.dma_start(const_sb[:], consts).then_inc(const_in, 16)
            act.wait_ge(c_sb_in, 16)
            A_(c_silu[:], c_sb[:], ACT.Silu).then_inc(once, 1)
            act.wait_ge(once, 1)
            for n in range(MOD1):
                if n == 2:
                    act.wait_ge(const_in, 16)
                    A_(ones_r[:], ident, ACT.Identity, bias=1.0, scale=0.0).then_inc(once, 1)
                c, k = divmod(n, KD)
                act.wait_ge(mod_in[k], 16 * (c + 1))
                if n > 4 and (n - 4) % KD:
                    act.wait_ge(mod_sum_p, (KD - 1) * ((n - 4) // KD) + (n - 4) % KD)
                dst = (mod_sum, sum_first)[c][:, 0, UW // 2:] if k == 0 else prod[:, k % 4, :]
                A_(dst, mod_first[:, k, UW // 2:], ACT.Copy, scale=c_silu[:, k, 0:1]).then_inc(prod_ok, 1)
            act.dma_start(gate_w[:], wgate).then_inc(gw_in, 16)
            act.wait_ge(small_in, 16 * 7)
            A_(n0_hi[:], n0_sb[:], ACT.Copy).then_inc(once, 1)
            act.wait_ge(mod_ready, 1)
            act.wait_ge(x_in, 16)
            for k in range(KD):
                A_(x_sb[:, k, 0:NC], x_sb[:, k, 0:NC], ACT.Identity, scale=mod_sb[:, KD + k, 0:1],
                   bias=mod_sb[:, k, 0:1]).then_inc(x_mod_c, 1)
                act.wait_ge(x_mod_c, k + 1)
                act.wait_ge(x_mod, k + 1)
                A_(h_hi[:, k, :], x_sb[:, k, :], ACT.Copy).then_inc(h_hi_ok, 1)
            act.wait_ge(dft_in, 48)
            for hi, st in ((dx_hi[:].rearrange("p a b -> p (a b)"), dx_st),
                           (dc_hi[:].rearrange("p a b -> p (a b)"), dc_st),
                           (dl_hi[:].rearrange("p a b c -> p (a b c)"), dl_st)):
                A_(hi, st[:], ACT.Copy).then_inc(dft_hi_ok, 1)
            act.wait_ge(gw_in, 16)
            A_(gw_hi[:], gate_w[:], ACT.Copy).then_inc(gate_act, 1)

            with act.Fori(0, NG) as g:
                for p in range(2):
                    act.wait_ge(units_done, U_PASS1 + 2 * g + p + 1)
                    A_(uf_hi[:, p, :], joined(p), ACT.Copy).then_inc(uf_hi_ok, 1)
                for tt in range(TT):
                    act.wait_ge(xch_done, 5 * g + tt + 1)
                    A_(x_hi[:, tt, :], psum[:, 4 + tt % 3, 0:XW], ACT.Copy).then_inc(xch_hi_ok, 1)
                for kind in range(2):
                    act.wait_ge(pos_done, 2 * g + kind + 1)
                    A_(ft_hi[:, NG * kind + g, :], grids(kind), ACT.Copy).then_inc(ft_hi_ok, 1)

            act.wait_ge(gate_acc, 1)
            A_(two(gt[:]), psum[:, 5:7, 0:NT // 2], ACT.Identity, bias=gbias[:, 0:1]).then_inc(gate_act, 1)
            act.wait_ge(gate_act, 2)
            A_(gt_e[:], gt[:], ACT.Abs).then_inc(gate_act, 1)
            act.wait_ge(gate_act, 3)
            A_(gt_e[:], gt_e[:], ACT.Exp, scale=-1.0).then_inc(gate_act, 1)
            act.wait_ge(gate_act, 4)
            A_(gt_e[:], gt_e[:], ACT.Ln, bias=1.0).then_inc(gate_act, 1)
            with act.Fori(0, KD) as j:
                act.wait_ge(units_done, U_B + 2 * j + 1)
                A_(gb_sb[:], joined(0), ACT.Sigmoid).then_inc(taken[0], 1)
                act.wait_ge(taken[1], A_B + j + 2)
                act.dma_start(z_dram[j], z_sb[:]).then_inc(z_stored, 16)
            act.wait_ge(gates_ok, 2)
            act.dma_start(new_m[0], em_rows[64:64 + H, NC - 1:NC]).then_inc(m_stored, 16)
            act.dma_start(new_m[1], em_rows[96:96 + H, 0:1]).then_inc(m_stored, 16)
            act.wait_ge(em_acc, 1)
            em_flat = em_t[:].rearrange("p t g c -> p (t g c)")
            A_(em_flat, flat[:, 5 * 512:5 * 512 + NT], ACT.Copy).then_inc(em_ok, 1)
            act.wait_ge(em_ok, 1)
            A_(enm_t[:], em_t[:, :, 2:4, :], ACT.Exp, scale=-1.0).then_inc(em_ok, 1)

            act.wait_ge(m_stored, 32)
            act.wait_ge(z_stored, 16 * (KD + 1))
            def turned(h, u):
                tok = wlat(u) if u < LT else slice(0, NC)
                act.wait_ge(yg_ok, 5 * h + u + 2)
                act.dma_start(yg_dram[h, :, :, tok].rearrange("v p t -> p v t"), yg_sb[:]).then_inc(yg_stored, 16)

            def forward(h, u):
                act.wait_ge(rec_ok, 5 * h + u + 1)
                act.wait_ge(num_done, 5 * h + u + 1)
                A_(h_sb[:], psum[:, 5, :], ACT.Copy, scale=rec[:, 0:1]).then_inc(hf_ok, 1)

            def final_states(h, A):
                for v in range(KV + 1):
                    p, tile = v % 2, 1 + v // 2
                    if v < KV:
                        if p == 0:
                            act.wait_ge(st_done, 5 * h + v + 1)
                            act.wait_ge(st_stored[p], 32 * h + 16 * (v // 2) + 16)
                            A_(st_sb[:, p, :], psum[:, 2 * p, :], ACT.Copy).then_inc(taken[p], 1)
                        act.wait_ge(taken[p], A + tile + 2)
                        act.dma_start(new_C[:, h, v * P:(v + 1) * P, :].rearrange("a p d -> p a d"),
                                      st_sb[:, p, :].rearrange("p (a d) -> p a d", a=2)).then_inc(st_stored[p], 16)
                    else:
                        act.wait_ge(st_done, 5 * h + v + 1)
                        act.wait_ge(nn_stored, 16 * h + 16)
                        A_(nn_sb[:], psum[0:1, 2 * p, :], ACT.Copy).then_inc(taken[p], 1)
                        act.wait_ge(taken[p], A + tile + 2)
                        act.dma_start(new_n[:, h, :].unsqueeze(0),
                                      nn_sb[:, :].rearrange("p (a d) -> p a d", a=2)).then_inc(nn_stored, 16)

            def head(h, tail):
                U = U_HEAD + HU * h
                A = A_HEAD + HA * h

                def gate(v):
                    pair = O_PAIR[v]
                    act.wait_ge(units_done, U + 8 + v + 1)
                    A_(og[:, v, :], joined(pair), ACT.Tanh, scale=0.5).then_inc(taken[pair], 1)

                def weights(u):
                    act.wait_ge(diag_ok, 5 * h + u + 1)
                    w, inter = w_sb[:, u % 2], i_sb[:, u % 2]
                    if u == LT:
                        A_(w[:, 0:2, :], w[:, 0:2, :], ACT.Exp).then_inc(e_ok, 1)
                        return
                    A_(w[:, u:u + 2, :], w[:, u:u + 2, :], ACT.Exp)
                    for s in range(u):
                        A_(w[:, s, :], r_sb[:, 0, wlat(u)], ACT.Exp, bias=em_t[:, 1 + s, 0, bass.ds(h, 1)])
                    for s in range(u + 1, LT):
                        A_(w[:, s + 1, :], r_sb[:, 1, wlat(u)], ACT.Exp, bias=em_t[:, 1 + s, 1, bass.ds(h, 1)])
                    for d in range(2):
                        ins = A_(inter[:, d, :], r_sb[:, d, wlat(u)], ACT.Exp, bias=m0b[:, d, bass.ds(h, 1)])
                    ins.then_inc(e_ok, 1)

                def p_round(u):
                    act.wait_ge(p_f_ok, 5 * h + u + 1)
                    if u >= 2:
                        act.wait_ge(num_done, 5 * h + u - 1)
                    if u < LT:
                        A_(p_hi[:, u % 2, :, :], w_sb[:, u % 2, :, :], ACT.Copy)
                        A_(qi_hi[:, u % 2, :, :, :], qi_f[:], ACT.Copy).then_inc(p_hi_ok, 1)
                    else:
                        A_(p_hi[:, u % 2, 0:2, :], w_sb[:, u % 2, 0:2, :], ACT.Copy).then_inc(p_hi_ok, 1)

                def qk(n, dst, scale):
                    act.wait_ge(units_done, U + n + 1)
                    A_(dst[:, n % 2, :], joined(n % 2), ACT.Copy, scale=scale).then_inc(qk_hi_ok, 1)

                if tail:
                    forward(h - 1, 4)
                qk(0, q_hi, 1.0)
                if tail:
                    turned(h - 1, 3)
                qk(1, q_hi, 1.0)
                if tail:
                    final_states(h - 1, A)
                    turned(h - 1, 4)
                qk(2, k_hi, QSCALE)
                for d in range(2):
                    act.wait_ge(r_done, 2 * h + d + 1)
                    A_(r_sb[:, d, :], joined(2 + d), ACT.Copy).then_inc(r_ok, 1)
                weights(0)
                weights(1)
                qk(3, k_hi, QSCALE)
                act.wait_ge(c_in, 16 * h + 16)
                A_(c_hi[:], c_raw[:], ACT.Copy).then_inc(c_hi_ok, 1)
                act.wait_ge(units_done, U + 8)
                for tt in range(TT):
                    A_(v_hi[:, tt, :], psum[:, (0, 4, 5, 6, 7)[tt], :], ACT.Copy).then_inc(v_hi_ok, 1)
                gate(0)
                p_round(0)
                gate(1)
                weights(2)
                p_round(1)
                forward(h, 0)
                weights(3)
                gate(2)
                p_round(2)
                forward(h, 1)
                weights(4)
                gate(3)
                turned(h, 0)
                p_round(3)
                forward(h, 2)
                turned(h, 1)
                p_round(4)
                act.wait_ge(taken[1], A + 8)
                A_(kw_hi[:], kw_f[:], ACT.Copy).then_inc(kw_hi_ok, 1)
                forward(h, 3)
                turned(h, 2)

            head(0, False)
            with act.Fori(1, H) as h:
                head(h, True)

            def gate_a(j, pair):
                act.wait_ge(units_done, j + (U_GA + 1))
                A_(ga_sb[:, j, :], joined(pair), ACT.Sigmoid).then_inc(taken[pair], 1)

            forward(H - 1, 4)
            gate_a(0, 0)
            turned(H - 1, 3)
            gate_a(1, 1)
            final_states(H - 1, A_GA)
            turned(H - 1, 4)
            with act.Fori(0, H * KV // 8) as i:
                for p in range(2):
                    gate_a(2 * i + 2 + p, p)
                    for r in range(4):
                        t = 8 * i + (4 * p + r)
                        act.wait_ge(ygs_in[r], 32 * i + 16 * (p + 1))
                        A_(yg_hi[:, t, :], yg_st[:, r, :], ACT.Copy,
                           scale=gain_h[:, bass.ds(t, 1)]).then_inc(ygs_hi_ok, 1)
            for p in range(2):
                gate_a(KD - 2 + p, p)
            with act.Fori(0, KD) as j:
                act.wait_ge(m_f_ok, j + 1)
                A_(mg_hi[:, j, :], m_sb[:], ACT.Copy).then_inc(m_hi_ok, 1)
            with act.Fori(0, KD // 2) as i:
                for p in range(2):
                    act.wait_ge(taken[p], A_OUT + i + 2)
                    act.wait_ge(stats_done, 2 * i + p + 1)
                    A_(r_hi[:, p, :], r_all[:, 2 * i + p, :], ACT.Copy).then_inc(r_split, 1)
                    A_(sq_f[:, p, :], r_all[:, 2 * i + p, :], ACT.Square).then_inc(sq_f_ok, 1)
                    act.wait_ge(sq_f_ok, 2 * i + p + 1)
                    A_(sq_hi[:, p, :], sq_f[:, p, :], ACT.Copy).then_inc(sq_split, 1)
            act.wait_ge(stats_done, 2 + KD)
            A_(mu[:], joined(2), ACT.Copy, scale=1.0 / DMODEL).then_inc(mu_ok, 1)
            A_(musq[:], joined(2), ACT.Square, scale=1.0 / DMODEL).then_inc(mu_ok, 1)
            act.wait_ge(var_b_ok, 1)
            A_(rstd_b[:], var_b[:], ACT.Sqrt, bias=eps_sb[:, 0:1]).then_inc(sd_b_ok, 1)
            for j in range(KD):
                act.wait_ge(t2_ok, j + 1)
                if j >= 2:
                    act.wait_ge(h2_ok, j - 1)
                A_(h2_f[:, j % 2, 0:NC], r_all[:, j, 0:NC], ACT.Identity, scale=h2_s[:, j, 0:1], bias=h2_b[:, j, 0:1])
                A_(h2_f[:, j % 2, NC:NT], r_all[:, j, NC:NT], ACT.Identity, scale=h2_s[:, j, 1:2],
                   bias=h2_b[:, j, 1:2]).then_inc(h2f_ok, 1)
                act.wait_ge(h2f_ok, j + 1)
                A_(h2_hi[:, j, :], h2_f[:, j % 2, :], ACT.Copy).then_inc(h2_hi_ok, 1)

            with act.Fori(0, KF) as i:
                act.wait_ge(units_done, U_FF1 + 2 * i + 1)
                A_(s_sb[:], joined(0), ACT.Silu).then_inc(taken[0], 1)
                act.wait_ge(taken[1], A_FF1 + i + 2)
                A_(f_hi[:, i, :], ff_sb[:], ACT.Copy).then_inc(f_hi_ok, 1)
            with act.Fori(0, KD // 2) as i:
                for p in range(2):
                    act.wait_ge(rt2_done, 2 * i + p + 1)
                    dst = rows2[:, :, :].rearrange("p t (j c) -> p t j c", c=P)[:, :, 2 * i + p, :]
                    a = (4 + 2 * p) * 512
                    A_(dst, flat[:, a:a + NT].rearrange("p (t c) -> p t c", c=P), ACT.Copy).then_inc(rows2_ok, 1)
            act.wait_ge(var2_ok, 1)
            A_(sd[:], sd[:], ACT.Sqrt).then_inc(sd2_ok, 1)
            act.wait_ge(norm_ok, 1)
            for tt in range(TT):
                A_(rows2[:, tt, :], rows2[:, tt, :], ACT.Identity, scale=rstd[:, tt:tt + 1],
                   bias=nmr[:, tt:tt + 1]).then_inc(norm_ok, 1)

        @block.vector
        def _(v):
            steps = [0]

            def own(ins, value=None):
                steps[0] += 1
                ins.then_inc(dve, 1)
                v.wait_ge(dve, steps[0] if value is None else value(steps[0]))

            def sub(out, a, b):
                return v.tensor_tensor(out, a, b.bitcast(F32), ALU.subtract)

            v.sem_inc(yg_ok, 1)
            v.sem_inc(c_ok, 1)
            v.sem_inc(f_ok, 1)
            for _i in range(2):
                v.sem_inc(m_ok, 1)
            for _i in range(4):
                v.sem_inc(ygs_ok, 1)
            def mod_add(n, k, ring, slot, acc, first):
                for g, done in enumerate((mod_sum0, mod_sum1)):
                    part = slice(0, UW // 2 if first and g == 0 else UW)
                    w, a, c = ring[:, slot, part], acc[:, g, part], c_silu[:, k, g:g + 1]
                    if not (first and n == 0):
                        v.wait_ge(done, n)
                    if k == 0:
                        v.tensor_scalar(a, w, c, None, ALU.mult).then_inc(done, 1)
                    else:
                        v.scalar_tensor_tensor(out=a, in0=w, scalar=c, in1=a, op0=ALU.mult, op1=ALU.add)\
                            .then_inc(done, 1)

            def mod_adds(c, ks):
                for k in ks:
                    v.wait_ge(mod2_in[k % 2], 64 * c + (16 * (k // 2 + 1) - 128))
                    if k == 0:
                        v.wait_ge(mod_done, c)
                    mod_add(KD * c + k, k, mod_ring, k % 2, mod_sum, False)

            v.wait_ge(once, 1)
            for n in range(MOD1):
                v.wait_ge(mod_in[n % KD], 16 * (n // KD + 1))
                mod_add(n, n % KD, mod_first, n % KD, (mod_sum, sum_first)[n // KD], True)
            v.wait_ge(small_in, 16 * 7)
            own(v.memset(eps_sb[:], EPS))
            own(v.tensor_scalar(gain_h[:], gain_sb[:], 0.5, None, ALU.mult))
            own(v.tensor_scalar(aln[:], ln_sb[:], ALPHA, None, ALU.mult))
            v.wait_ge(once, 3)
            sub(n0_lo[:], n0_sb[:], n0_hi[:]).then_inc(once_v, 1)
            v.wait_ge(mod_done, 2)
            ps_mod = psum[:, 7, 0:2 * NMOD].rearrange("p (m g) -> p m g", g=2)
            own(v.tensor_tensor(mod_sb[:, 0:MOD1, :], ps_mod[:, 0:MOD1, :], bmod_sb[:, 0:MOD1, :], ALU.add))
            v.tensor_scalar(mod_sb[:, KD:MOD1, :], mod_sb[:, KD:MOD1, :], 1.0, None, ALU.add).then_inc(mod_ready, 1)
            v.wait_ge(mod_ready, 1)
            v.wait_ge(x_in, 16)

            def h_rest(k):
                v.wait_ge(h_hi_ok, k + 1)
                sub(h_lo[:, k, :], x_sb[:, k, :], h_hi[:, k, :]).then_inc(h_ok, 1)

            for k in range(KD):
                v.tensor_scalar(x_sb[:, k, NC:NT], x_sb[:, k, NC:NT], mod_sb[:, KD + k, 1:2], mod_sb[:, k, 1:2],
                                ALU.mult, ALU.add).then_inc(x_mod, 1)
                if k >= 1:
                    h_rest(k - 1)
            h_rest(KD - 1)
            for n, (lo, hi, st) in enumerate(((dx_lo, dx_hi, dx_st), (dc_lo, dc_hi, dc_st))):
                v.wait_ge(dft_hi_ok, n + 1)
                sub(lo[:].rearrange("p a b -> p (a b)"), st[:], hi[:].rearrange("p a b -> p (a b)"))\
                    .then_inc(dft_ok, 1)

            def group(g):
                for p in range(2):
                    v.wait_ge(uf_hi_ok, 2 * g + p + 1)
                    sub(uf_lo[:, p, :], joined(p), uf_hi[:, p, :]).then_inc(taken[p], 1)
                for tt in range(TT):
                    v.wait_ge(xch_hi_ok, 5 * g + tt + 1)
                    sub(x_lo[:, tt, :], psum[:, 4 + tt % 3, 0:XW], x_hi[:, tt, :]).then_inc(xch_ok, 1)
                for kind in range(2):
                    v.wait_ge(ft_hi_ok, 2 * g + kind + 1)
                    sub(ft_lo[:, NG * kind + g, :], grids(kind), ft_hi[:, NG * kind + g, :])\
                        .then_inc(taken[kind], 1)

            with v.Fori(0, NG // 2) as gg:
                for odd in range(2):
                    mod_adds(gg + 2, range(4 * odd, 4 * odd + 4))
                    group(2 * gg + odd)

            own(v.memset(one4[:], 1.0))
            own(v.memset(r_rows[:], 0.0))
            own(v.memset(em_rows[:], 0.0))
            v.wait_ge(gate_act, 2)
            own(v.tensor_scalar(gt_m[:], gt[:], 0.0, None, ALU.min))
            v.wait_ge(gate_act, 5)
            own(v.tensor_tensor(gt_m[:], gt_m[:], gt_e[:], ALU.subtract))
            spans = (slice(0, NC), slice(NC, NT))
            backs = (slice(NC - 1, None, -1), slice(NT - 1, NC - 1, -1))
            for src, dst, row in ((gt, igs, 0), (gt_m, lfs, 64)):
                own(v.tensor_copy(dst[:, 0, :], src[row:row + H, :]))
                for s, b in zip(spans, backs):
                    own(v.tensor_copy(dst[:, 1, s], src[row + 32:row + 32 + H, b]))
            for d in range(2):
                for n, s in enumerate(spans):
                    own(v.tensor_tensor_scan(bs[:, d, s], one4[:, s], lfs[:, d, s], 0.0, ALU.mult, ALU.add))
                    own(v.tensor_tensor_scan(ms[:, d, s], lfs[:, d, s], igs[:, d, s],
                                             m0r[:, d:d + 1] if n else 0.0, ALU.add, ALU.max))
            own(v.tensor_tensor(r_rows[0:H, :], bs[:, 0, :], ms[:, 0, :], ALU.subtract))
            own(v.tensor_tensor(em_rows[0:H, :], igs[:, 0, :], bs[:, 0, :], ALU.subtract))
            own(v.tensor_copy(em_rows[64:64 + H, :], ms[:, 0, :]))
            for s, b in zip(spans, backs):
                own(v.tensor_tensor(r_rows[32:32 + H, s], bs[:, 1, b], ms[:, 1, b], ALU.subtract))
                own(v.tensor_tensor(em_rows[32:32 + H, s], igs[:, 1, b], bs[:, 1, b], ALU.subtract))
                if s is spans[0]:
                    own(v.tensor_copy(em_rows[96:96 + H, s], ms[:, 1, b]))
                else:
                    v.tensor_copy(em_rows[96:96 + H, s], ms[:, 1, b]).then_inc(gates_ok, 1)
            with v.Fori(0, 2) as jj:
                for jr in range(KD // 2):
                    j = jj * (KD // 2) + jr
                    mod_adds(jj + 4, range(2 * jr, 2 * jr + 2))
                    v.wait_ge(taken[0], A_B + j + 2)
                    v.wait_ge(units_done, U_B + 2 * j + 2)
                    v.wait_ge(z_stored, 16 * j + 16)
                    v.tensor_tensor(z_sb[:], joined(1), gb_sb[:], ALU.mult).then_inc(taken[1], 1)
            v.wait_ge(mod_done, 6)
            own(v.tensor_tensor(mod_sb[:, MOD1:NMOD, :], ps_mod[:, MOD1:NMOD, :], bmod_sb[:, MOD1:NMOD, :], ALU.add))
            own(v.tensor_scalar(mod_sb[:, 4 * KD:5 * KD, :], mod_sb[:, 4 * KD:5 * KD, :], 1.0, None, ALU.add))
            lg = ln_sb[:, 0, :].unsqueeze(2).broadcast_to([P, KD, 2])
            lb = ln_sb[:, 1, :].unsqueeze(2).broadcast_to([P, KD, 2])
            own(v.tensor_tensor(h2_s[:], mod_sb[:, 4 * KD:5 * KD, :], lg, ALU.mult))
            own(v.tensor_tensor(h2_b[:], mod_sb[:, 4 * KD:5 * KD, :], lb, ALU.mult))
            own(v.tensor_tensor(h2_b[:], h2_b[:], mod_sb[:, 3 * KD:4 * KD, :], ALU.add))

            base = steps[0]
            COMBINE = 15
            PER_HEAD = 2 + TT * COMBINE

            def combine(h, u, chain):
                tile = 1 + u if u < LT else 0
                v.wait_ge(den_done, 5 * h + u + 1)
                den = den_at(u).rearrange("p (a b) -> p a b", b=2)[:, :, 0]
                chain(v.scalar_tensor_tensor(out=den_sb[:], in0=den, scalar=-1.0, in1=enm_t[:, tile, :, h],
                                             op0=ALU.mult, op1=ALU.max))
                v.tensor_tensor(den_sb[:], den, den_sb[:], ALU.max).then_inc(den_read, 1)
                v.wait_ge(den_read, 5 * h + u + 1)
                v.reciprocal(rec[:], den_sb[:]).then_inc(rec_ok, 1)
                v.wait_ge(rec_ok, 5 * h + u + 1)
                v.wait_ge(hf_ok, 5 * h + u + 1)
                v.scalar_tensor_tensor(out=h_sb[:], in0=psum[:, 6, :], scalar=rec[:, 1:2], in1=h_sb[:],
                                       op0=ALU.mult, op1=ALU.add).then_inc(num_free, 1)
                v.wait_ge(num_free, 5 * h + u + 1)
                chain(v.bn_stats(stats[:], h_sb[:]))
                v.sem_inc(stats_seen, 1)
                chain(v.bn_aggr(mv[:, 0, :], stats[:]))
                chain(v.tensor_scalar(nt_v[:], mv[:, 0, 1:2], EPS, None, ALU.add))
                chain(v.tensor_scalar(nt_a[:].bitcast(I32), nt_v[:].bitcast(I32), 1, None,
                                      ALU.logical_shift_right))
                chain(v.tensor_scalar(nt_y[:].bitcast(I32), nt_a[:].bitcast(I32), -1.0, MAGIC,
                                      ALU.mult, ALU.add))
                for _n in range(3):
                    chain(v.scalar_tensor_tensor(out=nt_a[:], in0=nt_y[:], scalar=nt_v[:, 0:1], in1=nt_y[:],
                                                 op0=ALU.mult, op1=ALU.mult))
                    chain(v.tensor_scalar(nt_a[:], nt_a[:], -0.5, 1.5, ALU.mult, ALU.add))
                    chain(v.tensor_tensor(nt_y[:], nt_y[:], nt_a[:], ALU.mult))
                if u >= 1:
                    v.wait_ge(t_done, 5 * h + u)
                v.tensor_scalar(hn_sb[:], h_sb[:], mv[:, 0, 0:1], nt_y[:, 0:1], ALU.subtract, ALU.mult)\
                    .then_inc(hn_ok, 1)

            def gated(h, u):
                tok = wlat(u) if u < LT else slice(0, NC)
                v.wait_ge(t_done, 5 * h + u + 1)
                v.wait_ge(taken[0], A_HEAD + HA * h + 8)
                v.wait_ge(taken[1], A_HEAD + HA * h + 7)
                v.wait_ge(yg_stored, 80 * h + 16 * u + 16)
                v.scalar_tensor_tensor(out=yg_sb[:], in0=og[:, :, tok], scalar=1.0,
                                       in1=psum[:, 7, :].rearrange("p (v t) -> p v t", t=P),
                                       op0=ALU.add, op1=ALU.mult).then_inc(yg_ok, 1)

            def odd_state(h, tile):
                v.wait_ge(st_done, 5 * h + tile + 1)
                v.wait_ge(st_stored[1], 32 * h + 16 * (tile // 2) + 16)
                v.tensor_copy(st_sb[:, 1, :], psum[:, 2, :]).then_inc(taken[1], 1)

            def head(h, tail):
                U = U_HEAD + HU * h
                A = A_HEAD + HA * h
                steps[0] = base - (COMBINE if tail else 0)

                def chain(ins):
                    steps[0] += 1
                    ins.then_inc(dve, 1)
                    v.wait_ge(dve, h * PER_HEAD + steps[0])

                def diag(u):
                    if u == 0:
                        v.wait_ge(r_ok, 2 * h + 2)
                        v.wait_ge(em_ok, 2)
                    elif u >= 2:
                        v.wait_ge(p_ok, 5 * h + u - 1)
                    w = w_sb[:, u % 2]
                    pos, tile, tok = (u, 1 + u, wlat(u)) if u < LT else (0, 0, slice(0, NC))
                    v.scalar_tensor_tensor(out=w[:, pos, :], in0=r_sb[:, 0, tok],
                                           scalar=em_t[:, tile, 0, bass.ds(h, 1)], in1=mask_f,
                                           op0=ALU.add, op1=ALU.add)
                    v.scalar_tensor_tensor(out=w[:, pos + 1, :], in0=r_sb[:, 1, tok],
                                           scalar=em_t[:, tile, 1, bass.ds(h, 1)], in1=mask_b,
                                           op0=ALU.add, op1=ALU.add).then_inc(diag_ok, 1)

                def probs(u):
                    w = w_sb[:, u % 2]
                    v.wait_ge(e_ok, 5 * h + u + 1)
                    if u == LT:
                        chain(v.tensor_copy(wg[:, 0:1], w[:, 0, NC - 1:NC]))
                        chain(v.tensor_copy(wg[:, 1:2], w[:, 1, 0:1]))
                    v.wait_ge(s_done, 5 * h + u + 1)
                    if u < LT:
                        s4 = psum[:, 4, :].rearrange("p (s t) -> p s t", t=P)
                        v.tensor_tensor(w[:, 0:u + 1, :], w[:, 0:u + 1, :], s4[:, 0:u + 1, :], ALU.mult)
                        v.tensor_tensor(w[:, u + 1:, :], w[:, u + 1:, :], s4[:, u:, :], ALU.mult)\
                            .then_inc(s_free, 1)
                        for d in range(2):
                            ins = v.tensor_tensor(qi_f[:, d, :, :], q_f[:, :, u * P:(u + 1) * P],
                                                  i_sb[:, u % 2, d, :].unsqueeze(1).broadcast_to([P, KQ, P]), ALU.mult)
                        ins.then_inc(p_f_ok, 1)
                    else:
                        s1 = psum[:, 4, 0:P]
                        v.tensor_tensor(w[:, 0, :], w[:, 0, :], s1, ALU.mult)
                        v.tensor_tensor(w[:, 1, :], w[:, 1, :], s1, ALU.mult).then_inc(s_free, 1)
                        v.wait_ge(s_free, 5 * h + 5)
                        v.sem_inc(p_f_ok, 1)

                def p_rest(u):
                    v.wait_ge(p_hi_ok, 5 * h + u + 1)
                    if u < LT:
                        sub(p_lo[:, u % 2, :, :], w_sb[:, u % 2, :, :], p_hi[:, u % 2, :, :])
                        sub(qi_lo[:, u % 2, :, :, :], qi_f[:], qi_hi[:, u % 2, :, :, :]).then_inc(p_ok, 1)
                    else:
                        sub(p_lo[:, u % 2, 0:2, :], w_sb[:, u % 2, 0:2, :], p_hi[:, u % 2, 0:2, :]).then_inc(p_ok, 1)

                v.tensor_scalar(r_head[:], r_rows[:], onehot[:, bass.ds(h, 1)], None, ALU.mult).then_inc(rh_ok, 1)

                def qk_rest(n):
                    v.wait_ge(qk_hi_ok, 4 * h + n + 1)
                    src = joined(n % 2)
                    if n < 2:
                        v.tensor_copy(q_f[:, n, :], src[:, NC:NT])
                        sub(q_lo[:, n, :], src, q_hi[:, n, :]).then_inc(taken[n % 2], 1)
                    else:
                        v.tensor_scalar(k_c[:, n % 2, :], src[:, 0:NC], QSCALE, None, ALU.mult)
                        v.scalar_tensor_tensor(out=k_lo[:, n % 2, :], in0=src, scalar=QSCALE,
                                               in1=k_hi[:, n % 2, :].bitcast(F32), op0=ALU.mult,
                                               op1=ALU.subtract).then_inc(taken[n % 2], 1)

                if tail:
                    combine(h - 1, 4, chain)
                qk_rest(0)
                if tail:
                    gated(h - 1, 3)
                qk_rest(1)
                if tail:
                    gated(h - 1, 4)
                    odd_state(h - 1, 1)
                    odd_state(h - 1, 3)
                qk_rest(2)
                diag(0)
                diag(1)
                qk_rest(3)
                v.wait_ge(c_hi_ok, h + 1)
                sub(c_lo[:], c_raw[:], c_hi[:]).then_inc(c_ok, 1)
                for tt in range(TT):
                    v.wait_ge(v_hi_ok, 5 * h + tt + 1)
                    sub(v_lo[:, tt, :], psum[:, (0, 4, 5, 6, 7)[tt], :], v_hi[:, tt, :]).then_inc(v_ok, 1)
                probs(0)
                p_rest(0)
                diag(2)
                probs(1)
                p_rest(1)
                diag(3)
                combine(h, 0, chain)
                probs(2)
                p_rest(2)
                diag(4)
                combine(h, 1, chain)
                gated(h, 0)
                probs(3)
                p_rest(3)
                combine(h, 2, chain)
                gated(h, 1)
                probs(4)
                p_rest(4)
                v.wait_ge(kt_done, h + 1)
                v.tensor_scalar(kw_f[:, 0, :], psum[:, 2, 0:DQK], wg[:, 0:1], None, ALU.mult)
                v.tensor_scalar(kw_f[:, 1, :], psum[:, 2, 0:DQK], wg[:, 1:2], None, ALU.mult).then_inc(taken[1], 1)
                v.wait_ge(kw_hi_ok, h + 1)
                sub(kw_lo[:], kw_f[:], kw_hi[:]).then_inc(kw_ok, 1)
                combine(h, 3, chain)
                gated(h, 2)
                assert steps[0] == base + PER_HEAD - COMBINE

            head(0, False)
            with v.Fori(1, H) as h:
                head(h, True)
            steps[0] = base + H * PER_HEAD - COMBINE
            combine(H - 1, 4, own)
            gated(H - 1, 3)
            gated(H - 1, 4)
            odd_state(H - 1, 1)
            odd_state(H - 1, 3)

            with v.Fori(0, H * KV // 4) as i:
                for r in range(4):
                    v.wait_ge(ygs_hi_ok, 4 * i + r + 1)
                    v.scalar_tensor_tensor(out=yg_lo[:, 4 * i + r, :], in0=yg_st[:, r, :],
                                           scalar=gain_h[:, bass.ds(4 * i + r, 1)],
                                           in1=yg_hi[:, 4 * i + r, :].bitcast(F32),
                                           op0=ALU.mult, op1=ALU.subtract).then_inc(ygs_ok, 1)
            with v.Fori(0, KD // 2) as i:
                for p in range(2):
                    j = 2 * i + p
                    v.wait_ge(units_done, U_MIX + 4 * i + 2 * p + 2)
                    v.wait_ge(z_in[p], 16 * i + 16)
                    v.wait_ge(m_ok, j + 2)
                    v.tensor_tensor(m_sb[:], joined(p), ga_sb[:, j, :], ALU.mult).then_inc(taken[p], 1)
                    v.wait_ge(taken[p], A_MIX + i + 2)
                    v.tensor_tensor(m_sb[:], m_sb[:], z_st[:, p, :], ALU.add).then_inc(m_f_ok, 1)
                    v.wait_ge(m_hi_ok, j + 1)
                    sub(mg_lo[:, j, :], m_sb[:], mg_hi[:, j, :]).then_inc(m_ok, 1)

            def residual(i, p, unit, r, gcol, out):
                j = 2 * i + p
                v.wait_ge(units_done, unit)
                src = joined(p)
                for g, span in enumerate((slice(0, NC), slice(NC, NT))):
                    ins = v.scalar_tensor_tensor(out=out[:, span], in0=src[:, span],
                                                 scalar=mod_sb[:, gcol + j, g:g + 1],
                                                 in1=r[:, j, span], op0=ALU.mult, op1=ALU.add)
                ins.then_inc(taken[p], 1)

            for n, part in enumerate((slice(0, 2), slice(2, KD))):
                v.wait_ge(xs_in[n], 16)
                own(v.tensor_scalar(r_all[:, part, :], r_all[:, part, :], ALPHA, None, ALU.mult))
            with v.Fori(0, KD // 2) as i:
                for p in range(2):
                    j = 2 * i + p
                    residual(i, p, U_OUT + 2 * i + p + 1, r_all, 2 * KD, r_all[:, j, :])
                    v.wait_ge(r_split, j + 1)
                    sub(r_lo[:, p, :], r_all[:, j, :], r_hi[:, p, :])
                    v.wait_ge(sq_split, j + 1)
                    sub(sq_lo[:, p, :], sq_f[:, p, :], sq_hi[:, p, :]).then_inc(st_in, 1)
            v.wait_ge(mu_ok, 2)
            v.scalar_tensor_tensor(out=var_b[:], in0=joined(3), scalar=1.0 / DMODEL, in1=musq[:], op0=ALU.mult,
                                   op1=ALU.subtract).then_inc(var_b_ok, 1)
            for j in range(0, KD, 2):
                own(v.tensor_tensor(r_all[:, j, :], r_all[:, j, :], mu[:], ALU.subtract))
            v.wait_ge(sd_b_ok, 1)
            own(v.reciprocal(rstd_b[:], rstd_b[:]))

            def h2_rest(j):
                v.wait_ge(h2_hi_ok, j + 1)
                sub(h2_lo[:, j, :], h2_f[:, j % 2, :], h2_hi[:, j, :]).then_inc(h2_ok, 1)

            for j in range(KD):
                if j % 2:
                    v.wait_ge(centred, j // 2 + 1)
                v.tensor_tensor(r_all[:, j, :], r_all[:, j, :], rstd_b[:], ALU.mult).then_inc(t2_ok, 1)
                if j:
                    h2_rest(j - 1)
            h2_rest(KD - 1)
            v.wait_ge(x1_stored, 16)

            with v.Fori(0, KF) as i:
                v.wait_ge(taken[0], A_FF1 + i + 2)
                v.wait_ge(units_done, U_FF1 + 2 * i + 2)
                v.wait_ge(f_ok, i + 1)
                v.tensor_tensor(ff_sb[:], joined(1), s_sb[:], ALU.mult).then_inc(taken[1], 1)
                v.wait_ge(f_hi_ok, i + 1)
                sub(f_lo[:, i, :], ff_sb[:], f_hi[:, i, :]).then_inc(f_ok, 1)
            def row_stats(j):
                v.wait_ge(rows2_ok, j + 3)
                tiles = rows2[:, :, :].rearrange("p t (j c) -> p t j c", c=P)
                for tt in range(TT):
                    ins = v.bn_stats(stats2[:, tt, j, :], tiles[:, tt, j, :])
                return ins

            v.wait_ge(x1s_in[0], 16)
            for p in range(2):
                residual(0, p, U_FF2 + len(FQ) * (p + 1), x2_all, 5 * KD, r2_t[:, p, :])
            row_stats(0)
            v.wait_ge(x1s_in[1], 16)
            with v.Fori(1, KD // 2) as i:
                for p in range(2):
                    v.wait_ge(rt2_done, 2 * i + p - 1)
                    residual(i, p, U_FF2 + 2 * len(FQ) * i + len(FQ) * (p + 1), x2_all, 5 * KD, r2_t[:, p, :])
                    row_stats(2 * i + p - 1)
            own(row_stats(KD - 1))
            for tt in range(TT):
                ins = v.bn_aggr(mv[:, tt, :], stats2[:, tt, :, :])
            own(ins)
            v.tensor_scalar(sd[:], mv[:, :, 1], EPS, None, ALU.add).then_inc(var2_ok, 1)
            v.wait_ge(sd2_ok, 1)
            own(v.reciprocal(rstd[:], sd[:]))
            v.scalar_tensor_tensor(out=nmr[:], in0=mv[:, :, 0], scalar=-1.0, in1=rstd[:], op0=ALU.mult, op1=ALU.mult)\
                .then_inc(norm_ok, 1)
            v.wait_ge(lnr_in, 16)
            for tt in range(TT):
                v.wait_ge(norm_ok, tt + 2)
                v.tensor_tensor(rows2[:, tt, :], rows2[:, tt, :], ln_row[:, 0, :], ALU.mult).then_inc(gain_ok, 1)
                if tt not in (0, 2):
                    v.wait_ge(gain_ok, tt + 1)
                    v.tensor_tensor(rows2[:, tt, :], rows2[:, tt, :], ln_row[:, 1, :], ALU.add).then_inc(y_ok, 1)


_OUTS = [("y_prompt", (NC, DMODEL)), ("y_sample", (NL, DMODEL)), ("new_C", (2, H, DV, DQK)),
         ("new_n", (2, H, DQK)), ("new_m", (2, H, 1))]


def dft_constants():
    c = np.arange(DG)
    ang = 2 * np.pi * np.outer(c, c) / DG
    cos, sin = np.cos(ang) / np.sqrt(DG), np.sin(ang) / np.sqrt(DG)
    chan = np.zeros((DG, XW))
    chan[:, 0:P] = cos[:, 0:P]
    chan[:, 0] = (cos[:, 0] + cos[:, P]) / 2
    chan[:, P:2 * P] = sin[:, 0:P]
    chan[:, 2 * P] = (cos[:, P] - cos[:, 0]) / 2
    t = np.arange(NC)
    a = 2 * np.pi * np.outer(t, t) / NC
    pos_c = np.stack([np.cos(a), np.sin(a)]) / np.sqrt(NC)
    r, w = np.arange(NL) // GRID_W, np.arange(NL) % GRID_W
    a = 2 * np.pi * (np.outer(r, r) * GRID_W / NL + np.outer(w, w) / GRID_W)
    pos_l = np.stack([np.cos(a), np.sin(a)]) / np.sqrt(NL)
    f = np.float32
    return (np.ascontiguousarray(pos_c.transpose(1, 0, 2), f).reshape(P, 2 * NC),
            np.ascontiguousarray(pos_l.reshape(2, LT, P, NL).transpose(2, 0, 1, 3), f).reshape(P, 2 * LT * NL),
            np.ascontiguousarray(chan.reshape(2, P, XW).transpose(1, 0, 2), f).reshape(P, 2 * XW))


def const_block():
    s, t = np.arange(P)[:, None], np.arange(P)[None, :]
    out = np.zeros((P, 5 * P + H), np.float32)
    out[:, 0:P] = np.eye(P)
    out[:, P:2 * P] = np.where(s <= t, 0.0, -1e30)
    out[:, 2 * P:3 * P] = np.where(s >= t, 0.0, -1e30)
    out[0:H, 3 * P:4 * P] = 1.0
    out[32:32 + H, 4 * P:5 * P] = 1.0
    for h in range(H):
        out[h, 5 * P + h] = out[32 + h, 5 * P + h] = 1.0
    return out


def blocks(w):
    k, n = w.shape
    return w.reshape(k // P, P, n // P, P).transpose(2, 1, 0, 3).reshape(n // P, P, k)


def kernel(**inputs):
    import concourse.bacc as _bacc
    from concourse.bass_utils import run_bass_kernel_spmd as _run

    a = {k: np.asarray(v) for k, v in inputs.items()}
    w_in = a["w_in"][0]
    cuts = [0, H * DQK, 2 * H * DQK, 2 * H * DQK + DM, 2 * H * DQK + 2 * DM]
    g_end = cuts[4] + 4 * H
    wq, wk, wv, wo = (w_in[:, cuts[i]:cuts[i + 1]] for i in range(4))
    wg = w_in[:, cuts[4]:g_end]
    wf, wga, wgb = (w_in[:, g_end + i * DMODEL:g_end + (i + 1) * DMODEL] for i in range(3))
    wb = a["w_branch_b"][0].reshape(NG, DG, KD, P)
    low = wb[:, 0:P]
    high = np.concatenate([wb[:, P:P + 1], wb[:, :P:-1]], axis=1)
    ub = np.stack([low, high]).transpose(3, 2, 0, 1, 4).reshape(KD, P, UW)
    gb = blocks(wgb)
    q, k, o = blocks(wq), blocks(wk), blocks(wo)
    vv = wv.reshape(4, 2, P, H, DV).transpose(3, 0, 2, 1, 4).reshape(H, 4, P, 2 * DV)
    wa = blocks(a["w_branch_a"][0]).reshape(KD, P, 2, UW).transpose(0, 2, 1, 3)
    ffi = blocks(a["w_ffn_in"][0])
    parts = [blocks(wf), np.stack([gb, ub], axis=1).reshape(2 * KD, P, UW)]
    for h in range(H):
        parts += [q[2 * h:2 * h + 2], k[2 * h:2 * h + 2], vv[h], o[4 * h:4 * h + 4]]
    parts += [blocks(wga), wa.reshape(2 * KD, P, UW), blocks(a["w_out"][0]),
              np.stack([ffi[:KF], ffi[KF:]], axis=1).reshape(2 * KF, P, UW)]
    ffo = np.zeros((KD, P, len(FQ) * UW), np.float32)
    ffo[:, :, :KF * P] = blocks(a["w_ffn_out"][0])
    parts.append(ffo.reshape(KD, P, len(FQ), UW).transpose(0, 2, 1, 3).reshape(len(FQ) * KD, P, UW))
    wunits = np.concatenate(parts)
    gates = np.zeros((KD, P, P), np.float32)
    gbias = np.zeros((P, 1), np.float32)
    for d in range(2):
        for kind in range(2):
            row, col = 64 * kind + 32 * d, (2 * d + kind) * H
            gates[:, :, row:row + H] = wg[:, col:col + H].reshape(KD, P, H)
            gbias[row:row + H, 0] = a["b_gate"][0][col:col + H]
    x = np.concatenate([a["x_prompt"][0], a["x_sample"][0]])
    cc = np.stack([a["c_ctx"], a["c"][0]])
    sm = a["state_m"][0, 0]
    sn = a["state_n"][0, 0].reshape(2, H, KQ, P).transpose(3, 1, 0, 2)
    pos_c, pos_l, chan = dft_constants()
    ln = np.stack([a["ln_gain"][0], a["ln_bias"][0]], axis=1)
    arrays = {
        "wunits": wunits, "wmod": a["w_mod"][0].reshape(KD, P, 6, UW).transpose(2, 0, 1, 3).reshape(NMOD, P, UW),
        "xT": x.reshape(NT, KD, P).transpose(2, 1, 0), "cT": cc.reshape(2, KD, P).transpose(2, 1, 0),
        "bmod": np.repeat(a["b_mod"][0].reshape(NMOD, P).T[:, :, None], 2, axis=2),
        "consts": const_block(), "dft_c": pos_c, "dft_l": pos_l, "dft_x": chan,
        "wgate": gates.transpose(1, 0, 2).reshape(P, UW), "gate_bias": gbias,
        "stateC": a["state_C"][0, 0].reshape(2, H, DV, KQ, P).transpose(1, 4, 0, 3, 2),
        "state_n": np.repeat(sn[..., None], 2, axis=4), "m0_rows": sm.T,
        "m0_bcast": np.repeat(sm[None], P, axis=0), "gainT": a["mh_gain"][0].reshape(H * KV, P).T,
        "lnT": ln[0].reshape(2, KD, P).transpose(2, 0, 1), "ln_rows": np.repeat(ln[1][None], P, axis=0),
    }
    nc = _bacc.Bacc("TRN2", target_bir_lowering=False, num_devices=1)
    args, host = [], {}
    for name, value in arrays.items():
        value = np.ascontiguousarray(value)
        host[f"in_{name}"] = value
        args.append(nc.dram_tensor(f"in_{name}", value.shape, F32, kind="ExternalInput").ap())
    for name, shape in _OUTS:
        args.append(nc.dram_tensor(f"out_{name}", shape, F32, kind="ExternalOutput").ap())
    build(nc, *args)
    r = _run(nc, [host], core_ids=[0]).results[0]
    return (r["out_y_prompt"][None], r["out_y_sample"][None], r["out_new_C"][None, None],
            r["out_new_n"][None, None], r["out_new_m"][None, None, :, :, 0])
```
